# Optimizing a Trainium2 kernel written in Bass

```python
import math
import jax, jax.numpy as jnp
from jax import lax
import numpy as np

D_MODEL = 1024
BATCH = 1
SEQ = 256
DEPTH = 2

CHUNK = 64
Q_BLOCK = 128
EPS = 1e-6
SB_HEAD_DIM = 64
SB_WIDTH = D_MODEL // 2
SB_HEADS = SB_WIDTH // SB_HEAD_DIM
CONV_WIDTH = D_MODEL // 2
CONV_KERNEL = 31
EVEN_IN = 3 * SB_WIDTH + 2 * CONV_WIDTH
EVEN_MIX = SB_WIDTH + CONV_WIDTH
DIFF_HEAD_DIM = 64
DIFF_HEADS = D_MODEL // (2 * DIFF_HEAD_DIM)
DIFF_V_DIM = 2 * DIFF_HEAD_DIM
DIFF_QK_WIDTH = DIFF_HEADS * 2 * DIFF_HEAD_DIM
ODD_IN = 2 * DIFF_QK_WIDTH + DIFF_HEADS * DIFF_V_DIM
ODD_MIX = DIFF_HEADS * DIFF_V_DIM
ALIBI_MAX_EXP = 8.0
N_GROUPS = 4
EXPERTS_PER_GROUP = 8
N_EXPERTS = N_GROUPS * EXPERTS_PER_GROUP
TOP_K = 2
D_EXPERT = D_MODEL // 2
MOE_BLOCK = 256
N_EVEN = (DEPTH + 1) // 2
N_ODD = DEPTH // 2

kernel_name = "hybrid_stickbreak_conformer_diffattn_hmoe"

def rmsnorm(x, g):
    x32 = x.astype(jnp.float32)
    y = x32 * lax.rsqrt(jnp.mean(x32 * x32, axis=-1, keepdims=True) + EPS)
    return (y * g.astype(jnp.float32)).astype(x.dtype)

def stick_breaking_attention(q, k, v):
    B, H, S, d = q.shape
    nb = S // Q_BLOCK
    scale = d ** -0.5
    qb = q.reshape(B, H, nb, Q_BLOCK, d).transpose(2, 0, 1, 3, 4)
    key_pos = jnp.arange(S)

    def block(args):
        q_blk, i = args
        z = jnp.einsum('bhqd,bhkd->bhqk', q_blk, k).astype(jnp.float32) * scale
        t = i * Q_BLOCK + jnp.arange(Q_BLOCK)
        causal = key_pos[None, :] < t[:, None]
        log_fail = jnp.where(causal, jax.nn.log_sigmoid(-z), 0.0)
        tail = lax.cumsum(log_fail, axis=3, reverse=True) - log_fail
        a = jnp.where(causal, jnp.exp(jax.nn.log_sigmoid(z) + tail), 0.0)
        return jnp.einsum('bhqk,bhkd->bhqd', a.astype(v.dtype), v)

    out = lax.map(block, (qb, jnp.arange(nb)))
    return out.transpose(1, 2, 0, 3, 4).reshape(B, H, S, d)

def conformer_conv(u, b_glu, dw, dw_b, ln_g, ln_b):
    u = u + b_glu
    a, g = jnp.split(u, 2, axis=-1)
    h = a * jax.nn.sigmoid(g)
    h = lax.conv_general_dilated(h, dw[:, None, :], window_strides=(1,),
                                 padding=[(CONV_KERNEL - 1, 0)],
                                 dimension_numbers=('NWC', 'WIO', 'NWC'),
                                 feature_group_count=CONV_WIDTH) + dw_b
    h32 = h.astype(jnp.float32)
    mu = jnp.mean(h32, axis=-1, keepdims=True)
    var = jnp.mean(jnp.square(h32 - mu), axis=-1, keepdims=True)
    h = ((h32 - mu) * lax.rsqrt(var + EPS) * ln_g.astype(jnp.float32) + ln_b.astype(jnp.float32)).astype(u.dtype)
    return jax.nn.silu(h)

def diff_attention(q1, q2, k1, k2, v, lam, slopes):
    B, H, S, d = q1.shape
    nb = S // Q_BLOCK
    scale = d ** -0.5
    key_pos = jnp.arange(S)

    def to_blocks(t):
        return t.reshape(B, H, nb, Q_BLOCK, d).transpose(2, 0, 1, 3, 4)

    def block(args):
        qa, qb, i = args
        t = i * Q_BLOCK + jnp.arange(Q_BLOCK)
        allowed = (key_pos[None, :] // CHUNK) <= (t[:, None] // CHUNK)
        dist = jnp.abs(t[:, None] - key_pos[None, :]).astype(jnp.float32)
        bias = jnp.where(allowed[None], -slopes[:, None, None] * dist[None], -jnp.inf)
        s1 = jnp.einsum('bhqd,bhkd->bhqk', qa, k1).astype(jnp.float32) * scale + bias
        s2 = jnp.einsum('bhqd,bhkd->bhqk', qb, k2).astype(jnp.float32) * scale + bias
        p = jax.nn.softmax(s1, axis=-1) - lam * jax.nn.softmax(s2, axis=-1)
        return jnp.einsum('bhqk,bhkd->bhqd', p.astype(v.dtype), v)

    out = lax.map(block, (to_blocks(q1), to_blocks(q2), jnp.arange(nb)))
    return out.transpose(1, 2, 0, 3, 4).reshape(B, H, S, DIFF_V_DIM)

def even_mixer(h, w_in, b_glu, dw, dw_b, ln_g, ln_b, w_out):
    B, S, _ = h.shape
    proj = h @ w_in

    def heads(t):
        return t.reshape(B, S, SB_HEADS, SB_HEAD_DIM).transpose(0, 2, 1, 3)

    q = heads(proj[..., :SB_WIDTH])
    k = heads(proj[..., SB_WIDTH:2 * SB_WIDTH])
    v = heads(proj[..., 2 * SB_WIDTH:3 * SB_WIDTH])
    a_out = stick_breaking_attention(q, k, v).transpose(0, 2, 1, 3).reshape(B, S, SB_WIDTH)
    b_out = conformer_conv(proj[..., 3 * SB_WIDTH:], b_glu, dw, dw_b, ln_g, ln_b)
    return jnp.concatenate([a_out, b_out], axis=-1) @ w_out

def odd_mixer(h, w_in, q_g, k_g, lq1, lk1, lq2, lk2, sub_g, w_out, lam_init, slopes):
    B, S, _ = h.shape
    proj = h @ w_in
    q = proj[..., :DIFF_QK_WIDTH].reshape(B, S, DIFF_HEADS, 2, DIFF_HEAD_DIM)
    k = proj[..., DIFF_QK_WIDTH:2 * DIFF_QK_WIDTH].reshape(B, S, DIFF_HEADS, 2, DIFF_HEAD_DIM)
    v = proj[..., 2 * DIFF_QK_WIDTH:].reshape(B, S, DIFF_HEADS, DIFF_V_DIM).transpose(0, 2, 1, 3)
    q = rmsnorm(q, q_g).transpose(0, 2, 3, 1, 4)
    k = rmsnorm(k, k_g).transpose(0, 2, 3, 1, 4)
    lam = (jnp.exp(jnp.sum(lq1.astype(jnp.float32) * lk1.astype(jnp.float32)))
           - jnp.exp(jnp.sum(lq2.astype(jnp.float32) * lk2.astype(jnp.float32))) + lam_init)
    o = diff_attention(q[:, :, 0], q[:, :, 1], k[:, :, 0], k[:, :, 1], v, lam, slopes)
    o = rmsnorm(o, sub_g) * (1.0 - lam_init)
    o = o.transpose(0, 2, 1, 3).reshape(B, S, ODD_MIX)
    return o @ w_out

def hierarchical_moe(h, w_group, b_group, w_router, b_router, w_gate, w_up, w_down):
    B, S, D = h.shape
    N = B * S
    xf = h.reshape(N, D)
    g_logits = (xf @ w_group).astype(jnp.float32) + b_group.astype(jnp.float32)
    g_prob = jax.nn.softmax(g_logits, axis=-1)
    g_idx = jnp.argmax(g_logits, axis=-1).astype(jnp.int32)
    g_w = jnp.take_along_axis(g_prob, g_idx[:, None], axis=-1)[:, 0]
    e_logits = ((xf @ w_router).astype(jnp.float32) + b_router.astype(jnp.float32)).reshape(N, N_GROUPS, EXPERTS_PER_GROUP)
    e_logits = jnp.take_along_axis(e_logits, g_idx[:, None, None], axis=1)[:, 0]
    top_v, top_i = lax.top_k(e_logits, TOP_K)
    e_w = jax.nn.softmax(top_v, axis=-1) * g_w[:, None]
    e_id = g_idx[:, None] * EXPERTS_PER_GROUP + top_i.astype(jnp.int32)
    flat_e = e_id.reshape(-1)
    flat_w = e_w.reshape(-1)
    flat_tok = jnp.repeat(jnp.arange(N, dtype=jnp.int32), TOP_K)
    order = jnp.argsort(flat_e)
    sorted_e = flat_e[order]
    counts = jnp.zeros(N_EXPERTS, jnp.int32).at[flat_e].add(1)
    padded = (counts + MOE_BLOCK - 1) // MOE_BLOCK * MOE_BLOCK
    pad_end = jnp.cumsum(padded)
    pad_start = pad_end - padded
    start = jnp.cumsum(counts) - counts
    dest = pad_start[sorted_e] + jnp.arange(N * TOP_K, dtype=jnp.int32) - start[sorted_e]
    n_blocks = -(-(N * TOP_K) // MOE_BLOCK) + N_EXPERTS
    P = n_blocks * MOE_BLOCK
    slot_tok = jnp.zeros(P, jnp.int32).at[dest].set(flat_tok[order])
    slot_w = jnp.zeros(P, jnp.float32).at[dest].set(flat_w[order])
    block_e = jnp.minimum(jnp.searchsorted(pad_end, jnp.arange(n_blocks) * MOE_BLOCK, side='right'),
                          N_EXPERTS - 1).astype(jnp.int32)
    xs = xf[slot_tok].reshape(n_blocks, MOE_BLOCK, D)

    def expert_block(args):
        xb, e = args
        return (jax.nn.silu(xb @ w_gate[e]) * (xb @ w_up[e])) @ w_down[e]

    ys = lax.map(expert_block, (xs, block_e)).reshape(P, D)
    out = jnp.zeros((N, D), ys.dtype).at[slot_tok].add(ys * slot_w[:, None].astype(ys.dtype))
    return out.reshape(B, S, D)

def setup_inputs(seed: int = 0) -> dict:
    key = jax.random.key(seed)
    ks = jax.random.split(key, 32)

    def nrm(k, shape, std):
        return jax.random.normal(k, shape, jnp.float32) * std

    D = D_MODEL
    return {
        "x": nrm(ks[0], (BATCH, SEQ, D), 1.0),
        "c": nrm(ks[1], (BATCH, D), 1.0),
        "w_ada": nrm(ks[2], (DEPTH, D, 6 * D), 0.5 * D ** -0.5),
        "b_ada": nrm(ks[3], (DEPTH, 6 * D), 0.02),
        "mix_norm_g": 1.0 + nrm(ks[4], (DEPTH, D), 0.02),
        "ffn_norm_g": 1.0 + nrm(ks[5], (DEPTH, D), 0.02),
        "even_w_in": nrm(ks[6], (N_EVEN, D, EVEN_IN), D ** -0.5),
        "conv_b_glu": nrm(ks[7], (N_EVEN, 2 * CONV_WIDTH), 0.02),
        "conv_dw": nrm(ks[8], (N_EVEN, CONV_KERNEL, CONV_WIDTH), CONV_KERNEL ** -0.5),
        "conv_dw_b": nrm(ks[9], (N_EVEN, CONV_WIDTH), 0.02),
        "conv_ln_g": 1.0 + nrm(ks[10], (N_EVEN, CONV_WIDTH), 0.02),
        "conv_ln_b": nrm(ks[11], (N_EVEN, CONV_WIDTH), 0.02),
        "even_w_out": nrm(ks[12], (N_EVEN, EVEN_MIX, D), EVEN_MIX ** -0.5),
        "odd_w_in": nrm(ks[13], (N_ODD, D, ODD_IN), D ** -0.5),
        "qk_norm_q": 1.0 + nrm(ks[14], (N_ODD, DIFF_HEAD_DIM), 0.02),
        "qk_norm_k": 1.0 + nrm(ks[15], (N_ODD, DIFF_HEAD_DIM), 0.02),
        "lambda_q1": nrm(ks[16], (N_ODD, DIFF_HEAD_DIM), 0.1),
        "lambda_k1": nrm(ks[17], (N_ODD, DIFF_HEAD_DIM), 0.1),
        "lambda_q2": nrm(ks[18], (N_ODD, DIFF_HEAD_DIM), 0.1),
        "lambda_k2": nrm(ks[19], (N_ODD, DIFF_HEAD_DIM), 0.1),
        "diff_sub_g": 1.0 + nrm(ks[20], (N_ODD, DIFF_V_DIM), 0.02),
        "odd_w_out": nrm(ks[21], (N_ODD, ODD_MIX, D), ODD_MIX ** -0.5),
        "moe_w_group": nrm(ks[22], (DEPTH, D, N_GROUPS), D ** -0.5),
        "moe_b_group": nrm(ks[23], (DEPTH, N_GROUPS), 0.01),
        "moe_w_router": nrm(ks[24], (DEPTH, D, N_EXPERTS), D ** -0.5),
        "moe_b_router": nrm(ks[25], (DEPTH, N_EXPERTS), 0.01),
        "moe_w_gate": nrm(ks[26], (DEPTH, N_EXPERTS, D, D_EXPERT), D ** -0.5),
        "moe_w_up": nrm(ks[27], (DEPTH, N_EXPERTS, D, D_EXPERT), D ** -0.5),
        "moe_w_down": nrm(ks[28], (DEPTH, N_EXPERTS, D_EXPERT, D), D_EXPERT ** -0.5),
    }

def reference(x, c, w_ada, b_ada, mix_norm_g, ffn_norm_g, even_w_in, conv_b_glu, conv_dw,
              conv_dw_b, conv_ln_g, conv_ln_b, even_w_out, odd_w_in, qk_norm_q, qk_norm_k,
              lambda_q1, lambda_k1, lambda_q2, lambda_k2, diff_sub_g, odd_w_out,
              moe_w_group, moe_b_group, moe_w_router, moe_b_router, moe_w_gate, moe_w_up,
              moe_w_down):
    slopes = jnp.exp2(-ALIBI_MAX_EXP * jnp.arange(1, DIFF_HEADS + 1, dtype=jnp.float32) / DIFF_HEADS)
    c_act = jax.nn.silu(c)
    for layer in range(DEPTH):
        mod = c_act @ w_ada[layer] + b_ada[layer]
        sh1, sc1, g1, sh2, sc2, g2 = jnp.split(mod[:, None, :], 6, axis=-1)
        h = rmsnorm(x, mix_norm_g[layer]) * (1.0 + sc1) + sh1
        j = layer // 2
        if layer % 2 == 0:
            y = even_mixer(h, even_w_in[j], conv_b_glu[j], conv_dw[j], conv_dw_b[j],
                           conv_ln_g[j], conv_ln_b[j], even_w_out[j])
        else:
            lam_init = 0.8 - 0.6 * math.exp(-0.3 * layer)
            y = odd_mixer(h, odd_w_in[j], qk_norm_q[j], qk_norm_k[j], lambda_q1[j], lambda_k1[j],
                          lambda_q2[j], lambda_k2[j], diff_sub_g[j], odd_w_out[j], lam_init, slopes)
        x = x + g1 * y
        h = rmsnorm(x, ffn_norm_g[layer]) * (1.0 + sc2) + sh2
        x = x + g2 * hierarchical_moe(h, moe_w_group[layer], moe_b_group[layer], moe_w_router[layer],
                                      moe_b_router[layer], moe_w_gate[layer], moe_w_up[layer],
                                      moe_w_down[layer])
    return x


_drawn_inputs = setup_inputs


def setup_inputs(seed=0):
    import zlib

    import numpy as np

    out = dict(_drawn_inputs(seed))
    spreads = {}
    factors = {'mix_norm_g': 6.591,
     'ffn_norm_g': 3.586,
     'conv_b_glu': 8.0,
     'conv_dw_b': 5.384,
     'conv_ln_g': 6.438,
     'conv_ln_b': 8.0,
     'qk_norm_q': 8.0,
     'qk_norm_k': 8.0,
     'diff_sub_g': 24.813,
     'moe_b_group': 6.073,
     'moe_b_router': 4.92}
    for name, (base, spread) in spreads.items():
        noise = np.random.default_rng([zlib.crc32(name.encode()), seed]).standard_normal(out[name].shape)
        drawn = base * np.exp(spread * noise) if base else spread * noise
        out[name] = __import__('jax').numpy.asarray(drawn.astype(out[name].dtype))
    for name, factor in factors.items():
        out[name] = (out[name] * factor).astype(out[name].dtype)
    return out
```

```python
import math
from contextlib import ExitStack

import concourse.bass as bass
from concourse import mybir

P = 128
F32 = mybir.dt.float32
BF16 = mybir.dt.bfloat16
I32 = mybir.dt.int32
U32 = mybir.dt.uint32
ALU = mybir.AluOpType
ACT = mybir.ActivationFunctionType
AX = mybir.AxisListType

EPS = 1e-6
FAR = 1.0e6
NEG = -1.0e30
LOWEST = -3.0e38
EXP_FLOOR = -80.0


def build_trunk(nc, x, c, w_ada, b_ada, mix_norm_g, ffn_norm_g, even_w_in, conv_b_glu, conv_dw, conv_dw_b,
                conv_ln_g, conv_ln_b, even_w_out, odd_w_in, qk_norm_q, qk_norm_k, lambda_q1, lambda_k1,
                lambda_q2, lambda_k2, diff_sub_g, odd_w_out, moe_w_group, moe_b_group, moe_w_router,
                moe_b_router, moe_w_gate, moe_w_up, moe_w_down, out):
    _, S, D = x.shape
    TB = S // P
    KD = D // P
    TAPS, CONV = conv_dw.shape[1:]
    CB = CONV // P
    PAD = TAPS - 1
    HD = 64
    NPAIR = (even_w_in.shape[2] - 2 * CONV) // 3 // P
    NH = D // P
    NG = moe_w_group.shape[2]
    NE, _, F = moe_w_gate.shape[1:]
    EPG = NE // NG
    KF = F // P
    SLOT = 64
    EP = NE // 2
    ROUNDS = S // SLOT
    LAM0 = 0.8 - 0.6 * math.exp(-0.3)
    QSCALE = HD ** -0.5
    NL = NG + NE
    HALF = 512
    RING = 4
    UNROLL = 4

    ctx = ExitStack()
    with ctx:
        def sb(name, shape, dt=F32):
            return ctx.enter_context(nc.sbuf_tensor(name, shape, dt))

        def sem(name):
            return ctx.enter_context(nc.semaphore(name))

        RINGT = sb("weight_ring", [P, RING, 8 * 1024])
        X = sb("x_tokens", [P, TB, D])
        HT = sb("h_or_mix_T", [P, KD, S])
        GATE = sb("gate_rows", [P, 3, D])
        SHIFT = sb("shift", [P, 4, KD])
        SCALE = sb("scale", [P, 4, KD])
        GAIN = sb("norm_gain", [P, 4, KD])
        BADA = sb("ada_bias", [P, 12, KD])
        CCOL = sb("cond_cols", [P, 3, KD])
        IDENT = sb("ident", [P, P])
        NEGTRI = sb("neg_tri", [P, P])
        NEGONE = sb("neg_one", [P, P])
        ONES = sb("ones", [P, P])
        BEFORE = sb("before", [P, P])
        HEADSUM = sb("head_sum", [P, P])
        SEL = sb("select_partials", [P, P])
        SLOTNO = sb("slot_number", [P, P])
        EXPNO = sb("expert_number", [P, NE])
        GRPNO = sb("group_of_expert", [P, NE])
        NDIST = sb("neg_distance", [P, 3 * P])
        EPSC = sb("eps", [P, 1])
        CV1 = sb("conv_taps", [P, TAPS * CB])
        CV2 = sb("small_cols", [P, 32])
        WR = sb("router_w", [P, 2, KD, NL])
        RB = sb("router_b", [P, 2, NL])
        LAMV = sb("lambda_rows", [P, 4, HD])
        LAM = sb("lambda", [P, 8])
        STAT = sb("norm_stat", [P, 4])
        LG = sb("router_logits", [P, TB, NL])
        GL8 = sb("group_logits", [P, TB, 8])
        GM8 = sb("group_top", [P, TB, 8])
        GI8 = sb("group_index", [P, TB, 8], U32)
        EM = sb("expert_logits", [P, TB, NE])
        EM8 = sb("expert_top", [P, TB, 8])
        EI8 = sb("expert_index", [P, TB, 8], U32)
        RT = sb("route_scratch", [P, 12, TB])
        EXPSEL = sb("chosen_experts", [P, TB, 2])
        EXPW = sb("chosen_weights", [P, TB, 2])
        ONEHOT = sb("expert_onehot", [P, 3, TB, NE])
        RANK = sb("rank_in_expert", [P, TB, 2])
        POS = sb("slot_of_token", [P, TB, 2])
        POST = sb("slot_scratch", [P, 3, TB, 2])
        CNT = sb("largest_count", [P, 1])
        CNTI = sb("largest_count_int", [P, 1], I32)

        U = sb("phase_region", [P, 9984])

        def part_of(at, *shape, dt=F32):
            n = math.prod(shape)
            words = n if dt == F32 else n // 2
            v = U[:, at:at + words]
            if dt != F32:
                v = v.bitcast(dt)
            if len(shape) == 1:
                return v
            names = "abcd"[:len(shape)]
            return v.rearrange(f"p ({' '.join(names)}) -> p {' '.join(names)}", **dict(zip(names, shape)))

        XN = part_of(0, TB, KD, P)
        QTe = part_of(0, NPAIR, S)
        KTe = part_of(1024, NPAIR, S)
        Ve = part_of(2048, TB, NPAIR * P)
        CIN = part_of(3072, CB, S + PAD)
        CSQ = part_of(3072, CB, S)
        CACC = part_of(4288, CB, S)
        SPe = part_of(5312, 2, 2, 3 * P)
        PRe = part_of(6848, 2, 2, 3 * P)
        RSTD = part_of(8384, S)
        CROW = part_of(6848, 2, P)
        CREP = part_of(8640, KD, 32)
        PART = part_of(8896, 1024)
        QTo = part_of(0, NH, S)
        KTo = part_of(2048, NH, S)
        Vo = part_of(4096, TB, D)
        SCo = part_of(6144, 2, 2, 3 * P)
        PRo = part_of(7680, 3 * P)
        PTo = part_of(8064, 3 * P)
        SQo = [part_of(8448, S), part_of(8960, S)]
        RSo = [part_of(8704, S), part_of(9216, S)]
        BIAS = part_of(9216, 2, 3 * P)
        STo = ONEHOT[:, 0, :, :]
        XT = part_of(0, 2, KD, P)
        XN3 = part_of(2048, 3, TB, KD, P, dt=BF16)
        TH = part_of(5120, F)
        T1 = part_of(5632, F)
        HID = part_of(6144, KF, P)
        HIDT = part_of(6656, KF, P)
        YS = part_of(7168, D)
        SG = part_of(8192, 2, TB, P, dt=BF16)
        SW = part_of(8448, TB, P)
        SWT = part_of(8704, 2, TB, P)
        TMPA = part_of(9216, TB, P)
        TMPB = part_of(9472, TB, P)
        TMPC = part_of(9728, TB, P)

        PS = ctx.enter_context(nc.psum_tensor("psum", [P, 8, 512], F32))

        slab_in = [sem(f"slab_in_{i}") for i in range(RING)]
        cond_in = sem("cond_in")
        x_in = sem("x_in")
        vectors_in = sem("vectors_in")
        gate_bias_in = sem("gate_bias_in")
        pool_step = sem("pool_step")
        consts_ready = sem("consts_ready")
        dve_step = sem("dve_step")
        act_step = sem("act_step")
        cond_exp = sem("cond_exp")
        cond_in_place = sem("cond_in_place")
        cond_negated = sem("cond_negated")
        ada_summed = sem("ada_summed")
        ada_copied = sem("ada_copied")
        ada_joined = sem("ada_joined")
        ada_ready = sem("ada_ready")
        rows_turned = sem("rows_turned")
        cols_ready = sem("cols_ready")
        norm_stat = sem("norm_stat")
        xn_ready = sem("xn_ready")
        xn_turned = sem("xn_turned")
        h_dve = sem("h_dve")
        h_act = sem("h_act")
        proj_done = sem("proj_done")
        qkv_out = sem("qkv_out")
        glu_out = sem("glu_out")
        glu_exp = sem("glu_exp")
        z_ready = sem("z_ready")
        softlog = sem("softlog")
        fail_sum_in = sem("fail_sum_in")
        fails_masked = sem("fails_masked")
        logs_ready = sem("logs_ready")
        logs_min = sem("logs_min")
        probs_exp = sem("probs_exp")
        probs_masked = sem("probs_masked")
        pv_done = sem("pv_done")
        heads_out = sem("heads_out")
        conv_done = sem("conv_done")
        conv_mean = sem("conv_mean")
        conv_centred = sem("conv_centred")
        conv_squared = sem("conv_squared")
        conv_var = sem("conv_var")
        conv_rstd = sem("conv_rstd")
        conv_floor = sem("conv_floor")
        conv_exp = sem("conv_exp")
        conv_out = sem("conv_out")
        wout_done = sem("wout_done")
        x_mixed = sem("x_mixed")
        qk_squared = sem("qk_squared")
        qk_mean = sem("qk_mean")
        qk_rstd = sem("qk_rstd")
        qk_out = sem("qk_out")
        v_out = sem("v_out")
        lam_sum = sem("lam_sum")
        lam_exp = sem("lam_exp")
        head_bias = sem("head_bias")
        scores_done = sem("scores_done")
        scores_max = sem("scores_max")
        scores_exp = sem("scores_exp")
        diff_ready = sem("diff_ready")
        diff_turned = sem("diff_turned")
        diffT_ready = sem("diffT_ready")
        o_done = sem("o_done")
        o_squared = sem("o_squared")
        o_mean = sem("o_mean")
        o_rstd = sem("o_rstd")
        o_out = sem("o_out")
        logits_done = sem("logits_done")
        group_top = sem("group_top")
        group_exp = sem("group_exp")
        expert_top = sem("expert_top")
        expert_exp = sem("expert_exp")
        onehot_ready = sem("onehot_ready")
        rank_done = sem("rank_done")
        count_ready = sem("count_ready")
        split_act = sem("split_act")
        split_dve = sem("split_dve")
        moe_cleared = sem("moe_cleared")
        slots_built = sem("slots_built")
        weights_built = sem("weights_built")
        gathered = sem("gathered")
        xt_dve = sem("xt_dve")
        xt_act = sem("xt_act")
        gate_done = sem("gate_done")
        up_done = sem("up_done")
        tanh_done = sem("tanh_done")
        t1_done = sem("t1_done")
        hidden_ready = sem("hidden_ready")
        hidden_turned = sem("hidden_turned")
        hiddenT_ready = sem("hiddenT_ready")
        weights_turned = sem("weights_turned")
        weightsT_ready = sem("weightsT_ready")
        down_done = sem("down_done")
        y_ready = sem("y_ready")
        combined = sem("combined")
        x_added = sem("x_added")
        slot_step = sem("slot_step")
        more = [{n: sem(f"more{L}_{n}") for n in ("slabs", "slots", "dve", "gathered", "gate", "tanh", "up", "turned",
                                                   "copied", "down", "combined", "added")} for L in range(2)]
        out_stored = sem("out_stored")

        ADA = [0, 1, 2, 3, 4, 5, 6, 7, 9, 10, 8, 11]
        fills = [(2, 3), (4, 5), (6, 7), (8, 9)]
        head_slabs = ([("ada", a, ada_summed, a + 1) for a in range(2)]
                      + [("even_in", 0, proj_done, 8), ("even_in", 1, proj_done, 14), ("even_in", 2, proj_done, 18)]
                      + [("ada", a, ada_summed, a + 1) for a in range(2, 10)]
                      + [("even_out", 0, wout_done, 4)]
                      + [("ada", a, ada_summed, a + 1) for a in range(10, 12)])
        mid_slabs = [("odd_in", 0, proj_done, 26), ("odd_in", 1, proj_done, 34), ("odd_in", 2, proj_done, 38),
                     ("odd_out", 0, wout_done, 8)]
        MOE0 = [len(head_slabs), len(head_slabs) + 3 * EP + len(mid_slabs)]
        MID0 = MOE0[0] + 3 * EP
        assert all(n % RING == 0 for n in (*MOE0, MID0)) and (3 * UNROLL) % RING == 0 and EP % UNROLL == 0
        GROUP = 3 * UNROLL // RING

        def place(n):
            return RINGT[:, n % RING, :]

        def landed(n):
            return 16 * (n // RING + 1)

        def slab_index(kind, arg):
            for n, s in enumerate(head_slabs):
                if s[:2] == (kind, arg):
                    return n
            for n, s in enumerate(mid_slabs):
                if s[:2] == (kind, arg):
                    return MID0 + n

        ada_src = w_ada.rearrange("l (p k) n -> l p k n", k=KD)
        even_in_src = even_w_in[0].rearrange("(p k) n -> p k n", k=KD)
        odd_in_src = odd_w_in[0].rearrange("(p k) n -> p k n", k=KD)
        out_srcs = {"even_out": even_w_out[0].rearrange("(k p) n -> p k n", p=P),
                    "odd_out": odd_w_out[0].rearrange("(k p) n -> p k n", p=P)}
        gate_src = moe_w_gate.rearrange("l e (p k) f -> l p e (k f)", k=KD)
        up_src = moe_w_up.rearrange("l e (p k) f -> l p e (k f)", k=KD)
        down_src = moe_w_down.rearrange("l e (p k) n -> l p e (k n)", k=KF)

        def wide(n, cols=1024):
            return place(n)[:, 0:KD * cols].rearrange("p (k n) -> p k n", k=KD)

        def pair_slab(n):
            return place(n).rearrange("p (e n) -> p e n", e=2)

        block = ctx.enter_context(nc.Block())

        def overflow_loads(sp, L):
            m = more[L]
            sp.wait_ge(count_ready, L + 1)
            count = sp.value_load(CNTI[0:1, 0:1], min_val=0, max_val=S)
            with sp.If(count > SLOT):
                with sp.Fori(0, ROUNDS - 1) as r:
                    with sp.Fori(0, EP) as q:
                        step = r * EP + q
                        sp.wait_ge(down_done, EP * (L + 1))
                        sp.wait_ge(m["down"], step)
                        for w, src in enumerate((gate_src, up_src, down_src)):
                            sp.dma_start(pair_slab(w), src[L, :, bass.ds(q * 2, 2), :]).then_inc(m["slabs"], 16)
                sp.wait_ge(m["added"], 4 * EP * (ROUNDS - 1))

        @block.sync
        def _(sp):
            def load_fixed(n, kind, arg):
                if kind == "ada":
                    m = ADA[arg]
                    src = ada_src[m // 6, :, :, (m % 6) * D:(m % 6 + 1) * D]
                    dst = wide(n)
                elif kind in ("even_in", "odd_in"):
                    src = (even_in_src if kind == "even_in" else odd_in_src)
                    cols = min(1024, src.shape[2] - 1024 * arg)
                    src = src[:, :, 1024 * arg:1024 * arg + cols]
                    dst = wide(n, cols)
                else:
                    src, dst = out_srcs[kind], wide(n)
                sp.dma_start(dst, src).then_inc(slab_in[n % RING], 16)

            def load_experts(L):
                base = MOE0[L]
                with sp.Fori(0, EP // UNROLL) as i:
                    for j in range(UNROLL):
                        for w, src in enumerate((gate_src, up_src, down_src)):
                            n = base + 3 * j + w
                            pair = i * UNROLL + j
                            if 3 * j + w >= RING:
                                q = (3 * j + w - RING) // 3
                                used = (gate_done, up_done, down_done)[(3 * j + w - RING) % 3]
                                sp.wait_ge(used, i * UNROLL + (EP * L + q + 1))
                            else:
                                q = (3 * (j + UNROLL) + w - RING) // 3 - UNROLL
                                used = (gate_done, up_done, down_done)[(3 * (j + UNROLL) + w - RING) % 3]
                                if EP * L + q + 1 > 0:
                                    sp.wait_ge(used, i * UNROLL + (EP * L + q + 1))
                                else:
                                    sp.wait_ge(used, i * UNROLL)
                            if 3 * j + w < RING:
                                s, v = (head_slabs + mid_slabs)[len(head_slabs) - RING + 3 * j + w + len(mid_slabs) * L][2:]
                                sp.wait_ge(s, v)
                            sp.dma_start(pair_slab(n), src[L, :, bass.ds(pair * 2, 2), :]).then_inc(slab_in[n % RING], 16)

            for n, (kind, arg, _, _) in enumerate(head_slabs):
                if n >= RING:
                    sp.wait_ge(*head_slabs[n - RING][2:])
                load_fixed(n, kind, arg)
            load_experts(0)
            overflow_loads(sp, 0)
            for n, (kind, arg, _, _) in enumerate(mid_slabs):
                q, w = divmod(3 * EP - RING + n, 3)
                sp.wait_ge((gate_done, up_done, down_done)[w], q + 1)
                load_fixed(MID0 + n, kind, arg)
            load_experts(1)
            overflow_loads(sp, 1)
            for t in range(TB):
                sp.wait_ge(x_added, 2 * (4 * (EP + 1)) - 4 + 2 * (t + 1))
                sp.dma_start(out[0, t * P:(t + 1) * P, :], X[:, t, :]).then_inc(out_stored, 16)
            sp.wait_ge(out_stored, 16 * TB)

        @block.gpsimd
        def _(pool):
            g = nc.gpsimd
            steps = [0]

            def link(ins):
                steps[0] += 1
                ins.then_inc(pool_step, 1)
                pool.wait_ge(pool_step, steps[0])

            for t, v in ((IDENT, 0.0), (NEGTRI, -1.0), (NEGONE, -1.0), (ONES, 1.0), (BEFORE, 1.0),
                         (HEADSUM, 0.0), (SEL, 0.0)):
                link(g.memset(t[:, :], v))
            link(g.memset(EPSC[:, :], EPS))
            link(g.affine_select(out=IDENT[:, :], in_=IDENT[:, :], compare_op=ALU.not_equal, fill=1.0, base=0,
                                 pattern=[[-1, P]], channel_multiplier=1))
            link(g.affine_select(out=NEGTRI[:, :], in_=NEGTRI[:, :], compare_op=ALU.is_ge, fill=0.0, base=0,
                                 pattern=[[-1, P]], channel_multiplier=1))
            link(g.affine_select(out=BEFORE[:, :], in_=BEFORE[:, :], compare_op=ALU.is_gt, fill=0.0, base=0,
                                 pattern=[[1, P]], channel_multiplier=-1))
            for h in range(2):
                link(g.memset(HEADSUM[h * HD:(h + 1) * HD, h * HD:(h + 1) * HD], 1.0))
            for r in range(4):
                link(g.memset(SEL[32 * r:32 * r + 1, :], 1.0))
            link(g.iota(SLOTNO[:, :], pattern=[[1, P]], base=0, channel_multiplier=0, allow_small_or_imprecise_dtypes=True))
            link(g.iota(EXPNO[:, :], pattern=[[1, NE]], base=0, channel_multiplier=0, allow_small_or_imprecise_dtypes=True))
            link(g.iota(GRPNO[:, :], pattern=[[1, NG], [0, EPG]], base=0, channel_multiplier=0,
                        allow_small_or_imprecise_dtypes=True))
            link(g.iota(NDIST[:, 0:P], pattern=[[-1, P]], base=0, channel_multiplier=1, allow_small_or_imprecise_dtypes=True))
            link(g.iota(NDIST[:, P:3 * P], pattern=[[-1, 2 * P]], base=P, channel_multiplier=1,
                        allow_small_or_imprecise_dtypes=True))
            g.memset(GL8[:, :, :], LOWEST).then_inc(consts_ready, 1)

            def keep_past(tile, i, ready, done):
                pool.wait_ge(ready, i + 1)
                for h in range(2):
                    for at in (0, 2 * P):
                        v = tile[:, i % 2, h, at:at + P]
                        g.affine_select(out=v, in_=v, compare_op=ALU.is_gt, fill=0.0, base=0,
                                        pattern=[[1, P]], channel_multiplier=-1).then_inc(done, 1)

            for i in range(NPAIR):
                keep_past(SPe, i, fail_sum_in, fails_masked)
                keep_past(PRe, i, probs_exp, probs_masked)

            for h in range(NH):
                if h == 0:
                    pool.wait_ge(qk_out, 16)
                    pool.wait_ge(cols_ready, 4)
                if h >= 2:
                    pool.wait_ge(scores_max, h - 1)
                g.tensor_scalar(BIAS[:, h % 2, :], NDIST[:, :], 2.0 ** (-8.0 * (h + 1) / NH), 0.0,
                                ALU.mult, ALU.add).then_inc(head_bias, 1)

        @block.scalar
        def _(act):
            a = nc.scalar
            steps = [0]

            def link(ins):
                steps[0] += 1
                ins.then_inc(act_step, 1)
                act.wait_ge(act_step, steps[0])

            act.dma_start(CCOL[:, 0, :], c.rearrange("o (p k) -> p (o k)", k=KD)).then_inc(cond_in, 16)
            act.dma_start(X[:, :, :], x[0].rearrange("(t p) d -> p t d", p=P)).then_inc(x_in, 16)
            n_vec = [0]

            def vector(dst, src):
                n_vec[0] += 1
                act.dma_start(dst, src).then_inc(vectors_in, 16)

            with nc.allow_non_contiguous_dma(reason="small vectors"):
                for L in range(2):
                    vector(BADA[:, 6 * L:6 * L + 6, :], b_ada[L].rearrange("(j p k) -> p j k", p=P, k=KD))
                    vector(GAIN[:, 2 * L, :], mix_norm_g[L].rearrange("(p k) -> p k", k=KD))
                    vector(GAIN[:, 2 * L + 1, :], ffn_norm_g[L].rearrange("(p k) -> p k", k=KD))
                    vector(GATE[:, 1 + L, :], b_ada[L, 5 * D:6 * D].partition_broadcast(P))
                    vector(WR[:, L, :, 0:NG], moe_w_group[L].rearrange("(p k) g -> p k g", k=KD))
                    vector(WR[:, L, :, NG:NL], moe_w_router[L].rearrange("(p k) e -> p k e", k=KD))
                    vector(RB[:, L, 0:NG], moe_b_group[L].partition_broadcast(P))
                    vector(RB[:, L, NG:NL], moe_b_router[L].partition_broadcast(P))
                vector(GATE[:, 0, :], b_ada[0, 2 * D:3 * D].partition_broadcast(P))
                vector(CROW[0:TAPS * CB, 0, :], conv_dw[0].rearrange("t (b c) -> (t b) c", c=P))
                vector(CROW[0:8, 1, :], conv_b_glu[0].rearrange("(b c) -> b c", c=P))
                vector(CROW[8:12, 1, :], conv_dw_b[0].rearrange("(b c) -> b c", c=P))
                vector(CROW[12:16, 1, :], conv_ln_g[0].rearrange("(b c) -> b c", c=P))
                vector(CROW[16:20, 1, :], conv_ln_b[0].rearrange("(b c) -> b c", c=P))
                vector(CROW[20:21, 1, :], diff_sub_g)
                for r, v in ((21, qk_norm_q), (22, qk_norm_k)):
                    for h in range(2):
                        vector(CROW[r:r + 1, 1, h * HD:(h + 1) * HD], v)
                for n, v in enumerate((lambda_q1, lambda_k1, lambda_q2, lambda_k2)):
                    vector(LAMV[:, n, :], v[0].partition_broadcast(P))
            assert n_vec[0] == N_VECTORS

            act.wait_ge(cond_negated, 1)
            a.activation(CCOL[:, 1, :], CCOL[:, 1, :], ACT.Exp, scale=-1.0).then_inc(cond_exp, 1)

            def norm_statistics(stage):
                for t in range(TB):
                    link(a.activation(XN[:, t, :, :].rearrange("p k q -> p (k q)"), X[:, t, :], ACT.Square,
                                      accum_out=STAT[:, t:t + 1]))
                link(a.activation(STAT[:, 2:4], STAT[:, 0:2], ACT.Ln, scale=1.0 / D, bias=EPSC[:, 0:1]))
                a.activation(STAT[:, 2:4], STAT[:, 2:4], ACT.Exp, scale=-0.5).then_inc(norm_stat, 1)

            def modulate(stage):
                for k in range(KD // 2, KD):
                    act.wait_ge(xn_turned, 4 * stage + k // 2 + 1)
                    a.activation(HT[:, k, :], PS[:, k // 2, (k % 2) * S:(k % 2 + 1) * S], ACT.Identity, scale=SCALE[:, stage, k:k + 1],
                                 bias=SHIFT[:, stage, k:k + 1]).then_inc(h_act, 1)

            def copy_partials(n):
                act.wait_ge(ada_summed, n + 1)
                if n:
                    act.wait_ge(ada_joined, n)
                a.copy(PART[:, :].rearrange("p (b n) -> p b n", b=2), PS[:, 4:6, :]).then_inc(ada_copied, 1)

            act.wait_ge(x_in, 16)
            act.wait_ge(consts_ready, 1)
            norm_statistics(0)
            copy_partials(0)
            copy_partials(1)
            act.wait_ge(ada_ready, 2)
            modulate(0)
            for u in range(10):
                act.wait_ge(proj_done, u + 1)
                if u < 4:
                    a.mul(QTe[:, u, :], PS[:, u % 4, 0:S], QSCALE).then_inc(qkv_out, 1)
                elif u < 8:
                    a.copy(KTe[:, u - 4, :], PS[:, u % 4, 0:S]).then_inc(qkv_out, 1)
                else:
                    a.copy(Ve[:, u - 8, :], PS[:, u % 4, :]).then_inc(qkv_out, 1)
            act.wait_ge(glu_out, 8)
            a.activation(CACC[:, :, :], CACC[:, :, :], ACT.Exp, scale=-1.0).then_inc(glu_exp, 1)

            def soft_logs(i):
                act.wait_ge(z_ready, i + 1)
                if i >= 2:
                    act.wait_ge(logs_ready, i - 1)
                b = 2 * (i % 2)
                v = SPe[:, i % 2, :, :]
                link(a.activation(v, PS[:, b:b + 2, 0:3 * P], ACT.Abs))
                link(a.activation(v, v, ACT.Exp, scale=-1.0))
                a.activation(v, v, ACT.Ln, bias=1.0).then_inc(softlog, 1)

            soft_logs(0)
            for i in range(NPAIR):
                if i + 1 < NPAIR:
                    soft_logs(i + 1)
                for n in fills[i]:
                    copy_partials(n)
                act.wait_ge(logs_min, i + 1)
                v = PRe[:, i % 2, :, :]
                a.activation(v, v, ACT.Exp).then_inc(probs_exp, 1)
                act.wait_ge(pv_done, i + 1)
                a.copy(HT[:, i, :], PS[:, 7, 0:S]).then_inc(heads_out, 1)
            act.wait_ge(conv_centred, 1)
            a.activation(CSQ[:, :, :], CACC[:, :, :], ACT.Square).then_inc(conv_squared, 1)
            act.wait_ge(conv_var, 1)
            link(a.activation(RSTD[:, :], PS[:, 7, S:2 * S], ACT.Ln, scale=1.0 / CONV, bias=EPSC[:, 0:1]))
            a.activation(RSTD[:, :], RSTD[:, :], ACT.Exp, scale=-0.5).then_inc(conv_rstd, 1)
            act.wait_ge(conv_floor, 1)
            a.activation(CSQ[:, :, :], CSQ[:, :, :], ACT.Exp, scale=-1.0).then_inc(conv_exp, 1)

            def moe(L):
                stage = 2 * L + 1
                norm_statistics_after = (x_mixed, 4 * (L + 1))
                act.wait_ge(*norm_statistics_after)
                norm_statistics(stage)
                if L == 0:
                    act.dma_start(GATE[:, 0, :], b_ada[1, 2 * D:3 * D].partition_broadcast(P)).then_inc(gate_bias_in, 16)
                modulate(stage)
                act.wait_ge(xn_ready, 2 * (stage + 1))
                a.copy(XN3[:, 0], XN[:, :, :, :]).then_inc(split_act, 1)
                act.wait_ge(group_top, L + 1)
                for t in range(TB):
                    a.activation(RT[:, 8 + 2 * t:10 + 2 * t, :].rearrange("p a b -> p (a b)")[:, 0:NG],
                                 GL8[:, t, 0:NG], ACT.Exp, bias=RT[:, 0, t:t + 1],
                                 accum_out=RT[:, 1, t:t + 1]).then_inc(group_exp, 1)
                if L == 0:
                    copy_partials(10)
                act.wait_ge(split_dve, 2 * L + 1)
                a.copy(XN3[:, 1], XN[:, :, :, :]).then_inc(split_act, 1)
                act.wait_ge(expert_top, L + 1)
                a.activation(RT[:, 5, :], RT[:, 4, :], ACT.Exp).then_inc(expert_exp, 1)
                if L == 0:
                    copy_partials(11)
                act.wait_ge(split_dve, 2 * L + 2)
                a.copy(XN3[:, 2], XN[:, :, :, :]).then_inc(split_act, 1)

                def spread(count, buf):
                    act.wait_ge(gathered, count)
                    for k in range(KD // 2, KD):
                        a.activation(XT[:, buf, k, :], PS[:, 2 + k // 4, (k % 4) * P:(k % 4 + 1) * P], ACT.Identity,
                                     scale=SCALE[:, stage, k:k + 1], bias=SHIFT[:, stage, k:k + 1]).then_inc(xt_act, 1)

                spread((EP + 1) * L + 1, 0)
                with act.Fori(0, EP // UNROLL) as i:
                    for j in range(UNROLL):
                        n = i * UNROLL + (EP * L + j)
                        act.wait_ge(gate_done, n + 1)
                        act.wait_ge(hidden_ready, n)
                        a.activation(TH[:, :], PS[:, 0, :], ACT.Tanh, scale=0.5).then_inc(tanh_done, 1)
                        spread(n + (L + 2), (j + 1) % 2)
                        act.wait_ge(weights_turned, n + 1)
                        a.copy(SWT[:, j % 2, :, :].rearrange("p t s -> p (t s)"), PS[:, 5, 0:TB * P]).then_inc(weightsT_ready, 1)
                        act.wait_ge(hidden_turned, n + 1)
                        a.copy(HIDT[:, :, :].rearrange("p k s -> p (k s)"), PS[:, 4, :]).then_inc(hiddenT_ready, 1)

                m = more[L]
                act.wait_ge(count_ready, L + 1)
                count = act.value_load(CNTI[0:1, 0:1], min_val=0, max_val=S)
                with act.If(count > SLOT):
                    with act.Fori(0, EP * (ROUNDS - 1)) as step:
                        act.wait_ge(m["gate"], step + 1)
                        a.activation(TH[:, :], PS[:, 0, :], ACT.Tanh, scale=0.5).then_inc(m["tanh"], 1)
                        act.wait_ge(m["turned"], step + 1)
                        a.copy(SWT[:, 0, :, :].rearrange("p t s -> p (t s)"), PS[:, 5, 0:TB * P]).then_inc(m["copied"], 1)
                        a.copy(HIDT[:, :, :].rearrange("p k s -> p (k s)"), PS[:, 4, :]).then_inc(m["copied"], 1)
                    act.wait_ge(m["added"], 4 * EP * (ROUNDS - 1))

            moe(0)

            act.wait_ge(x_added, 4 * (EP + 1))
            norm_statistics(2)
            modulate(2)
            act.wait_ge(lam_sum, 1)
            a.activation(LAM[:, 2:4], LAM[:, 0:2], ACT.Exp).then_inc(lam_exp, 1)
            for u in range(20):
                act.wait_ge(proj_done, 18 + u + 1)
                if u < 16:
                    if u >= 2:
                        act.wait_ge(qk_mean, u - 1)
                    a.activation(SQo[u % 2][:, :], PS[:, u % 4, 0:S], ACT.Square).then_inc(qk_squared, 1)
                if 1 <= u <= 16:
                    w = u - 1
                    act.wait_ge(qk_mean, w + 1)
                    if w >= 2:
                        act.wait_ge(qk_out, w - 1)
                    link(a.activation(RSo[w % 2][:, :], PS[:, 4 + w % 2, 0:S], ACT.Ln, scale=1.0 / HD, bias=EPSC[:, 0:1]))
                    a.activation(RSo[w % 2][:, :], RSo[w % 2][:, :], ACT.Exp, scale=-0.5).then_inc(qk_rstd, 1)
                if u >= 16:
                    v = u - 16
                    a.copy(Vo[:, v // 2, (v % 2) * HALF:(v % 2 + 1) * HALF], PS[:, u % 4, :]).then_inc(v_out, 1)

            def exps(h):
                act.wait_ge(scores_max, h + 1)
                for cc in range(2):
                    for t in range(TB):
                        v = SCo[:, h % 2, cc, t * P:(1 + 2 * t) * P]
                        k = 2 * cc + t
                        ins = a.activation(v, v, ACT.Exp, bias=STo[:, h % 2, 4 + k:5 + k], accum_out=STo[:, h % 2, 8 + k:9 + k])
                        ins.then_inc(scores_exp, 1)

            exps(0)
            for h in range(NH):
                if h + 1 < NH:
                    exps(h + 1)
                act.wait_ge(diff_turned, h + 1)
                a.copy(PTo[:, :], PS[:, 4, 0:3 * P]).then_inc(diffT_ready, 1)
                act.wait_ge(o_done, h + 1)
                a.activation(SQo[0][:, :], PS[:, 6, 0:S], ACT.Square).then_inc(o_squared, 1)
                act.wait_ge(o_mean, h + 1)
                if h:
                    act.wait_ge(o_out, h)
                link(a.activation(RSo[0][:, :], PS[:, 7, 0:S], ACT.Ln, scale=1.0 / P, bias=EPSC[:, 0:1]))
                a.activation(RSo[0][:, :], RSo[0][:, :], ACT.Exp, scale=-0.5).then_inc(o_rstd, 1)

            moe(1)

        @block.vector
        def _(dve):
            v = nc.vector
            steps = [0]

            def link(ins):
                steps[0] += 1
                ins.then_inc(dve_step, 1)
                dve.wait_ge(dve_step, steps[0])

            dve.wait_ge(cond_in, 16)
            v.tensor_scalar(CCOL[:, 1, :], CCOL[:, 0, :], EXP_FLOOR, None, ALU.max).then_inc(cond_negated, 1)
            dve.wait_ge(cond_exp, 1)
            link(v.tensor_scalar(CCOL[:, 1, :], CCOL[:, 1, :], 1.0, None, ALU.add))
            link(v.reciprocal(CCOL[:, 2, :], CCOL[:, 1, :]))
            link(v.tensor_tensor(CCOL[:, 1, :], CCOL[:, 0, :], CCOL[:, 2, :], ALU.mult))
            v.tensor_copy(CREP[:, :, :], CCOL[:, 1, :].unsqueeze(2).broadcast_to([P, KD, 32])).then_inc(cond_in_place, 1)

            dve.wait_ge(rows_turned, 2)
            v.tensor_copy(CV1[:, :], PS[:, 6, 0:TAPS * CB]).then_inc(cols_ready, 1)
            v.tensor_copy(CV2[:, 0:23], PS[:, 6, P:P + 23]).then_inc(cols_ready, 1)
            dve.wait_ge(cols_ready, 2)
            v.tensor_scalar(CV2[:, 23:24], CV2[:, 20:21], 1.0 - LAM0, None, ALU.mult)
            v.tensor_scalar(CV2[:, 24:25], CV2[:, 21:22], QSCALE, None, ALU.mult).then_inc(cols_ready, 1)
            dve.wait_ge(consts_ready, 1)
            link(v.scalar_tensor_tensor(out=NDIST[:, :], in0=NDIST[:, :], scalar=-1.0, in1=NDIST[:, :],
                                        op0=ALU.mult, op1=ALU.min))
            link(v.memset(NDIST[0:HD, HD:P], NEG))
            v.memset(NDIST[0:HD, P + 3 * HD:3 * P], NEG).then_inc(cols_ready, 1)
            dve.wait_ge(vectors_in, 16 * N_VECTORS)
            for n in range(2):
                link(v.tensor_tensor(LAMV[:, 2 * n, :], LAMV[:, 2 * n, :], LAMV[:, 2 * n + 1, :], ALU.mult))
                ins = v.tensor_reduce(LAM[:, n:n + 1], LAMV[:, 2 * n, :], AX.X, ALU.add)
                if n == 0:
                    link(ins)
                else:
                    ins.then_inc(lam_sum, 1)

            def take_modulation(n):
                m = ADA[n]
                L, j = divmod(m, 6)
                dve.wait_ge(ada_joined, n + 1)
                if j in (0, 3):
                    v.tensor_tensor(SHIFT[:, 2 * L + j // 3, :], PS[:, 6, 0:KD], BADA[:, m, :], ALU.add).then_inc(ada_ready, 1)
                elif j in (1, 4):
                    st = 2 * L + j // 3
                    link(v.tensor_tensor(SCALE[:, st, :], PS[:, 6, 0:KD], BADA[:, m, :], ALU.add))
                    v.scalar_tensor_tensor(out=SCALE[:, st, :], in0=SCALE[:, st, :], scalar=1.0, in1=GAIN[:, st, :],
                                           op0=ALU.add, op1=ALU.mult).then_inc(ada_ready, 1)
                else:
                    row = GATE[:, 0 if j == 2 else 1 + L, :]
                    if m == 8:
                        dve.wait_ge(gate_bias_in, 16)
                    link(v.tensor_tensor(row[:, 0:HALF], PS[:, 6, :], row[:, 0:HALF], ALU.add))
                    v.tensor_tensor(row[:, HALF:D], PS[:, 4, :], row[:, HALF:D], ALU.add).then_inc(ada_ready, 1)

            def normalise(stage):
                dve.wait_ge(norm_stat, stage + 1)
                for t in range(TB):
                    v.tensor_scalar(XN[:, t, :, :], X[:, t, :].rearrange("p (q k) -> p k q", k=KD),
                                    STAT[:, 2 + t:3 + t], None, ALU.mult).then_inc(xn_ready, 1)

            def modulate(stage):
                for k in range(KD // 2):
                    dve.wait_ge(xn_turned, 4 * stage + k // 2 + 1)
                    v.tensor_scalar(HT[:, k, :], PS[:, k // 2, (k % 2) * S:(k % 2 + 1) * S], SCALE[:, stage, k:k + 1],
                                    SHIFT[:, stage, k:k + 1], ALU.mult, ALU.add).then_inc(h_dve, 1)

            def add_mixed(L):
                for u in range(4):
                    t, h = divmod(u, 2)
                    dve.wait_ge(wout_done, 4 * L + u + 1)
                    if u == 0:
                        dve.wait_ge(ada_ready, 12 if L else 3)
                    link(v.tensor_tensor(PS[:, u, :], PS[:, u, :], GATE[:, 0, h * HALF:(h + 1) * HALF], ALU.mult))
                    xs = X[:, t, h * HALF:(h + 1) * HALF]
                    v.tensor_tensor(xs, PS[:, u, :], xs, ALU.add).then_inc(x_mixed, 1)

            normalise(0)
            take_modulation(0)
            take_modulation(1)
            dve.wait_ge(ada_ready, 2)
            modulate(0)
            link(v.memset(CIN[:, :, 0:PAD], 0.0))
            for b in range(CB):
                dve.wait_ge(proj_done, 10 + b + 1)
                v.tensor_scalar(CIN[:, b, PAD:PAD + S], PS[:, (10 + b) % 4, 0:S], CV2[:, b:b + 1], None,
                                ALU.add).then_inc(glu_out, 1)
            for b in range(CB):
                dve.wait_ge(proj_done, 14 + b + 1)
                v.tensor_scalar(CACC[:, b, :], PS[:, (14 + b) % 4, 0:S], CV2[:, 4 + b:5 + b], EXP_FLOOR,
                                ALU.add, ALU.max).then_inc(glu_out, 1)

            def glu():
                dve.wait_ge(glu_exp, 1)
                link(v.tensor_scalar(CACC[:, :, :], CACC[:, :, :], 1.0, None, ALU.add))
                link(v.reciprocal(CACC[:, :, :], CACC[:, :, :]))
                link(v.tensor_tensor(CIN[:, :, PAD:PAD + S], CIN[:, :, PAD:PAD + S], CACC[:, :, :], ALU.mult))

            def conv_taps(lo, hi):
                for j in range(lo, hi):
                    for b in range(CB):
                        src = CIN[:, b, j:j + S]
                        tap = CV1[:, j * CB + b:j * CB + b + 1]
                        if j == 0:
                            ins = v.tensor_scalar(CACC[:, b, :], src, tap, CV2[:, 8 + b:9 + b], ALU.mult, ALU.add)
                        else:
                            dve.wait_ge(conv_done, CB * (j - 1) + b + 1)
                            ins = v.scalar_tensor_tensor(out=CACC[:, b, :], in0=src, scalar=tap, in1=CACC[:, b, :],
                                                         op0=ALU.mult, op1=ALU.add)
                        ins.then_inc(conv_done, 1)

            def soft_plus(i):
                dve.wait_ge(softlog, i + 1)
                b = 2 * (i % 2)
                s = SPe[:, i % 2, :, :]
                v.scalar_tensor_tensor(out=s, in0=PS[:, b:b + 2, 0:3 * P], scalar=0.0, in1=s,
                                       op0=ALU.max, op1=ALU.add).then_inc(fail_sum_in, 1)

            glu()
            tap_ends = [0, 4, 8, 12, 16, 20, 24, 28, TAPS]
            soft_plus(0)
            for i in range(NPAIR):
                conv_taps(tap_ends[2 * i], tap_ends[2 * i + 1])
                if i + 1 < NPAIR:
                    soft_plus(i + 1)
                dve.wait_ge(logs_ready, i + 1)
                if i >= 2:
                    dve.wait_ge(pv_done, i - 1)
                b = 2 * (i % 2)
                v.tensor_scalar(PRe[:, i % 2, :, :], PS[:, b:b + 2, 0:3 * P], 0.0, None, ALU.min).then_inc(logs_min, 1)
                conv_taps(tap_ends[2 * i + 1], tap_ends[2 * i + 2])
                for n in fills[i]:
                    take_modulation(n)
            dve.wait_ge(conv_mean, 1)
            for b in range(CB):
                ins = v.scalar_tensor_tensor(out=CACC[:, b, :], in0=PS[:, 7, S:2 * S], scalar=-1.0 / CONV,
                                             in1=CACC[:, b, :], op0=ALU.mult, op1=ALU.add)
                if b + 1 < CB:
                    link(ins)
                else:
                    ins.then_inc(conv_centred, 1)
            dve.wait_ge(conv_rstd, 1)
            for b in range(CB):
                link(v.tensor_tensor(CACC[:, b, :], CACC[:, b, :], RSTD[:, :], ALU.mult))
                link(v.tensor_scalar(CACC[:, b, :], CACC[:, b, :], CV2[:, 12 + b:13 + b], CV2[:, 16 + b:17 + b],
                                     ALU.mult, ALU.add))
            v.tensor_scalar(CSQ[:, :, :], CACC[:, :, :], EXP_FLOOR, None, ALU.max).then_inc(conv_floor, 1)
            dve.wait_ge(conv_exp, 1)
            link(v.tensor_scalar(CSQ[:, :, :], CSQ[:, :, :], 1.0, None, ALU.add))
            link(v.reciprocal(CSQ[:, :, :], CSQ[:, :, :]))
            v.tensor_tensor(HT[:, 4:8, :], CACC[:, :, :], CSQ[:, :, :], ALU.mult).then_inc(conv_out, 1)
            add_mixed(0)

            def slot_positions():
                e64, off, pos = POST[:, 0], POST[:, 1], POST[:, 2]
                return [lambda: v.tensor_scalar(off, RANK[:, :, :], 0.0, FAR, ALU.is_lt, ALU.mult),
                        lambda: v.tensor_scalar(pos, RANK[:, :, :], float(SLOT), FAR, ALU.is_ge, ALU.mult),
                        lambda: v.tensor_tensor(off, off, pos, ALU.add),
                        lambda: v.tensor_scalar(e64, EXPSEL[:, :, :], float(SLOT), None, ALU.mult),
                        lambda: v.tensor_tensor(pos, RANK[:, :, :], e64, ALU.add),
                        lambda: v.tensor_tensor(POS[:, :, :], pos, off, ALU.add)]

            def moe(L):
                stage = 2 * L + 1
                normalise(stage)
                if L == 0:
                    dve.wait_ge(ada_ready, 10)
                modulate(stage)
                v.memset(YS[:, :], 0.0).then_inc(moe_cleared, 1)
                dve.wait_ge(logits_done, L + 1)
                link(v.tensor_tensor(LG[:, :, :], PS[:, 7, 0:TB * NL].rearrange("p (t n) -> p t n", t=TB),
                                     RB[:, L, :].unsqueeze(1).broadcast_to([P, TB, NL]), ALU.add))
                link(v.tensor_copy(GL8[:, :, 0:NG], LG[:, :, 0:NG]))
                for t in range(TB):
                    link(v.max(GM8[:, t, :], GL8[:, t, :]))
                    link(v.max_index(GI8[:, t, :], GM8[:, t, :], GL8[:, t, :]))
                v.tensor_scalar(RT[:, 0, :], GM8[:, :, 0], -1.0, None, ALU.mult).then_inc(group_top, 1)
                link(v.tensor_copy(RT[:, 2, :], GI8[:, :, 0]))
                for t in range(TB):
                    link(v.tensor_scalar(EM[:, t, :], GRPNO[:, :], RT[:, 2, t:t + 1], NEG, ALU.not_equal, ALU.mult))
                    link(v.tensor_tensor(EM[:, t, :], EM[:, t, :], LG[:, t, NG:NL], ALU.add))
                    link(v.max(EM8[:, t, :], EM[:, t, :]))
                    link(v.max_index(EI8[:, t, :], EM8[:, t, :], EM[:, t, :]))
                v.tensor_tensor(RT[:, 4, :], EM8[:, :, 1], EM8[:, :, 0], ALU.subtract).then_inc(expert_top, 1)
                link(v.tensor_copy(EXPSEL[:, :, :], EI8[:, :, 0:2]))
                for s in range(2):
                    for t in range(TB):
                        link(v.tensor_scalar(ONEHOT[:, s, t, :], EXPNO[:, :], EXPSEL[:, t, s:s + 1], None, ALU.is_equal))
                v.tensor_tensor(ONEHOT[:, 2, :, :], ONEHOT[:, 0, :, :], ONEHOT[:, 1, :, :], ALU.add).then_inc(onehot_ready, 1)
                dve.wait_ge(split_act, 3 * L + 1)
                v.tensor_tensor(XN[:, :, :, :], XN[:, :, :, :], XN3[:, 0], ALU.subtract).then_inc(split_dve, 1)
                if L == 0:
                    take_modulation(10)
                dve.wait_ge(group_exp, 2 * (L + 1))
                dve.wait_ge(expert_exp, L + 1)
                link(v.tensor_scalar(RT[:, 6, :], RT[:, 5, :], 1.0, None, ALU.add))
                link(v.tensor_tensor(RT[:, 6, :], RT[:, 6, :], RT[:, 1, :], ALU.mult))
                link(v.reciprocal(EXPW[:, :, 0], RT[:, 6, :]))
                link(v.tensor_tensor(EXPW[:, :, 1], EXPW[:, :, 0], RT[:, 5, :], ALU.mult))
                dve.wait_ge(rank_done, L + 1)
                for s in range(2):
                    link(v.tensor_tensor(ONEHOT[:, s, :, :], ONEHOT[:, s, :, :],
                                         PS[:, 7, P:P + TB * NE].rearrange("p (t n) -> p t n", t=TB), ALU.mult))
                    link(v.tensor_reduce(RANK[:, :, s], ONEHOT[:, s, :, :], AX.X, ALU.add))
                link(v.tensor_reduce(CNT[:, :], PS[:, 7, 2 * P:2 * P + NE], AX.X, ALU.max))
                v.tensor_copy(CNTI[:, :], CNT[:, :]).then_inc(count_ready, 1)
                for f in slot_positions():
                    link(f())
                dve.wait_ge(split_act, 3 * L + 2)
                v.tensor_tensor(XN[:, :, :, :], XN[:, :, :, :], XN3[:, 1], ALU.subtract).then_inc(split_dve, 1)
                if L == 0:
                    take_modulation(11)
                v.memset(SWT[:, :, :, :], 0.0).then_inc(moe_cleared, 1)

                def build_slots(buf, done):
                    for t in range(TB):
                        v.tensor_scalar(TMPA[:, t, :], SLOTNO[:, :], POS[:, t, 0:1], None, ALU.is_equal).then_inc(done[0], 1)
                    for t in range(TB):
                        dve.wait_ge(done[0], done[1] + t + 1)
                        v.scalar_tensor_tensor(out=SG[:, buf, t, :], in0=SLOTNO[:, :], scalar=POS[:, t, 1:2], in1=TMPA[:, t, :],
                                               op0=ALU.is_equal, op1=ALU.add).then_inc(slots_built, 1)

                def spread(count, buf):
                    dve.wait_ge(gathered, count)
                    for k in range(KD // 2):
                        v.tensor_scalar(XT[:, buf, k, :], PS[:, 2 + k // 4, (k % 4) * P:(k % 4 + 1) * P],
                                        SCALE[:, stage, k:k + 1], SHIFT[:, stage, k:k + 1],
                                        ALU.mult, ALU.add).then_inc(xt_dve, 1)

                def add_combined(done, last):
                    for u, bank in enumerate((0, 1, 5, 0)):
                        t, h = divmod(u, 2)
                        dve.wait_ge(combined, done + u + 1)
                        xs = X[:, t, h * HALF:(h + 1) * HALF]
                        v.tensor_tensor(xs, PS[:, bank, :], xs, ALU.add).then_inc(x_added, 1)

                per = 7
                base = (per * EP + 2) * L
                build_slots(0, (slot_step, base))
                spread((EP + 1) * L + 1, 0)
                with dve.Fori(0, EP // UNROLL) as i:
                    for j in range(UNROLL):
                        n = i * UNROLL + (EP * L + j)
                        st = i * (UNROLL * per) + (base + 2 + per * j)
                        if j:
                            dve.wait_ge(weights_turned, n)
                        else:
                            dve.wait_ge(weights_turned, n)
                        for t in range(TB):
                            v.tensor_scalar(TMPB[:, t, :], SLOTNO[:, :], POS[:, t, 0:1], EXPW[:, t, 0:1],
                                            ALU.is_equal, ALU.mult).then_inc(slot_step, 1)
                            v.tensor_scalar(TMPC[:, t, :], SLOTNO[:, :], POS[:, t, 1:2], EXPW[:, t, 1:2],
                                            ALU.is_equal, ALU.mult).then_inc(slot_step, 1)
                        for t in range(TB):
                            dve.wait_ge(slot_step, st + 2 * t + 2)
                            v.tensor_tensor(SW[:, t, :], TMPB[:, t, :], TMPC[:, t, :], ALU.add).then_inc(weights_built, 1)
                        dve.wait_ge(slot_step, st + 4)
                        v.tensor_scalar(POS[:, :, :], POS[:, :, :], -float(P), None, ALU.add).then_inc(slot_step, 1)
                        dve.wait_ge(slot_step, st + 5)
                        build_slots((j + 1) % 2, (slot_step, st + 5))
                        dve.wait_ge(tanh_done, n + 1)
                        v.scalar_tensor_tensor(out=T1[:, :], in0=TH[:, :], scalar=1.0, in1=PS[:, 0, :],
                                               op0=ALU.add, op1=ALU.mult).then_inc(t1_done, 1)
                        dve.wait_ge(t1_done, n + 1)
                        dve.wait_ge(up_done, n + 1)
                        dve.wait_ge(hidden_turned, n)
                        v.scalar_tensor_tensor(out=HID[:, :, :].rearrange("p k q -> p q k"),
                                               in0=T1[:, :].rearrange("p (q k) -> p q k", k=KF), scalar=0.5,
                                               in1=PS[:, 1, :].rearrange("p (q k) -> p q k", k=KF),
                                               op0=ALU.mult, op1=ALU.mult).then_inc(hidden_ready, 1)
                        spread(n + (L + 2), (j + 1) % 2)
                        add_combined(i * (4 * UNROLL) + (4 * (EP + 1) * L + 4 * j), False)
                        dve.wait_ge(down_done, n + 1)
                        for h in range(2):
                            v.tensor_tensor(YS[:, h * HALF:(h + 1) * HALF], PS[:, 6 + h, :],
                                            GATE[:, 1 + L, h * HALF:(h + 1) * HALF], ALU.mult).then_inc(y_ready, 1)
                add_combined(4 * (EP + 1) * L + 4 * EP, True)

                m = more[L]
                count = dve.value_load(CNTI[0:1, 0:1], min_val=0, max_val=S)
                per_round, per_pair = 8, 12
                with dve.If(count > SLOT):
                    with dve.Fori(0, ROUNDS - 1) as r:
                        at = r * (per_round + per_pair * EP)
                        if True:
                            dve.wait_ge(m["dve"], at)
                        v.tensor_scalar(RANK[:, :, :], RANK[:, :, :], -float(SLOT), None, ALU.add).then_inc(m["dve"], 1)
                        for n, f in enumerate(slot_positions()):
                            dve.wait_ge(m["dve"], at + n + 1)
                            f().then_inc(m["dve"], 1)
                        dve.wait_ge(m["dve"], at + 7)
                        v.tensor_copy(CNT[:, :], CNT[:, :]).then_inc(m["dve"], 1)
                        with dve.Fori(0, EP) as q:
                            step = r * EP + q
                            st = r * (per_round + per_pair * EP) + q * per_pair + per_round
                            dve.wait_ge(m["dve"], st)
                            dve.wait_ge(m["turned"], step)
                            for t in range(TB):
                                v.tensor_scalar(TMPA[:, t, :], SLOTNO[:, :], POS[:, t, 0:1], None,
                                                ALU.is_equal).then_inc(m["dve"], 1)
                                v.tensor_scalar(TMPB[:, t, :], SLOTNO[:, :], POS[:, t, 0:1], EXPW[:, t, 0:1],
                                                ALU.is_equal, ALU.mult).then_inc(m["dve"], 1)
                                v.tensor_scalar(TMPC[:, t, :], SLOTNO[:, :], POS[:, t, 1:2], EXPW[:, t, 1:2],
                                                ALU.is_equal, ALU.mult).then_inc(m["dve"], 1)
                            dve.wait_ge(m["dve"], st + 6)
                            for t in range(TB):
                                v.tensor_tensor(SW[:, t, :], TMPB[:, t, :], TMPC[:, t, :], ALU.add).then_inc(m["slots"], 1)
                                v.scalar_tensor_tensor(out=SG[:, 0, t, :], in0=SLOTNO[:, :], scalar=POS[:, t, 1:2],
                                                       in1=TMPA[:, t, :], op0=ALU.is_equal, op1=ALU.add).then_inc(m["slots"], 1)
                            dve.wait_ge(m["slots"], step * 4 + 4)
                            v.tensor_scalar(POS[:, :, :], POS[:, :, :], -float(P), None, ALU.add).then_inc(m["dve"], 1)
                            dve.wait_ge(m["gathered"], step + 1)
                            for k in range(KD):
                                ins = v.tensor_scalar(XT[:, 0, k, :], PS[:, 2 + k // 4, (k % 4) * P:(k % 4 + 1) * P],
                                                      SCALE[:, stage, k:k + 1], SHIFT[:, stage, k:k + 1], ALU.mult, ALU.add)
                            ins.then_inc(m["dve"], 1)
                            dve.wait_ge(m["tanh"], step + 1)
                            v.scalar_tensor_tensor(out=T1[:, :], in0=TH[:, :], scalar=1.0, in1=PS[:, 0, :],
                                                   op0=ALU.add, op1=ALU.mult).then_inc(m["dve"], 1)
                            dve.wait_ge(m["dve"], st + 9)
                            dve.wait_ge(m["up"], step + 1)
                            v.scalar_tensor_tensor(out=HID[:, :, :].rearrange("p k q -> p q k"),
                                                   in0=T1[:, :].rearrange("p (q k) -> p q k", k=KF), scalar=0.5,
                                                   in1=PS[:, 1, :].rearrange("p (q k) -> p q k", k=KF),
                                                   op0=ALU.mult, op1=ALU.mult).then_inc(m["dve"], 1)
                            dve.wait_ge(m["down"], step + 1)
                            for h in range(2):
                                v.tensor_tensor(YS[:, h * HALF:(h + 1) * HALF], PS[:, 6 + h, :],
                                                GATE[:, 1 + L, h * HALF:(h + 1) * HALF], ALU.mult).then_inc(m["dve"], 1)
                            for u in range(4):
                                t, h = divmod(u, 2)
                                dve.wait_ge(m["combined"], step * 4 + (u + 1))
                                xs = X[:, t, h * HALF:(h + 1) * HALF]
                                v.tensor_tensor(xs, PS[:, u, :], xs, ALU.add).then_inc(m["added"], 1)
                    dve.wait_ge(m["added"], 4 * EP * (ROUNDS - 1))

            moe(0)

            normalise(2)
            modulate(2)
            dve.wait_ge(lam_exp, 1)
            link(v.tensor_tensor(LAM[:, 4:5], LAM[:, 3:4], LAM[:, 2:3], ALU.subtract))
            link(v.tensor_scalar(LAM[:, 5:6], LAM[:, 4:5], -LAM0, None, ALU.add))
            for u in range(16):
                dve.wait_ge(qk_rstd, u + 1)
                dst, gain = (QTo, CV2[:, 24:25]) if u < 8 else (KTo, CV2[:, 22:23])
                v.scalar_tensor_tensor(out=dst[:, u % 8, :], in0=PS[:, u % 4, 0:S], scalar=gain, in1=RSo[u % 2][:, :],
                                       op0=ALU.mult, op1=ALU.mult).then_inc(qk_out, 1)

            def biased(h):
                dve.wait_ge(scores_done, h + 1)
                dve.wait_ge(head_bias, h + 1)
                if h >= 2:
                    dve.wait_ge(diff_ready, 2 * (h - 1))
                for cc in range(2):
                    for t in range(TB):
                        at = slice(t * P, (1 + 2 * t) * P)
                        k = 2 * cc + t
                        ins = v.tensor_tensor_reduce(SCo[:, h % 2, cc, at], PS[:, 2 * (h % 2) + cc, at], BIAS[:, h % 2, at],
                                                     1.0, LOWEST, ALU.add, ALU.max, STo[:, h % 2, k:k + 1])
                link(ins)
                v.tensor_scalar(STo[:, h % 2, 4:8], STo[:, h % 2, 0:4], -1.0, None, ALU.mult).then_inc(scores_max, 1)

            biased(0)
            for h in range(NH):
                if h + 1 < NH:
                    biased(h + 1)
                dve.wait_ge(scores_exp, 4 * (h + 1))
                st = STo[:, h % 2, :]
                link(v.reciprocal(st[:, 12:16], st[:, 8:12]))
                link(v.tensor_scalar(st[:, 16:18], st[:, 14:16], LAM[:, 5:6], None, ALU.mult))
                if h >= 1:
                    dve.wait_ge(diff_turned, h)
                for t in range(TB):
                    at = slice(t * P, (1 + 2 * t) * P)
                    link(v.tensor_scalar(SCo[:, h % 2, 0, at], SCo[:, h % 2, 0, at], st[:, 12 + t:13 + t], None, ALU.mult))
                    v.scalar_tensor_tensor(out=PRo[:, at], in0=SCo[:, h % 2, 1, at], scalar=st[:, 16 + t:17 + t],
                                           in1=SCo[:, h % 2, 0, at], op0=ALU.mult, op1=ALU.add).then_inc(diff_ready, 1)
                dve.wait_ge(o_rstd, h + 1)
                v.scalar_tensor_tensor(out=HT[:, h, :], in0=PS[:, 6, 0:S], scalar=CV2[:, 23:24], in1=RSo[0][:, :],
                                       op0=ALU.mult, op1=ALU.mult).then_inc(o_out, 1)
            add_mixed(1)
            moe(1)

        @block.tensor
        def _(pe):
            def mm(out_, lhsT, rhs, first, last, **kw):
                return pe.matmul(out_, lhsT, rhs, start=first, stop=last, **kw)

            def slab_ready(n):
                pe.wait_ge(slab_in[n % RING], landed(n))

            def modulation(n):
                m = ADA[n]
                s = slab_index("ada", n)
                slab_ready(s)
                if n == 0:
                    pe.wait_ge(cond_in_place, 1)
                else:
                    pe.wait_ge(ada_copied, n)
                    pe.wait_ge(ada_ready, n)
                w = wide(s)
                for h in range(2):
                    for k in range(KD):
                        g = k % 4
                        ins = mm(PS[32 * g:32 * g + 32, 4 + h, :], CREP[:, k, :], w[:, k, h * HALF:(h + 1) * HALF],
                                 k < 4, k >= 4, skip_group_check=True)
                ins.then_inc(ada_summed, 1)
                pe.wait_ge(ada_copied, n + 1)
                if m % 6 in (2, 5):
                    mm(PS[:, 6, :], SEL[:, :], PART[:, 0:HALF], True, True)
                    mm(PS[:, 4, :], SEL[:, :], PART[:, HALF:D], True, True).then_inc(ada_joined, 1)
                else:
                    cols = PART[:, :].rearrange("p (q k) -> p k q", k=KD)
                    for k in range(KD):
                        ins = mm(PS[:, 6, k:k + 1], cols[:, k, :], SEL[:, 0:1], True, True)
                    ins.then_inc(ada_joined, 1)

            def turn_xn(stage):
                pe.wait_ge(xn_ready, 2 * (stage + 1))
                for b in range(4):
                    for k in (2 * b, 2 * b + 1):
                        for t in range(TB):
                            ins = pe.transpose(PS[:, b, (k % 2) * S + t * P:(k % 2) * S + (t + 1) * P],
                                               XN[:, t, k, :], IDENT[:, :])
                    ins.then_inc(xn_turned, 1)

            def h_in_place(stage):
                pe.wait_ge(h_dve, 4 * (stage + 1))
                pe.wait_ge(h_act, 4 * (stage + 1))

            def project_T(bank, w, cols):
                for k in range(KD):
                    ins = mm(PS[:, bank, 0:S], w[:, k, cols:cols + P], HT[:, k, :], k == 0, k == KD - 1)
                return ins

            def project(bank, w, cols, t):
                for k in range(KD):
                    ins = mm(PS[:, bank, :], HT[:, k, t * P:(t + 1) * P], w[:, k, cols:cols + HALF], k == 0, k == KD - 1)
                return ins

            def mix_out(L, slab):
                slab_ready(slab)
                w = wide(slab)
                for u in range(4):
                    t, h = divmod(u, 2)
                    project(u, w, h * HALF, t).then_inc(wout_done, 1)

            pe.wait_ge(consts_ready, 1)
            pe.wait_ge(vectors_in, 16 * N_VECTORS)
            pe.transpose(PS[:, 6, 0:TAPS * CB], CROW[0:TAPS * CB, 0, :], IDENT[0:TAPS * CB, 0:TAPS * CB]).then_inc(rows_turned, 1)
            pe.transpose(PS[:, 6, P:P + 23], CROW[0:23, 1, :], IDENT[0:23, 0:23]).then_inc(rows_turned, 1)
            turn_xn(0)
            pe.wait_ge(cols_ready, 2)
            modulation(0)
            modulation(1)

            h_in_place(0)
            for u in range(18):
                s = slab_index("even_in", 0 if u < 8 else 1 if u < 14 else 2)
                if u in (0, 8, 14):
                    slab_ready(s)
                if u >= 4:
                    if u - 4 < 10:
                        pe.wait_ge(qkv_out, u - 3)
                    else:
                        pe.wait_ge(glu_out, u - 4 - 9)
                if u < 8:
                    ins = project_T(u % 4, wide(s), u * P)
                elif u < 10:
                    ins = project(u % 4, wide(s), 0, u - 8)
                elif u < 14:
                    ins = project_T(u % 4, wide(s), HALF + (u - 10) * P)
                else:
                    ins = project_T(u % 4, wide(s, HALF), (u - 14) * P)
                ins.then_inc(proj_done, 1)

            def logits(i):
                if i == 0:
                    pe.wait_ge(glu_out, 8)
                    pe.wait_ge(qkv_out, 10)
                if i >= 2:
                    pe.wait_ge(logs_min, i - 1)
                for h in range(2):
                    r = slice(h * HD, (h + 1) * HD)
                    b = 2 * (i % 2) + h
                    mm(PS[:, b, 0:S], KTe[r, i, 0:P], QTe[r, i, :], True, True)
                    ins = mm(PS[:, b, S:S + P], KTe[r, i, P:S], QTe[r, i, P:S], False, True, skip_group_check=True)
                ins.then_inc(z_ready, 1)

            def tails(i):
                pe.wait_ge(fails_masked, 4 * (i + 1))
                for h in range(2):
                    b = 2 * (i % 2) + h
                    s = SPe[:, i % 2, h, :]
                    mm(PS[:, b, 0:3 * P], NEGTRI[:, :], s, False, True, skip_group_check=True)
                    ins = mm(PS[:, b, P:S], NEGONE[:, :], s[:, S:S + P], False, True, skip_group_check=True)
                ins.then_inc(logs_ready, 1)

            def values(i):
                pe.wait_ge(probs_masked, 4 * (i + 1))
                if i:
                    pe.wait_ge(heads_out, i)
                for h in range(2):
                    cols = slice(i * P + h * HD, i * P + (h + 1) * HD)
                    pr = PRe[:, i % 2, h, :]
                    o = PS[h * HD:(h + 1) * HD, 7, :]
                    mm(o[:, 0:S], Ve[:, 0, cols], pr[:, 0:S], True, True, skip_group_check=True)
                    ins = mm(o[:, P:S], Ve[:, 1, cols], pr[:, S:S + P], False, True, skip_group_check=True)
                ins.then_inc(pv_done, 1)

            logits(0)
            for i in range(NPAIR):
                if i + 1 < NPAIR:
                    logits(i + 1)
                tails(i)
                for n in fills[i]:
                    modulation(n)
                values(i)
            pe.wait_ge(conv_done, TAPS * CB)
            pe.wait_ge(heads_out, NPAIR)
            for b in range(CB):
                ins = mm(PS[:, 7, S:2 * S], ONES[:, :], CACC[:, b, :], b == 0, b == CB - 1, skip_group_check=True)
            ins.then_inc(conv_mean, 1)
            pe.wait_ge(conv_squared, 1)
            for b in range(CB):
                ins = mm(PS[:, 7, S:2 * S], ONES[:, :], CSQ[:, b, :], b == 0, b == CB - 1, skip_group_check=True)
            ins.then_inc(conv_var, 1)
            pe.wait_ge(conv_out, 1)
            mix_out(0, slab_index("even_out", 0))

            def moe(L):
                stage = 2 * L + 1
                turn_xn(stage)
                h_in_place(stage)
                for t in range(TB):
                    for k in range(KD):
                        ins = mm(PS[:, 7, t * NL:(t + 1) * NL], HT[:, k, t * P:(t + 1) * P], WR[:, L, k, :],
                                 k == 0, k == KD - 1, skip_group_check=True)
                ins.then_inc(logits_done, 1)
                if L == 0:
                    modulation(10)
                pe.wait_ge(onehot_ready, L + 1)
                chosen = ONEHOT[:, 2, :, :]
                mm(PS[:, 7, P:P + NE], BEFORE[:, :], chosen[:, 0, :], True, True, skip_group_check=True)
                mm(PS[:, 7, P + NE:P + 2 * NE], BEFORE[:, :], chosen[:, 1, :], True, False, skip_group_check=True)
                mm(PS[:, 7, P + NE:P + 2 * NE], ONES[:, :], chosen[:, 0, :], False, True, skip_group_check=True)
                mm(PS[:, 7, 2 * P:2 * P + NE], ONES[:, :], chosen[:, 0, :], True, False, skip_group_check=True)
                mm(PS[:, 7, 2 * P:2 * P + NE], ONES[:, :], chosen[:, 1, :], False, True,
                   skip_group_check=True).then_inc(rank_done, 1)
                if L == 0:
                    modulation(11)

                def gather(buf, done):
                    for k in range(KD):
                        for t in range(TB):
                            for s in range(3):
                                ins = mm(PS[:, 2 + k // 4, (k % 4) * P:(k % 4 + 1) * P], XN3[:, s, t, k, :], SG[:, buf, t, :],
                                         t == 0 and s == 0, t == TB - 1 and s == 2)
                    ins.then_inc(done, 1)

                def widen(bank, w, xt, done):
                    for k in range(KD):
                        for e in range(2):
                            ins = mm(PS[e * SLOT:(e + 1) * SLOT, bank, :], xt[:, k, e * SLOT:(e + 1) * SLOT],
                                     w[:, e, k * F:(k + 1) * F], k == 0, k == KD - 1, skip_group_check=True)
                    ins.then_inc(done, 1)

                def narrow(w, done):
                    for h in range(2):
                        for k in range(KF):
                            for e in range(2):
                                ins = mm(PS[e * SLOT:(e + 1) * SLOT, 6 + h, :], HIDT[:, k, e * SLOT:(e + 1) * SLOT],
                                         w[:, e, k * D + h * HALF:k * D + (h + 1) * HALF], k == 0, k == KF - 1,
                                         skip_group_check=True)
                    ins.then_inc(done, 1)

                def turn_weights():
                    for t in range(TB):
                        ins = pe.transpose(PS[:, 5, t * P:(t + 1) * P], SW[:, t, :], IDENT[:, :])
                    return ins

                def turn_hidden():
                    for k in range(KF):
                        ins = pe.transpose(PS[:, 4, k * P:(k + 1) * P], HID[:, k, :], IDENT[:, :])
                    return ins

                def combine(buf, done):
                    for u, bank in enumerate((0, 1, 5, 0)):
                        t, h = divmod(u, 2)
                        if u == 3:
                            pe.wait_ge(x_added, done + 1)
                        mm(PS[:, bank, :], SWT[:, buf, t, :], YS[:, h * HALF:(h + 1) * HALF], True, True).then_inc(combined, 1)

                pe.wait_ge(split_act, 3 * (L + 1))
                pe.wait_ge(slots_built, 2 * ((EP + 1) * L + 1))
                gather(0, gathered)
                pe.wait_ge(moe_cleared, 2 * (L + 1))
                with pe.Fori(0, EP // UNROLL) as i:
                    for j in range(UNROLL):
                        n = i * UNROLL + (EP * L + j)
                        adds = i * (4 * UNROLL) + (4 * (EP + 1) * L + 4 * j)
                        slabs = [MOE0[L] + 3 * j + w for w in range(3)]
                        land = [i * (16 * GROUP) + landed(s) for s in slabs]
                        pe.wait_ge(xt_dve, i * (4 * UNROLL) + 4 * ((EP + 1) * L + j + 1))
                        pe.wait_ge(xt_act, i * (4 * UNROLL) + 4 * ((EP + 1) * L + j + 1))
                        pe.wait_ge(x_added, adds)
                        pe.wait_ge(slab_in[slabs[0] % RING], land[0])
                        widen(0, pair_slab(slabs[0]), XT[:, j % 2], gate_done)
                        pe.wait_ge(slab_in[slabs[1] % RING], land[1])
                        widen(1, pair_slab(slabs[1]), XT[:, j % 2], up_done)
                        pe.wait_ge(slots_built, i * (2 * UNROLL) + 2 * ((EP + 1) * L + j + 2))
                        gather((j + 1) % 2, gathered)
                        pe.wait_ge(weights_built, n * 2 + 2)
                        turn_weights().then_inc(weights_turned, 1)
                        pe.wait_ge(hidden_ready, n + 1)
                        turn_hidden().then_inc(hidden_turned, 1)
                        pe.wait_ge(y_ready, n * 2)
                        pe.wait_ge(weightsT_ready, n + 1)
                        combine((j + 1) % 2, adds)
                        pe.wait_ge(hiddenT_ready, n + 1)
                        pe.wait_ge(slab_in[slabs[2] % RING], land[2])
                        narrow(pair_slab(slabs[2]), down_done)
                pe.wait_ge(y_ready, 2 * EP * (L + 1))
                pe.wait_ge(x_added, 4 * (EP + 1) * L + 4 * EP)
                combine((UNROLL + 1) % 2, 4 * (EP + 1) * L + 4 * EP)

                m = more[L]
                pe.wait_ge(count_ready, L + 1)
                count = pe.value_load(CNTI[0:1, 0:1], min_val=0, max_val=S)
                with pe.If(count > SLOT):
                    pe.wait_ge(x_added, 4 * (EP + 1) * (L + 1))
                    with pe.Fori(0, ROUNDS - 1) as r:
                        with pe.Fori(0, EP) as q:
                            step = r * EP + q
                            st = r * (8 + 12 * EP) + q * 12 + 8
                            pe.wait_ge(m["added"], step * 4)
                            pe.wait_ge(m["slots"], step * 4 + 4)
                            gather(0, m["gathered"])
                            pe.wait_ge(m["slabs"], step * 48 + 48)
                            pe.wait_ge(m["dve"], st + 8)
                            widen(0, pair_slab(0), XT[:, 0], m["gate"])
                            widen(1, pair_slab(1), XT[:, 0], m["up"])
                            turn_weights()
                            pe.wait_ge(m["dve"], st + 10)
                            turn_hidden().then_inc(m["turned"], 1)
                            pe.wait_ge(m["copied"], step * 2 + 2)
                            narrow(pair_slab(2), m["down"])
                            pe.wait_ge(m["dve"], st + 12)
                            for u in range(4):
                                t, h = divmod(u, 2)
                                mm(PS[:, u, :], SWT[:, 0, t, :], YS[:, h * HALF:(h + 1) * HALF],
                                   True, True).then_inc(m["combined"], 1)
                    pe.wait_ge(m["added"], 4 * EP * (ROUNDS - 1))

            moe(0)

            turn_xn(2)
            h_in_place(2)

            def head_sums(u):
                pe.wait_ge(qk_squared, u + 1)
                if u >= 2:
                    pe.wait_ge(qk_rstd, u - 1)
                mm(PS[:, 4 + u % 2, 0:S], HEADSUM[:, :], SQo[u % 2][:, :], True, True).then_inc(qk_mean, 1)

            for u in range(20):
                s = slab_index("odd_in", 0 if u < 8 else 1 if u < 16 else 2)
                if u in (0, 8, 16):
                    slab_ready(s)
                if u >= 4:
                    pe.wait_ge(qk_out, u - 3)
                if u < 16:
                    ins = project_T(u % 4, wide(s), (u % 8) * P)
                else:
                    ins = project(u % 4, wide(s), ((u - 16) % 2) * HALF, (u - 16) // 2)
                ins.then_inc(proj_done, 1)
                if 1 <= u <= 16:
                    head_sums(u - 1)

            def scores(h):
                if h == 0:
                    pe.wait_ge(qk_out, 16)
                    pe.wait_ge(v_out, 4)
                if h >= 2:
                    pe.wait_ge(scores_max, h - 1)
                for t in range(TB):
                    for cc in range(2):
                        r = slice(cc * HD, (cc + 1) * HD)
                        ins = mm(PS[:, 2 * (h % 2) + cc, t * P:(1 + 2 * t) * P], QTo[r, h, t * P:(t + 1) * P],
                                 KTo[r, h, 0:(t + 1) * P], True, True, skip_group_check=True)
                ins.then_inc(scores_done, 1)

            scores(0)
            for h in range(NH):
                if h + 1 < NH:
                    scores(h + 1)
                pe.wait_ge(diff_ready, 2 * (h + 1))
                if h:
                    pe.wait_ge(diffT_ready, h)
                for n in range(3):
                    ins = pe.transpose(PS[:, 4, n * P:(n + 1) * P], PRo[:, n * P:(n + 1) * P], IDENT[:, :])
                ins.then_inc(diff_turned, 1)
                pe.wait_ge(diffT_ready, h + 1)
                if h:
                    pe.wait_ge(o_out, h)
                mm(PS[:, 6, 0:S], Vo[:, 0, h * P:(h + 1) * P], PTo[:, 0:S], True, True, skip_group_check=True)
                mm(PS[:, 6, P:S], Vo[:, 1, h * P:(h + 1) * P], PTo[:, S:S + P], False, True,
                   skip_group_check=True).then_inc(o_done, 1)
                pe.wait_ge(o_squared, h + 1)
                mm(PS[:, 7, 0:S], ONES[:, :], SQo[0][:, :], True, True, skip_group_check=True).then_inc(o_mean, 1)
            pe.wait_ge(o_out, NH)
            mix_out(1, slab_index("odd_out", 0))
            moe(1)


N_VECTORS = 2 * 8 + 1 + 1 + 4 + 1 + 4 + 4


_INS = ["x", "c", "w_ada", "b_ada", "mix_norm_g", "ffn_norm_g", "even_w_in", "conv_b_glu", "conv_dw", "conv_dw_b",
        "conv_ln_g", "conv_ln_b", "even_w_out", "odd_w_in", "qk_norm_q", "qk_norm_k", "lambda_q1", "lambda_k1",
        "lambda_q2", "lambda_k2", "diff_sub_g", "odd_w_out", "moe_w_group", "moe_b_group", "moe_w_router",
        "moe_b_router", "moe_w_gate", "moe_w_up", "moe_w_down"]


def kernel(**inputs):
    import numpy as np
    import concourse.bacc as bacc
    from concourse.bass_utils import run_bass_kernel_spmd

    nc = bacc.Bacc("TRN2", target_bir_lowering=False, num_devices=1)
    arrays, args = {}, []
    for name in _INS:
        a = np.ascontiguousarray(inputs[name])
        arrays[f"in_{name}"] = a
        args.append(nc.dram_tensor(f"in_{name}", a.shape, mybir.dt.from_np(a.dtype), kind="ExternalInput").ap())
    result = nc.dram_tensor("out", inputs["x"].shape, F32, kind="ExternalOutput").ap()
    build_trunk(nc, *args, result)
    r = run_bass_kernel_spmd(nc, [arrays], core_ids=[0])
    return r.results[0]["out"]
```

```python
import math
from contextlib import ExitStack

import concourse.bass as bass
from concourse import mybir

P = 128
F32 = mybir.dt.float32
BF16 = mybir.dt.bfloat16
I32 = mybir.dt.int32
U32 = mybir.dt.uint32
ALU = mybir.AluOpType
ACT = mybir.ActivationFunctionType
AX = mybir.AxisListType

EPS = 1e-6
FAR = 1.0e6
NEG = -1.0e30
LOWEST = -3.0e38
SIGMOID_FLOOR = -43.0


def build_trunk(nc, x, c, w_ada, b_ada, mix_norm_g, ffn_norm_g, even_w_in, conv_b_glu, conv_dw, conv_dw_b,
                conv_ln_g, conv_ln_b, even_w_out, odd_w_in, qk_norm_q, qk_norm_k, lambda_q1, lambda_k1,
                lambda_q2, lambda_k2, diff_sub_g, odd_w_out, moe_w_group, moe_b_group, moe_w_router,
                moe_b_router, moe_w_gate, moe_w_up, moe_w_down, out):
    _, S, D = x.shape
    TB = S // P
    KD = D // P
    TAPS, CONV = conv_dw.shape[1:]
    CB = CONV // P
    PAD = TAPS - 1
    HD = 64
    NPAIR = (even_w_in.shape[2] - 2 * CONV) // 3 // P
    NH = D // P
    NG = moe_w_group.shape[2]
    NE, _, F = moe_w_gate.shape[1:]
    EPG = NE // NG
    KF = F // P
    SLOT = 64
    EP = NE // 2
    ROUNDS = S // SLOT
    LAM0 = 0.8 - 0.6 * math.exp(-0.3)
    QSCALE = HD ** -0.5
    NL = NG + NE
    HALF = 512
    RING = 4
    UNROLL = 4

    ctx = ExitStack()
    with ctx:
        def sb(name, shape, dt=F32):
            return ctx.enter_context(nc.sbuf_tensor(name, shape, dt))

        def sem(name):
            return ctx.enter_context(nc.semaphore(name))

        RINGT = sb("weight_ring", [P, RING, 8 * 1024])
        X = sb("x_tokens", [P, TB, D])
        HT = sb("h_or_mix_T", [P, KD, S])
        GATE = sb("gate_rows", [P, 2, D])
        PART = sb("ada_partials", [P, 1024])
        SHIFT = sb("shift", [P, 4, KD])
        SCALE = sb("scale", [P, 4, KD])
        GAIN = sb("norm_gain", [P, 4, KD])
        BADA = sb("ada_bias", [P, 12, KD])
        CCOL = sb("cond_cols", [P, 3, KD])
        IDENT = sb("ident", [P, P])
        NEGS = sb("neg_tri_and_one", [P, 2, P])
        NEGTRI, NEGONE = NEGS[:, 0, :], NEGS[:, 1, :]
        ONES = sb("ones", [P, P])
        BEFORE = sb("before", [P, P])
        HEADSUM = sb("head_sum", [P, P])
        SEL = sb("select_partials", [P, P])
        SLOTNO = sb("slot_number", [P, P])
        EXPNO = sb("expert_number", [P, NE])
        GRPNO = sb("group_of_expert", [P, NE])
        NDIST = sb("neg_distance", [P, 3 * P])
        EPSC = sb("eps", [P, 1])
        CV1 = sb("conv_taps", [P, TAPS * CB])
        CV2 = sb("small_cols", [P, 32])
        WR = sb("router_w", [P, 2, KD, NL])
        RB = sb("router_b", [P, 2, NL])
        LAMV = sb("lambda_rows", [P, 4, HD])
        LAM = sb("lambda", [P, 8])
        STAT = sb("norm_stat", [P, 4])
        LG = sb("router_logits", [P, TB, NL])
        GL8 = sb("group_logits", [P, TB, 8])
        GM8 = sb("group_top", [P, TB, 8])
        GI8 = sb("group_index", [P, TB, 8], U32)
        EM = sb("expert_logits", [P, TB, NE])
        EM8 = sb("expert_top", [P, TB, 8])
        EI8 = sb("expert_index", [P, TB, 8], U32)
        RT = sb("route_scratch", [P, 12, TB])
        EXPSEL = sb("chosen_experts", [P, TB, 2])
        EXPW = sb("chosen_weights", [P, TB, 2])
        ONEHOT = sb("expert_onehot", [P, 3, TB, NE])
        RANK = sb("rank_in_expert", [P, TB, 2])
        POS = sb("slot_of_token", [P, TB, 2])
        POST = sb("slot_scratch", [P, 3, TB, 2])
        CNT = sb("largest_count", [P, 1])
        CNTI = sb("largest_count_int", [P, 1], I32)

        U = sb("phase_region", [P, 9984])

        def part_of(at, *shape, dt=F32):
            n = math.prod(shape)
            words = n if dt == F32 else n // 2
            v = U[:, at:at + words]
            if dt != F32:
                v = v.bitcast(dt)
            if len(shape) == 1:
                return v
            names = "abcd"[:len(shape)]
            return v.rearrange(f"p ({' '.join(names)}) -> p {' '.join(names)}", **dict(zip(names, shape)))

        XN = part_of(0, TB, KD, P)
        QTe = part_of(0, NPAIR, S)
        KTe = part_of(1024, NPAIR, S)
        Ve = part_of(2048, TB, NPAIR * P)
        CIN = part_of(3072, CB, S + PAD)
        CSQ = part_of(3072, CB, S)
        CACC = part_of(4288, CB, S)
        SPe = part_of(5312, 2, 2, 3 * P)
        PRe = part_of(6848, 2, 2, 3 * P)
        RSTD = part_of(8384, S)
        CROW = part_of(6848, 2, P)
        CREP = part_of(8640, KD, 32)
        CREP1 = NEGS[:, :, :].rearrange("p a (k n) -> p (a k) n", n=32)
        QTo = part_of(0, NH, S)
        KTo = part_of(2048, NH, S)
        Vo = part_of(4096, TB, D)
        SCo = part_of(6144, 2, 2, 3 * P)
        PRo = part_of(7680, 3 * P)
        PTo = part_of(8064, 3 * P)
        SQo = [part_of(8448, S), part_of(8960, S)]
        RSo = [part_of(8704, S), part_of(9216, S)]
        BIAS = part_of(9216, 2, 3 * P)
        STo = ONEHOT[:, 0, :, :]
        XT = part_of(0, 2, KD, P)
        XN3 = part_of(2048, 3, TB, KD, P, dt=BF16)
        TH = part_of(5120, F)
        T1 = part_of(5632, F)
        HID = part_of(6144, KF, P)
        HIDT = part_of(6656, KF, P)
        YS = part_of(7168, D)
        SG = part_of(8192, 2, TB, P, dt=BF16)
        SW = part_of(8448, TB, P)
        SWT = part_of(8704, 2, TB, P)
        TMPA = part_of(9216, TB, P)
        TMPB = part_of(9472, TB, P)
        TMPC = part_of(9728, TB, P)

        PS = ctx.enter_context(nc.psum_tensor("psum", [P, 8, 512], F32))

        slab_in = [sem(f"slab_in_{i}") for i in range(RING)]
        cond_in = sem("cond_in")
        x_in = sem("x_in")
        norm_in = sem("norm_in")
        rows_in = sem("rows_in")
        vectors_in = sem("vectors_in")
        gate_bias_in = sem("gate_bias_in")
        pool_step = sem("pool_step")
        consts_ready = sem("consts_ready")
        dve_step = sem("dve_step")
        act_step = sem("act_step")
        cond_exp = sem("cond_exp")
        cond_in_place = sem("cond_in_place")
        cond_negated = sem("cond_negated")
        ada_summed = sem("ada_summed")
        ada_copied = sem("ada_copied")
        ada_joined = sem("ada_joined")
        ada_ready = sem("ada_ready")
        rows_turned = sem("rows_turned")
        cols_ready = sem("cols_ready")
        norm_stat = sem("norm_stat")
        xn_ready = sem("xn_ready")
        xn_turned = sem("xn_turned")
        h_dve = sem("h_dve")
        h_act = sem("h_act")
        proj_done = sem("proj_done")
        qkv_out = sem("qkv_out")
        glu_out = sem("glu_out")
        glu_exp = sem("glu_exp")
        z_ready = sem("z_ready")
        softlog = sem("softlog")
        fail_sum_in = sem("fail_sum_in")
        fails_masked = sem("fails_masked")
        logs_ready = sem("logs_ready")
        logs_min = sem("logs_min")
        probs_exp = sem("probs_exp")
        probs_masked = sem("probs_masked")
        pv_done = sem("pv_done")
        heads_out = sem("heads_out")
        conv_done = sem("conv_done")
        conv_mean = sem("conv_mean")
        conv_centred = sem("conv_centred")
        conv_squared = sem("conv_squared")
        conv_var = sem("conv_var")
        conv_rstd = sem("conv_rstd")
        conv_floor = sem("conv_floor")
        conv_exp = sem("conv_exp")
        conv_out = sem("conv_out")
        wout_done = sem("wout_done")
        x_mixed = sem("x_mixed")
        qk_squared = sem("qk_squared")
        qk_mean = sem("qk_mean")
        qk_rstd = sem("qk_rstd")
        qk_out = sem("qk_out")
        v_out = sem("v_out")
        lam_sum = sem("lam_sum")
        lam_exp = sem("lam_exp")
        head_bias = sem("head_bias")
        scores_done = sem("scores_done")
        scores_max = sem("scores_max")
        scores_exp = sem("scores_exp")
        diff_ready = sem("diff_ready")
        diff_turned = sem("diff_turned")
        diffT_ready = sem("diffT_ready")
        o_done = sem("o_done")
        o_squared = sem("o_squared")
        o_mean = sem("o_mean")
        o_rstd = sem("o_rstd")
        o_out = sem("o_out")
        logits_done = sem("logits_done")
        group_top = sem("group_top")
        group_exp = sem("group_exp")
        expert_top = sem("expert_top")
        expert_exp = sem("expert_exp")
        onehot_ready = sem("onehot_ready")
        rank_done = sem("rank_done")
        count_ready = sem("count_ready")
        split_act = sem("split_act")
        split_pool = sem("split_pool")
        slots_built = sem("slots_built")
        weights_built = sem("weights_built")
        gathered = sem("gathered")
        xt_dve = sem("xt_dve")
        xt_act = sem("xt_act")
        gate_done = sem("gate_done")
        up_done = sem("up_done")
        tanh_done = sem("tanh_done")
        t1_done = sem("t1_done")
        hidden_ready = sem("hidden_ready")
        hidden_turned = sem("hidden_turned")
        hiddenT_ready = sem("hiddenT_ready")
        weights_turned = sem("weights_turned")
        weightsT_ready = sem("weightsT_ready")
        down_done = sem("down_done")
        y_ready = sem("y_ready")
        combined = sem("combined")
        x_added = sem("x_added")
        slot_step = sem("slot_step")
        more = [{n: sem(f"more{L}_{n}") for n in ("slabs", "slots", "dve", "gathered", "gate", "tanh", "up", "turned",
                                                   "copied", "down", "combined", "added")} for L in range(2)]
        out_stored = sem("out_stored")

        fills = {0: 2, 1: 3, 2: 4, 3: 5}
        fills1 = {0: 8, 2: 9, 4: 10, 6: 11}
        head_slabs = ([("ada", a, ada_summed, a + 1) for a in range(2)]
                      + [("even_in", 1, proj_done, 6), ("even_in", 2, proj_done, 10), ("even_in", 0, proj_done, 18)]
                      + [("ada", a, ada_summed, a + 1) for a in range(2, 6)]
                      + [("even_out", 0, wout_done, 4)])
        mid_slabs = ([("ada", a, ada_summed, a + 1) for a in range(6, 8)]
                     + [("odd_in", 0, proj_done, 26), ("odd_in", 1, proj_done, 34), ("odd_in", 2, proj_done, 38)]
                     + [("ada", a, ada_summed, a + 1) for a in range(8, 12)]
                     + [("odd_out", 0, wout_done, 8)])
        MOE0 = [len(head_slabs), len(head_slabs) + 3 * EP + len(mid_slabs)]
        MID0 = MOE0[0] + 3 * EP
        assert (3 * UNROLL) % RING == 0 and EP % UNROLL == 0
        GROUP = 3 * UNROLL // RING
        ADDS = 4 * (EP + 1) + 1

        def place(n):
            return RINGT[:, n % RING, :]

        def landed(n):
            return 16 * (n // RING + 1)

        def slab_index(kind, arg):
            for n, s in enumerate(head_slabs):
                if s[:2] == (kind, arg):
                    return n
            for n, s in enumerate(mid_slabs):
                if s[:2] == (kind, arg):
                    return MID0 + n

        ada_src = w_ada.rearrange("l (p k) n -> l p k n", k=KD)
        even_in_src = even_w_in[0].rearrange("(p k) n -> p k n", k=KD)
        odd_in_src = odd_w_in[0].rearrange("(p k) n -> p k n", k=KD)
        out_srcs = {"even_out": even_w_out[0].rearrange("(k p) n -> p k n", p=P),
                    "odd_out": odd_w_out[0].rearrange("(k p) n -> p k n", p=P)}
        gate_src = moe_w_gate.rearrange("l e (p k) f -> l p e (k f)", k=KD)
        up_src = moe_w_up.rearrange("l e (p k) f -> l p e (k f)", k=KD)
        down_src = moe_w_down.rearrange("l e (p k) n -> l p e (k n)", k=KF)

        def wide(n, cols=1024):
            return place(n)[:, 0:KD * cols].rearrange("p (k n) -> p k n", k=KD)

        def pair_slab(n):
            return place(n).rearrange("p (e n) -> p e n", e=2)

        block = ctx.enter_context(nc.Block())

        def overflow_loads(sp, L):
            m = more[L]
            sp.wait_ge(count_ready, L + 1)
            count = sp.value_load(CNTI[0:1, 0:1], min_val=0, max_val=S)
            with sp.If(count > SLOT):
                with sp.Fori(0, ROUNDS - 1) as r:
                    with sp.Fori(0, EP) as q:
                        step = r * EP + q
                        sp.wait_ge(down_done, EP * (L + 1))
                        sp.wait_ge(m["slots"], step * 4 + 4)
                        for w, src in enumerate((gate_src, up_src, down_src)):
                            sp.dma_start(pair_slab(w), src[L, :, bass.ds(q * 2, 2), :]).then_inc(m["slabs"], 16)
                sp.wait_ge(m["added"], 4 * EP * (ROUNDS - 1))

        @block.sync
        def _(sp):
            def load_fixed(n, kind, arg):
                if kind == "ada":
                    src = ada_src[arg // 6, :, :, (arg % 6) * D:(arg % 6 + 1) * D]
                    dst = wide(n)
                elif kind in ("even_in", "odd_in"):
                    src = (even_in_src if kind == "even_in" else odd_in_src)
                    cols = min(1024, src.shape[2] - 1024 * arg)
                    src = src[:, :, 1024 * arg:1024 * arg + cols]
                    dst = wide(n, cols)
                else:
                    src, dst = out_srcs[kind], wide(n)
                sp.dma_start(dst, src).then_inc(slab_in[n % RING], 16)

            def load_pair_slab(L, k, pair):
                n = MOE0[L] + k
                src = (gate_src, up_src, down_src)[k % 3]
                sp.dma_start(pair_slab(n), src[L, :, bass.ds(pair * 2, 2), :]).then_inc(slab_in[n % RING], 16)

            def load_experts(L):
                before = (head_slabs, mid_slabs)[L]
                for k in range(RING):
                    sp.wait_ge(*before[len(before) - RING + k][2:])
                    load_pair_slab(L, k, k // 3)

                def follow(turn, k):
                    sp.wait_ge((gate_done, up_done, down_done)[k % 3], turn * UNROLL + (EP * L + k // 3 + 1))
                    load_pair_slab(L, k + RING, turn * UNROLL + (k + RING) // 3)

                with sp.Fori(0, EP // UNROLL - 1) as i:
                    for k in range(3 * UNROLL):
                        follow(i, k)
                for k in range(3 * UNROLL - RING):
                    follow(EP // UNROLL - 1, k)

            sp.dma_start(CCOL[:, 0, :], c.rearrange("o (p k) -> p (o k)", k=KD)).then_inc(cond_in, 16)
            with nc.allow_non_contiguous_dma(reason="small vectors"):
                for L in range(2):
                    sp.dma_start(BADA[:, 6 * L:6 * L + 6, :], b_ada[L].rearrange("(j p k) -> p j k", p=P, k=KD)).then_inc(norm_in, 16)
                    sp.dma_start(GAIN[:, 2 * L, :], mix_norm_g[L].rearrange("(p k) -> p k", k=KD)).then_inc(norm_in, 16)
                    sp.dma_start(GAIN[:, 2 * L + 1, :], ffn_norm_g[L].rearrange("(p k) -> p k", k=KD)).then_inc(norm_in, 16)
            load_fixed(0, *head_slabs[0][:2])
            sp.dma_start(X[:, :, :], x[0].rearrange("(t p) d -> p t d", p=P)).then_inc(x_in, 16)
            for n, (kind, arg, _, _) in enumerate(head_slabs):
                if n == 0:
                    continue
                if n >= RING:
                    sp.wait_ge(*head_slabs[n - RING][2:])
                load_fixed(n, kind, arg)
            load_experts(0)
            overflow_loads(sp, 0)
            for n, (kind, arg, _, _) in enumerate(mid_slabs):
                if n < RING:
                    q, w = divmod(3 * EP - RING + n, 3)
                    sp.wait_ge((gate_done, up_done, down_done)[w], q + 1)
                else:
                    sp.wait_ge(*mid_slabs[n - RING][2:])
                load_fixed(MID0 + n, kind, arg)
            load_experts(1)
            overflow_loads(sp, 1)
            for t in range(TB):
                sp.wait_ge(x_added, ADDS + ADDS - 4 + 2 * (t + 1))
                sp.dma_start(out[0, t * P:(t + 1) * P, :], X[:, t, :]).then_inc(out_stored, 16)
            sp.wait_ge(out_stored, 16 * TB)

        @block.gpsimd
        def _(pool):
            g = nc.gpsimd
            steps = [0]

            def link(ins):
                steps[0] += 1
                ins.then_inc(pool_step, 1)
                pool.wait_ge(pool_step, steps[0])

            for t, v in ((IDENT, 0.0), (NEGTRI, -1.0), (NEGONE, -1.0), (ONES, 1.0), (BEFORE, 1.0),
                         (HEADSUM, 0.0), (SEL, 0.0)):
                link(g.memset(t[:, :], v))
            link(g.memset(EPSC[:, :], EPS))
            link(g.affine_select(out=IDENT[:, :], in_=IDENT[:, :], compare_op=ALU.not_equal, fill=1.0, base=0,
                                 pattern=[[-1, P]], channel_multiplier=1))
            link(g.affine_select(out=NEGTRI[:, :], in_=NEGTRI[:, :], compare_op=ALU.is_ge, fill=0.0, base=0,
                                 pattern=[[-1, P]], channel_multiplier=1))
            link(g.affine_select(out=BEFORE[:, :], in_=BEFORE[:, :], compare_op=ALU.is_gt, fill=0.0, base=0,
                                 pattern=[[1, P]], channel_multiplier=-1))
            for h in range(2):
                link(g.memset(HEADSUM[h * HD:(h + 1) * HD, h * HD:(h + 1) * HD], 1.0))
            for r in range(4):
                link(g.memset(SEL[32 * r:32 * r + 1, :], 1.0))
            link(g.iota(SLOTNO[:, :], pattern=[[1, P]], base=0, channel_multiplier=0, allow_small_or_imprecise_dtypes=True))
            link(g.iota(EXPNO[:, :], pattern=[[1, NE]], base=0, channel_multiplier=0, allow_small_or_imprecise_dtypes=True))
            link(g.iota(GRPNO[:, :], pattern=[[1, NG], [0, EPG]], base=0, channel_multiplier=0,
                        allow_small_or_imprecise_dtypes=True))
            link(g.iota(NDIST[:, 0:P], pattern=[[-1, P]], base=0, channel_multiplier=1, allow_small_or_imprecise_dtypes=True))
            link(g.iota(NDIST[:, P:3 * P], pattern=[[-1, 2 * P]], base=P, channel_multiplier=1,
                        allow_small_or_imprecise_dtypes=True))
            g.memset(GL8[:, :, :], LOWEST).then_inc(consts_ready, 1)

            def keep_past(tile, i, ready, done):
                pool.wait_ge(ready, i + 1)
                for h in range(2):
                    for at in (0, 2 * P):
                        v = tile[:, i % 2, h, at:at + P]
                        g.affine_select(out=v, in_=v, compare_op=ALU.is_gt, fill=0.0, base=0,
                                        pattern=[[1, P]], channel_multiplier=-1).then_inc(done, 1)

            for i in range(NPAIR):
                keep_past(SPe, i, fail_sum_in, fails_masked)
                keep_past(PRe, i, probs_exp, probs_masked)

            def split_tokens(L):
                for part in range(2):
                    pool.wait_ge(split_act, 3 * L + part + 1)
                    if part == 0:
                        pool.wait_ge(xn_turned, 4 * (2 * L + 2))
                    g.tensor_tensor(XN[:, :, :, :], XN[:, :, :, :], XN3[:, part], ALU.subtract).then_inc(split_pool, 1)

            split_tokens(0)

            for h in range(NH):
                if h == 0:
                    pool.wait_ge(qk_out, 16)
                    pool.wait_ge(cols_ready, 4)
                if h >= 2:
                    pool.wait_ge(scores_max, h - 1)
                g.tensor_scalar(BIAS[:, h % 2, :], NDIST[:, :], 2.0 ** (-8.0 * (h + 1) / NH), 0.0,
                                ALU.mult, ALU.add).then_inc(head_bias, 1)
            split_tokens(1)

        @block.scalar
        def _(act):
            a = nc.scalar
            steps = [0]

            def link(ins):
                steps[0] += 1
                ins.then_inc(act_step, 1)
                act.wait_ge(act_step, steps[0])

            def load_vectors(pairs, arrived):
                with nc.allow_non_contiguous_dma(reason="small vectors"):
                    for dst, src in pairs:
                        act.dma_start(dst, src).then_inc(arrived, 16)

            rows = [(CROW[0:TAPS * CB, 0, :], conv_dw[0].rearrange("t (b c) -> (t b) c", c=P)),
                    (CROW[0:8, 1, :], conv_b_glu[0].rearrange("(b c) -> b c", c=P)),
                    (CROW[8:12, 1, :], conv_dw_b[0].rearrange("(b c) -> b c", c=P)),
                    (CROW[12:16, 1, :], conv_ln_g[0].rearrange("(b c) -> b c", c=P)),
                    (CROW[16:20, 1, :], conv_ln_b[0].rearrange("(b c) -> b c", c=P)),
                    (CROW[20:21, 1, :], diff_sub_g)]
            rows += [(CROW[r:r + 1, 1, h * HD:(h + 1) * HD], v)
                     for r, v in ((21, qk_norm_q), (22, qk_norm_k)) for h in range(2)]
            assert len(rows) == N_ROWS
            load_vectors(rows, rows_in)
            a.preload_act_table_set("natural_log_exp_and_others")
            act.wait_ge(cond_negated, 1)
            a.activation(CCOL[:, 1, :], CCOL[:, 1, :], ACT.Exp, scale=-1.0).then_inc(cond_exp, 1)

            def norm_statistics(stage):
                for t in range(TB):
                    if stage in (1, 3):
                        act.wait_ge(x_mixed, 2 * stage - 2 + 2 * (t + 1))
                    link(a.activation(XN[:, t, :, :].rearrange("p k q -> p (k q)"), X[:, t, :], ACT.Square,
                                      accum_out=STAT[:, t:t + 1]))
                link(a.activation(STAT[:, 2:4], STAT[:, 0:2], ACT.Ln, scale=1.0 / D, bias=EPSC[:, 0:1]))
                a.activation(STAT[:, 2:4], STAT[:, 2:4], ACT.Exp, scale=-0.5).then_inc(norm_stat, 1)

            def modulate(stage):
                act.wait_ge(ada_ready, 3 * stage + 2)
                for k in range(KD // 2, KD):
                    act.wait_ge(xn_turned, 4 * stage + k // 2 + 1)
                    a.activation(HT[:, k, :], PS[:, k // 2, (k % 2) * S:(k % 2 + 1) * S], ACT.Identity, scale=SCALE[:, stage, k:k + 1],
                                 bias=SHIFT[:, stage, k:k + 1]).then_inc(h_act, 1)

            def copy_partials(n):
                act.wait_ge(ada_summed, n + 1)
                if n:
                    act.wait_ge(ada_joined, n)
                a.copy(PART[:, :].rearrange("p (b n) -> p b n", b=2), PS[:, 4:6, :]).then_inc(ada_copied, 1)

            act.wait_ge(x_in, 16)
            act.wait_ge(consts_ready, 1)
            norm_statistics(0)
            copy_partials(0)
            copy_partials(1)
            modulate(0)
            later = [(GATE[:, 0, :], b_ada[0, 2 * D:3 * D].partition_broadcast(P)),
                     (GATE[:, 1, :], b_ada[0, 5 * D:6 * D].partition_broadcast(P))]
            for L in range(2):
                later += [(WR[:, L, :, 0:NG], moe_w_group[L].rearrange("(p k) g -> p k g", k=KD)),
                          (WR[:, L, :, NG:NL], moe_w_router[L].rearrange("(p k) e -> p k e", k=KD)),
                          (RB[:, L, 0:NG], moe_b_group[L].partition_broadcast(P)),
                          (RB[:, L, NG:NL], moe_b_router[L].partition_broadcast(P))]
            later += [(LAMV[:, n, :], v[0].partition_broadcast(P))
                      for n, v in enumerate((lambda_q1, lambda_k1, lambda_q2, lambda_k2))]
            assert len(later) == N_VECTORS
            load_vectors(later, vectors_in)
            def take_projection(u):
                act.wait_ge(proj_done, u + 1)
                if u < 2:
                    ins = a.copy(Ve[:, u, :], PS[:, u % 4, :])
                elif u < 14:
                    ins = a.mul(QTe[:, u - 10, :], PS[:, u % 4, 0:S], QSCALE)
                else:
                    ins = a.copy(KTe[:, u - 14, :], PS[:, u % 4, 0:S])
                ins.then_inc(qkv_out, 1)

            def sigmoid(t, done):
                link(a.activation(t, t, ACT.Exp, scale=-1.0))
                link(a.activation(t, t, ACT.Ln, bias=1.0))
                a.activation(t, t, ACT.Exp, scale=-1.0).then_inc(done, 1)

            for u in (0, 1, 10):
                take_projection(u)
            act.wait_ge(glu_out, 8)
            sigmoid(CACC[:, :, :], glu_exp)
            for u in range(11, 18):
                take_projection(u)

            def soft_logs(i):
                act.wait_ge(z_ready, i + 1)
                if i >= 2:
                    act.wait_ge(logs_ready, i - 1)
                b = 2 * (i % 2)
                v = SPe[:, i % 2, :, :]
                link(a.activation(v, PS[:, b:b + 2, 0:3 * P], ACT.Abs))
                link(a.activation(v, v, ACT.Exp, scale=-1.0))
                a.activation(v, v, ACT.Ln, bias=1.0).then_inc(softlog, 1)

            def take_heads(i):
                act.wait_ge(pv_done, i + 1)
                a.copy(HT[:, i, :], PS[:, 7, 0:S]).then_inc(heads_out, 1)

            soft_logs(0)
            soft_logs(1)
            for i in range(NPAIR):
                act.wait_ge(logs_min, i + 1)
                v = PRe[:, i % 2, :, :]
                a.activation(v, v, ACT.Exp).then_inc(probs_exp, 1)
                if i:
                    take_heads(i - 1)
                copy_partials(fills[i])
                if i + 2 < NPAIR:
                    soft_logs(i + 2)
            take_heads(NPAIR - 1)
            act.wait_ge(conv_centred, 1)
            a.activation(CSQ[:, :, :], CACC[:, :, :], ACT.Square).then_inc(conv_squared, 1)
            act.wait_ge(conv_var, 1)
            link(a.activation(RSTD[:, :], PS[:, 7, S:2 * S], ACT.Ln, scale=1.0 / CONV, bias=EPSC[:, 0:1]))
            a.activation(RSTD[:, :], RSTD[:, :], ACT.Exp, scale=-0.5).then_inc(conv_rstd, 1)
            act.wait_ge(conv_floor, 1)
            sigmoid(CSQ[:, :, :], conv_exp)

            def moe(L):
                stage = 2 * L + 1
                norm_statistics(stage)
                if L == 0:
                    act.dma_start(GATE[:, 0, :], b_ada[1, 2 * D:3 * D].partition_broadcast(P)).then_inc(gate_bias_in, 16)
                modulate(stage)
                act.wait_ge(xn_ready, 2 * (stage + 1))
                a.copy(XN3[:, 0], XN[:, :, :, :]).then_inc(split_act, 1)
                act.wait_ge(group_top, L + 1)
                for t in range(TB):
                    a.activation(RT[:, 8 + 2 * t:10 + 2 * t, :].rearrange("p a b -> p (a b)")[:, 0:NG],
                                 GL8[:, t, 0:NG], ACT.Exp, bias=RT[:, 0, t:t + 1],
                                 accum_out=RT[:, 1, t:t + 1]).then_inc(group_exp, 1)
                act.wait_ge(split_pool, 2 * L + 1)
                a.copy(XN3[:, 1], XN[:, :, :, :]).then_inc(split_act, 1)
                act.wait_ge(expert_top, L + 1)
                a.activation(RT[:, 5, :], RT[:, 4, :], ACT.Exp).then_inc(expert_exp, 1)
                act.wait_ge(split_pool, 2 * L + 2)
                a.copy(XN3[:, 2], XN[:, :, :, :]).then_inc(split_act, 1)

                def spread(count, buf):
                    act.wait_ge(gathered, count)
                    for k in range(KD // 2, KD):
                        a.activation(XT[:, buf, k, :], PS[:, 2 + k // 4, (k % 4) * P:(k % 4 + 1) * P], ACT.Identity,
                                     scale=SCALE[:, stage, k:k + 1], bias=SHIFT[:, stage, k:k + 1]).then_inc(xt_act, 1)

                spread((EP + 1) * L + 1, 0)
                a.preload_act_table_set("exp_and_others")
                with act.Fori(0, EP // UNROLL) as i:
                    for j in range(UNROLL):
                        n = i * UNROLL + (EP * L + j)
                        act.wait_ge(gate_done, n + 1)
                        a.activation(TH[:, :], PS[:, 0, :], ACT.Tanh, scale=0.5).then_inc(tanh_done, 1)
                        spread(n + (L + 2), (j + 1) % 2)
                        act.wait_ge(weights_turned, n + 1)
                        a.copy(SWT[:, j % 2, :, :].rearrange("p t s -> p (t s)"), PS[:, 5, 0:TB * P]).then_inc(weightsT_ready, 1)
                        act.wait_ge(hidden_turned, n + 1)
                        a.copy(HIDT[:, :, :].rearrange("p k s -> p (k s)"), PS[:, 4, :]).then_inc(hiddenT_ready, 1)

                m = more[L]
                act.wait_ge(count_ready, L + 1)
                count = act.value_load(CNTI[0:1, 0:1], min_val=0, max_val=S)
                with act.If(count > SLOT):
                    with act.Fori(0, EP * (ROUNDS - 1)) as step:
                        act.wait_ge(m["gate"], step + 1)
                        a.activation(TH[:, :], PS[:, 0, :], ACT.Tanh, scale=0.5).then_inc(m["tanh"], 1)
                        act.wait_ge(m["turned"], step + 1)
                        a.copy(SWT[:, 0, :, :].rearrange("p t s -> p (t s)"), PS[:, 5, 0:TB * P]).then_inc(m["copied"], 1)
                        a.copy(HIDT[:, :, :].rearrange("p k s -> p (k s)"), PS[:, 4, :]).then_inc(m["copied"], 1)
                    act.wait_ge(m["added"], 4 * EP * (ROUNDS - 1))

            moe(0)

            act.wait_ge(x_added, ADDS)
            a.preload_act_table_set("natural_log_exp_and_others")
            act.dma_start(GATE[:, 1, :], b_ada[1, 5 * D:6 * D].partition_broadcast(P)).then_inc(gate_bias_in, 16)
            norm_statistics(2)
            copy_partials(6)
            copy_partials(7)
            modulate(2)
            act.wait_ge(lam_sum, 1)
            a.activation(LAM[:, 2:4], LAM[:, 0:2], ACT.Exp).then_inc(lam_exp, 1)
            for u in range(20):
                act.wait_ge(proj_done, 18 + u + 1)
                if u < 16:
                    if u >= 2:
                        act.wait_ge(qk_mean, u - 1)
                    a.activation(SQo[u % 2][:, :], PS[:, u % 4, 0:S], ACT.Square).then_inc(qk_squared, 1)
                if 1 <= u <= 16:
                    w = u - 1
                    act.wait_ge(qk_mean, w + 1)
                    if w >= 2:
                        act.wait_ge(qk_out, w - 1)
                    link(a.activation(RSo[w % 2][:, :], PS[:, 4 + w % 2, 0:S], ACT.Ln, scale=1.0 / HD, bias=EPSC[:, 0:1]))
                    a.activation(RSo[w % 2][:, :], RSo[w % 2][:, :], ACT.Exp, scale=-0.5).then_inc(qk_rstd, 1)
                if u >= 16:
                    v = u - 16
                    a.copy(Vo[:, v // 2, (v % 2) * HALF:(v % 2 + 1) * HALF], PS[:, u % 4, :]).then_inc(v_out, 1)

            def exps(h):
                act.wait_ge(scores_max, h + 1)
                for cc in range(2):
                    for t in range(TB):
                        v = SCo[:, h % 2, cc, t * P:(1 + 2 * t) * P]
                        k = 2 * cc + t
                        ins = a.activation(v, v, ACT.Exp, bias=STo[:, h % 2, 4 + k:5 + k], accum_out=STo[:, h % 2, 8 + k:9 + k])
                        ins.then_inc(scores_exp, 1)

            def out_rstd(h):
                act.wait_ge(o_mean, h + 1)
                if h:
                    act.wait_ge(o_out, h)
                link(a.activation(RSo[0][:, :], PS[:, 7, 0:S], ACT.Ln, scale=1.0 / P, bias=EPSC[:, 0:1]))
                a.activation(RSo[0][:, :], RSo[0][:, :], ACT.Exp, scale=-0.5).then_inc(o_rstd, 1)

            exps(0)
            exps(1)
            for h in range(NH):
                act.wait_ge(diff_turned, h + 1)
                a.copy(PTo[:, :], PS[:, 2, 0:3 * P]).then_inc(diffT_ready, 1)
                if h:
                    out_rstd(h - 1)
                if h in fills1:
                    copy_partials(fills1[h])
                if h + 2 < NH:
                    exps(h + 2)
                act.wait_ge(o_done, h + 1)
                a.activation(SQo[0][:, :], PS[:, 3, 0:S], ACT.Square).then_inc(o_squared, 1)
            out_rstd(NH - 1)

            moe(1)

        @block.vector
        def _(dve):
            v = nc.vector
            steps = [0]

            def link(ins):
                steps[0] += 1
                ins.then_inc(dve_step, 1)
                dve.wait_ge(dve_step, steps[0])

            dve.wait_ge(cond_in, 16)
            v.tensor_scalar(CCOL[:, 1, :], CCOL[:, 0, :], SIGMOID_FLOOR, None, ALU.max).then_inc(cond_negated, 1)
            dve.wait_ge(cond_exp, 1)
            link(v.tensor_scalar(CCOL[:, 1, :], CCOL[:, 1, :], 1.0, None, ALU.add))
            link(v.reciprocal(CCOL[:, 2, :], CCOL[:, 1, :]))
            link(v.tensor_tensor(CCOL[:, 1, :], CCOL[:, 0, :], CCOL[:, 2, :], ALU.mult))
            v.tensor_copy(CREP[:, :, :], CCOL[:, 1, :].unsqueeze(2).broadcast_to([P, KD, 32])).then_inc(cond_in_place, 1)

            def take_modulation(n):
                L, j = divmod(n, 6)
                dve.wait_ge(ada_joined, n + 1)
                if j in (0, 3):
                    v.tensor_tensor(SHIFT[:, 2 * L + j // 3, :], PS[:, 6, 0:KD], BADA[:, n, :], ALU.add).then_inc(ada_ready, 1)
                elif j in (1, 4):
                    st = 2 * L + j // 3
                    link(v.tensor_tensor(SCALE[:, st, :], PS[:, 6, 0:KD], BADA[:, n, :], ALU.add))
                    v.scalar_tensor_tensor(out=SCALE[:, st, :], in0=SCALE[:, st, :], scalar=1.0, in1=GAIN[:, st, :],
                                           op0=ALU.add, op1=ALU.mult).then_inc(ada_ready, 1)
                else:
                    row = GATE[:, j // 3, :]
                    if L == 0:
                        dve.wait_ge(vectors_in, 16 * N_VECTORS)
                    else:
                        dve.wait_ge(gate_bias_in, 32)
                    link(v.tensor_tensor(row[:, 0:HALF], PS[:, 6, :], row[:, 0:HALF], ALU.add))
                    v.tensor_tensor(row[:, HALF:D], PS[:, 4, :], row[:, HALF:D], ALU.add).then_inc(ada_ready, 1)

            def normalise(stage):
                dve.wait_ge(norm_stat, stage + 1)
                for t in range(TB):
                    v.tensor_scalar(XN[:, t, :, :], X[:, t, :].rearrange("p (q k) -> p k q", k=KD),
                                    STAT[:, 2 + t:3 + t], None, ALU.mult).then_inc(xn_ready, 1)

            def modulate(stage):
                dve.wait_ge(ada_ready, 3 * stage + 2)
                for k in range(KD // 2):
                    dve.wait_ge(xn_turned, 4 * stage + k // 2 + 1)
                    v.tensor_scalar(HT[:, k, :], PS[:, k // 2, (k % 2) * S:(k % 2 + 1) * S], SCALE[:, stage, k:k + 1],
                                    SHIFT[:, stage, k:k + 1], ALU.mult, ALU.add).then_inc(h_dve, 1)

            def add_mixed(L):
                for u in range(4):
                    t, h = divmod(u, 2)
                    dve.wait_ge(wout_done, 4 * L + u + 1)
                    if u == 0:
                        dve.wait_ge(ada_ready, 9 if L else 3)
                    link(v.tensor_tensor(PS[:, u, :], PS[:, u, :], GATE[:, 0, h * HALF:(h + 1) * HALF], ALU.mult))
                    xs = X[:, t, h * HALF:(h + 1) * HALF]
                    v.tensor_tensor(xs, PS[:, u, :], xs, ALU.add).then_inc(x_mixed, 1)

            normalise(0)
            dve.wait_ge(norm_in, 16 * 6)
            take_modulation(0)
            take_modulation(1)
            modulate(0)
            dve.wait_ge(rows_turned, 2)
            v.tensor_copy(CV1[:, :], PS[:, 6, 0:TAPS * CB]).then_inc(cols_ready, 1)
            v.tensor_copy(CV2[:, 0:23], PS[:, 6, P:P + 23]).then_inc(cols_ready, 1)
            dve.wait_ge(cols_ready, 2)
            v.tensor_scalar(CV2[:, 23:24], CV2[:, 20:21], 1.0 - LAM0, None, ALU.mult)
            v.tensor_scalar(CV2[:, 24:25], CV2[:, 21:22], QSCALE, None, ALU.mult).then_inc(cols_ready, 1)
            link(v.memset(CIN[:, :, 0:PAD], 0.0))
            for b in range(CB):
                dve.wait_ge(proj_done, 2 + b + 1)
                v.tensor_scalar(CIN[:, b, PAD:PAD + S], PS[:, (2 + b) % 4, 0:S], CV2[:, b:b + 1], None,
                                ALU.add).then_inc(glu_out, 1)
            for b in range(CB):
                dve.wait_ge(proj_done, 6 + b + 1)
                v.tensor_scalar(CACC[:, b, :], PS[:, (6 + b) % 4, 0:S], CV2[:, 4 + b:5 + b], SIGMOID_FLOOR,
                                ALU.add, ALU.max).then_inc(glu_out, 1)

            def glu():
                dve.wait_ge(glu_exp, 1)
                link(v.tensor_tensor(CIN[:, :, PAD:PAD + S], CIN[:, :, PAD:PAD + S], CACC[:, :, :], ALU.mult))

            def conv_taps(lo, hi):
                for j in range(lo, hi):
                    for b in range(CB):
                        src = CIN[:, b, j:j + S]
                        tap = CV1[:, j * CB + b:j * CB + b + 1]
                        if j == 0:
                            ins = v.tensor_scalar(CACC[:, b, :], src, tap, CV2[:, 8 + b:9 + b], ALU.mult, ALU.add)
                        else:
                            dve.wait_ge(conv_done, CB * (j - 1) + b + 1)
                            ins = v.scalar_tensor_tensor(out=CACC[:, b, :], in0=src, scalar=tap, in1=CACC[:, b, :],
                                                         op0=ALU.mult, op1=ALU.add)
                        ins.then_inc(conv_done, 1)

            def soft_plus(i):
                dve.wait_ge(softlog, i + 1)
                b = 2 * (i % 2)
                s = SPe[:, i % 2, :, :]
                v.scalar_tensor_tensor(out=s, in0=PS[:, b:b + 2, 0:3 * P], scalar=0.0, in1=s,
                                       op0=ALU.max, op1=ALU.add).then_inc(fail_sum_in, 1)

            glu()
            tap_ends = [18, 22, 25, 28, TAPS]
            conv_taps(0, tap_ends[0])
            soft_plus(0)
            soft_plus(1)
            for i in range(NPAIR):
                dve.wait_ge(logs_ready, i + 1)
                if i >= 2:
                    dve.wait_ge(pv_done, i - 1)
                b = 2 * (i % 2)
                v.tensor_scalar(PRe[:, i % 2, :, :], PS[:, b:b + 2, 0:3 * P], 0.0, None, ALU.min).then_inc(logs_min, 1)
                conv_taps(tap_ends[i], tap_ends[i + 1])
                take_modulation(fills[i])
                if i + 2 < NPAIR:
                    soft_plus(i + 2)
            dve.wait_ge(conv_mean, 1)
            for b in range(CB):
                ins = v.scalar_tensor_tensor(out=CACC[:, b, :], in0=PS[:, 7, S:2 * S], scalar=-1.0 / CONV,
                                             in1=CACC[:, b, :], op0=ALU.mult, op1=ALU.add)
                if b + 1 < CB:
                    link(ins)
                else:
                    ins.then_inc(conv_centred, 1)
            dve.wait_ge(consts_ready, 1)
            link(v.scalar_tensor_tensor(out=NDIST[:, :], in0=NDIST[:, :], scalar=-1.0, in1=NDIST[:, :],
                                        op0=ALU.mult, op1=ALU.min))
            link(v.memset(NDIST[0:HD, HD:P], NEG))
            v.memset(NDIST[0:HD, P + 3 * HD:3 * P], NEG).then_inc(cols_ready, 1)
            dve.wait_ge(vectors_in, 16 * N_VECTORS)
            for n in range(2):
                link(v.tensor_tensor(LAMV[:, 2 * n, :], LAMV[:, 2 * n, :], LAMV[:, 2 * n + 1, :], ALU.mult))
                ins = v.tensor_reduce(LAM[:, n:n + 1], LAMV[:, 2 * n, :], AX.X, ALU.add)
                if n == 0:
                    link(ins)
                else:
                    ins.then_inc(lam_sum, 1)

            dve.wait_ge(conv_rstd, 1)
            link(v.tensor_tensor(CACC[:, :, :], CACC[:, :, :], RSTD.unsqueeze(1).broadcast_to([P, CB, S]), ALU.mult))
            for b in range(CB):
                ins = v.tensor_scalar(CACC[:, b, :], CACC[:, b, :], CV2[:, 12 + b:13 + b], CV2[:, 16 + b:17 + b],
                                      ALU.mult, ALU.add)
            link(ins)
            v.tensor_scalar(CSQ[:, :, :], CACC[:, :, :], SIGMOID_FLOOR, None, ALU.max).then_inc(conv_floor, 1)
            dve.wait_ge(conv_exp, 1)
            v.tensor_tensor(HT[:, 4:8, :], CACC[:, :, :], CSQ[:, :, :], ALU.mult).then_inc(conv_out, 1)
            add_mixed(0)

            def slot_positions():
                e64, off, pos = POST[:, 0], POST[:, 1], POST[:, 2]
                return [lambda: v.tensor_scalar(off, RANK[:, :, :], 0.0, FAR, ALU.is_lt, ALU.mult),
                        lambda: v.tensor_scalar(pos, RANK[:, :, :], float(SLOT), FAR, ALU.is_ge, ALU.mult),
                        lambda: v.tensor_tensor(off, off, pos, ALU.add),
                        lambda: v.tensor_scalar(e64, EXPSEL[:, :, :], float(SLOT), None, ALU.mult),
                        lambda: v.tensor_tensor(pos, RANK[:, :, :], e64, ALU.add),
                        lambda: v.tensor_tensor(POS[:, :, :], pos, off, ALU.add)]

            def moe(L):
                stage = 2 * L + 1
                normalise(stage)
                modulate(stage)
                v.memset(YS[:, :], 0.0).then_inc(y_ready, 2)
                dve.wait_ge(logits_done, L + 1)
                link(v.tensor_tensor(LG[:, :, :], PS[:, 7, 0:TB * NL].rearrange("p (t n) -> p t n", t=TB),
                                     RB[:, L, :].unsqueeze(1).broadcast_to([P, TB, NL]), ALU.add))
                link(v.tensor_copy(GL8[:, :, 0:NG], LG[:, :, 0:NG]))
                for t in range(TB):
                    link(v.max(GM8[:, t, :], GL8[:, t, :]))
                    link(v.max_index(GI8[:, t, :], GM8[:, t, :], GL8[:, t, :]))
                v.tensor_scalar(RT[:, 0, :], GM8[:, :, 0], -1.0, None, ALU.mult).then_inc(group_top, 1)
                link(v.tensor_copy(RT[:, 2, :], GI8[:, :, 0]))
                for t in range(TB):
                    link(v.tensor_scalar(EM[:, t, :], GRPNO[:, :], RT[:, 2, t:t + 1], NEG, ALU.not_equal, ALU.mult))
                    link(v.tensor_tensor(EM[:, t, :], EM[:, t, :], LG[:, t, NG:NL], ALU.add))
                    link(v.max(EM8[:, t, :], EM[:, t, :]))
                    link(v.max_index(EI8[:, t, :], EM8[:, t, :], EM[:, t, :]))
                v.tensor_tensor(RT[:, 4, :], EM8[:, :, 1], EM8[:, :, 0], ALU.subtract).then_inc(expert_top, 1)
                link(v.tensor_copy(EXPSEL[:, :, :], EI8[:, :, 0:2]))
                for s in range(2):
                    for t in range(TB):
                        link(v.tensor_scalar(ONEHOT[:, s, t, :], EXPNO[:, :], EXPSEL[:, t, s:s + 1], None, ALU.is_equal))
                v.tensor_tensor(ONEHOT[:, 2, :, :], ONEHOT[:, 0, :, :], ONEHOT[:, 1, :, :], ALU.add).then_inc(onehot_ready, 1)
                dve.wait_ge(group_exp, 2 * (L + 1))
                dve.wait_ge(expert_exp, L + 1)
                link(v.tensor_scalar(RT[:, 6, :], RT[:, 5, :], 1.0, None, ALU.add))
                link(v.tensor_tensor(RT[:, 6, :], RT[:, 6, :], RT[:, 1, :], ALU.mult))
                link(v.reciprocal(EXPW[:, :, 0], RT[:, 6, :]))
                link(v.tensor_tensor(EXPW[:, :, 1], EXPW[:, :, 0], RT[:, 5, :], ALU.mult))
                dve.wait_ge(rank_done, L + 1)
                for s in range(2):
                    link(v.tensor_tensor(ONEHOT[:, s, :, :], ONEHOT[:, s, :, :],
                                         PS[:, 7, P:P + TB * NE].rearrange("p (t n) -> p t n", t=TB), ALU.mult))
                    link(v.tensor_reduce(RANK[:, :, s], ONEHOT[:, s, :, :], AX.X, ALU.add))
                link(v.tensor_reduce(CNT[:, :], PS[:, 7, 2 * P:2 * P + NE], AX.X, ALU.max))
                v.tensor_copy(CNTI[:, :], CNT[:, :]).then_inc(count_ready, 1)
                for f in slot_positions():
                    link(f())
                v.memset(SWT[:, :, :, :], 0.0).then_inc(x_added, 1)

                def build_slots(buf, done):
                    for t in range(TB):
                        v.tensor_scalar(TMPA[:, t, :], SLOTNO[:, :], POS[:, t, 0:1], None, ALU.is_equal).then_inc(done[0], 1)
                    for t in range(TB):
                        dve.wait_ge(done[0], done[1] + t + 1)
                        v.scalar_tensor_tensor(out=SG[:, buf, t, :], in0=SLOTNO[:, :], scalar=POS[:, t, 1:2], in1=TMPA[:, t, :],
                                               op0=ALU.is_equal, op1=ALU.add).then_inc(slots_built, 1)

                def spread(count, buf):
                    dve.wait_ge(gathered, count)
                    for k in range(KD // 2):
                        v.tensor_scalar(XT[:, buf, k, :], PS[:, 2 + k // 4, (k % 4) * P:(k % 4 + 1) * P],
                                        SCALE[:, stage, k:k + 1], SHIFT[:, stage, k:k + 1],
                                        ALU.mult, ALU.add).then_inc(xt_dve, 1)

                def add_combined(done, last):
                    for u, bank in enumerate((0, 1, 5, 0)):
                        t, h = divmod(u, 2)
                        dve.wait_ge(combined, done + u + 1)
                        xs = X[:, t, h * HALF:(h + 1) * HALF]
                        v.tensor_tensor(xs, PS[:, bank, :], xs, ALU.add).then_inc(x_added, 1)

                dve.wait_ge(ada_ready, 6 * (L + 1))
                per = 7
                base = (per * EP + 2) * L
                build_slots(0, (slot_step, base))
                spread((EP + 1) * L + 1, 0)
                with dve.Fori(0, EP // UNROLL) as i:
                    for j in range(UNROLL):
                        n = i * UNROLL + (EP * L + j)
                        st = i * (UNROLL * per) + (base + 2 + per * j)
                        for t in range(TB):
                            v.tensor_scalar(TMPB[:, t, :], SLOTNO[:, :], POS[:, t, 0:1], EXPW[:, t, 0:1],
                                            ALU.is_equal, ALU.mult).then_inc(slot_step, 1)
                            v.tensor_scalar(TMPC[:, t, :], SLOTNO[:, :], POS[:, t, 1:2], EXPW[:, t, 1:2],
                                            ALU.is_equal, ALU.mult).then_inc(slot_step, 1)
                        for t in range(TB):
                            dve.wait_ge(slot_step, st + 2 * t + 2)
                            v.tensor_tensor(SW[:, t, :], TMPB[:, t, :], TMPC[:, t, :], ALU.add).then_inc(weights_built, 1)
                        dve.wait_ge(slot_step, st + 4)
                        v.tensor_scalar(POS[:, :, :], POS[:, :, :], -float(P), None, ALU.add).then_inc(slot_step, 1)
                        dve.wait_ge(slot_step, st + 5)
                        build_slots((j + 1) % 2, (slot_step, st + 5))
                        dve.wait_ge(tanh_done, n + 1)
                        v.scalar_tensor_tensor(out=T1[:, :], in0=TH[:, :], scalar=1.0, in1=PS[:, 0, :],
                                               op0=ALU.add, op1=ALU.mult).then_inc(t1_done, 1)
                        dve.wait_ge(t1_done, n + 1)
                        dve.wait_ge(up_done, n + 1)
                        v.scalar_tensor_tensor(out=HID[:, :, :].rearrange("p k q -> p q k"),
                                               in0=T1[:, :].rearrange("p (q k) -> p q k", k=KF), scalar=0.5,
                                               in1=PS[:, 1, :].rearrange("p (q k) -> p q k", k=KF),
                                               op0=ALU.mult, op1=ALU.mult).then_inc(hidden_ready, 1)
                        spread(n + (L + 2), (j + 1) % 2)
                        add_combined(i * (4 * UNROLL) + (4 * (EP + 1) * L + 4 * j), False)
                        dve.wait_ge(down_done, n + 1)
                        for h in range(2):
                            v.tensor_tensor(YS[:, h * HALF:(h + 1) * HALF], PS[:, 6 + h, :],
                                            GATE[:, 1, h * HALF:(h + 1) * HALF], ALU.mult).then_inc(y_ready, 1)
                add_combined(4 * (EP + 1) * L + 4 * EP, True)

                m = more[L]
                count = dve.value_load(CNTI[0:1, 0:1], min_val=0, max_val=S)
                per_round, per_pair = 8, 12
                with dve.If(count > SLOT):
                    v.tensor_copy(CNT[:, :], CNT[:, :]).then_inc(m["dve"], 1)
                    with dve.Fori(0, ROUNDS - 1) as r:
                        at = r * (per_round + per_pair * EP) + 1
                        dve.wait_ge(m["dve"], at)
                        v.tensor_scalar(RANK[:, :, :], RANK[:, :, :], -float(SLOT), None, ALU.add).then_inc(m["dve"], 1)
                        for n, f in enumerate(slot_positions()):
                            dve.wait_ge(m["dve"], at + n + 1)
                            f().then_inc(m["dve"], 1)
                        dve.wait_ge(m["dve"], at + 7)
                        v.tensor_copy(CNT[:, :], CNT[:, :]).then_inc(m["dve"], 1)
                        with dve.Fori(0, EP) as q:
                            step = r * EP + q
                            st = r * (per_round + per_pair * EP) + q * per_pair + (per_round + 1)
                            dve.wait_ge(m["dve"], st)
                            for t in range(TB):
                                v.tensor_scalar(TMPA[:, t, :], SLOTNO[:, :], POS[:, t, 0:1], None,
                                                ALU.is_equal).then_inc(m["dve"], 1)
                                v.tensor_scalar(TMPB[:, t, :], SLOTNO[:, :], POS[:, t, 0:1], EXPW[:, t, 0:1],
                                                ALU.is_equal, ALU.mult).then_inc(m["dve"], 1)
                                v.tensor_scalar(TMPC[:, t, :], SLOTNO[:, :], POS[:, t, 1:2], EXPW[:, t, 1:2],
                                                ALU.is_equal, ALU.mult).then_inc(m["dve"], 1)
                            dve.wait_ge(m["dve"], st + 6)
                            for t in range(TB):
                                v.tensor_tensor(SW[:, t, :], TMPB[:, t, :], TMPC[:, t, :], ALU.add).then_inc(m["slots"], 1)
                                v.scalar_tensor_tensor(out=SG[:, 0, t, :], in0=SLOTNO[:, :], scalar=POS[:, t, 1:2],
                                                       in1=TMPA[:, t, :], op0=ALU.is_equal, op1=ALU.add).then_inc(m["slots"], 1)
                            dve.wait_ge(m["slots"], step * 4 + 4)
                            v.tensor_scalar(POS[:, :, :], POS[:, :, :], -float(P), None, ALU.add).then_inc(m["dve"], 1)
                            dve.wait_ge(m["gathered"], step + 1)
                            for k in range(KD):
                                ins = v.tensor_scalar(XT[:, 0, k, :], PS[:, 2 + k // 4, (k % 4) * P:(k % 4 + 1) * P],
                                                      SCALE[:, stage, k:k + 1], SHIFT[:, stage, k:k + 1], ALU.mult, ALU.add)
                            ins.then_inc(m["dve"], 1)
                            dve.wait_ge(m["tanh"], step + 1)
                            v.scalar_tensor_tensor(out=T1[:, :], in0=TH[:, :], scalar=1.0, in1=PS[:, 0, :],
                                                   op0=ALU.add, op1=ALU.mult).then_inc(m["dve"], 1)
                            dve.wait_ge(m["dve"], st + 9)
                            dve.wait_ge(m["up"], step + 1)
                            v.scalar_tensor_tensor(out=HID[:, :, :].rearrange("p k q -> p q k"),
                                                   in0=T1[:, :].rearrange("p (q k) -> p q k", k=KF), scalar=0.5,
                                                   in1=PS[:, 1, :].rearrange("p (q k) -> p q k", k=KF),
                                                   op0=ALU.mult, op1=ALU.mult).then_inc(m["dve"], 1)
                            dve.wait_ge(m["down"], step + 1)
                            for h in range(2):
                                v.tensor_tensor(YS[:, h * HALF:(h + 1) * HALF], PS[:, 6 + h, :],
                                                GATE[:, 1, h * HALF:(h + 1) * HALF], ALU.mult).then_inc(m["dve"], 1)
                            for u in range(4):
                                t, h = divmod(u, 2)
                                dve.wait_ge(m["combined"], step * 4 + (u + 1))
                                xs = X[:, t, h * HALF:(h + 1) * HALF]
                                v.tensor_tensor(xs, PS[:, u, :], xs, ALU.add).then_inc(m["added"], 1)
                    dve.wait_ge(m["added"], 4 * EP * (ROUNDS - 1))

            moe(0)

            v.tensor_copy(CREP1[:, :, :], CCOL[:, 1, :].unsqueeze(2).broadcast_to([P, KD, 32])).then_inc(cond_in_place, 1)
            normalise(2)
            take_modulation(6)
            take_modulation(7)
            modulate(2)
            dve.wait_ge(lam_exp, 1)
            link(v.tensor_tensor(LAM[:, 4:5], LAM[:, 3:4], LAM[:, 2:3], ALU.subtract))
            link(v.tensor_scalar(LAM[:, 5:6], LAM[:, 4:5], -LAM0, None, ALU.add))
            for u in range(16):
                dve.wait_ge(qk_rstd, u + 1)
                dst, gain = (QTo, CV2[:, 24:25]) if u < 8 else (KTo, CV2[:, 22:23])
                v.scalar_tensor_tensor(out=dst[:, u % 8, :], in0=PS[:, u % 4, 0:S], scalar=gain, in1=RSo[u % 2][:, :],
                                       op0=ALU.mult, op1=ALU.mult).then_inc(qk_out, 1)

            def biased(h):
                dve.wait_ge(scores_done, h + 1)
                dve.wait_ge(head_bias, h + 1)
                if h >= 2:
                    dve.wait_ge(diff_ready, 2 * (h - 1))
                for cc in range(2):
                    for t in range(TB):
                        at = slice(t * P, (1 + 2 * t) * P)
                        k = 2 * cc + t
                        ins = v.tensor_tensor_reduce(SCo[:, h % 2, cc, at], PS[:, cc, at], BIAS[:, h % 2, at],
                                                     1.0, LOWEST, ALU.add, ALU.max, STo[:, h % 2, k:k + 1])
                link(ins)
                v.tensor_scalar(STo[:, h % 2, 4:8], STo[:, h % 2, 0:4], -1.0, None, ALU.mult).then_inc(scores_max, 1)

            def head_out(h):
                dve.wait_ge(o_rstd, h + 1)
                v.scalar_tensor_tensor(out=HT[:, h, :], in0=PS[:, 3, 0:S], scalar=CV2[:, 23:24], in1=RSo[0][:, :],
                                       op0=ALU.mult, op1=ALU.mult).then_inc(o_out, 1)

            biased(0)
            biased(1)
            for h in range(NH):
                dve.wait_ge(scores_exp, 4 * (h + 1))
                st = STo[:, h % 2, :]
                link(v.reciprocal(st[:, 12:16], st[:, 8:12]))
                v.tensor_scalar(st[:, 16:18], st[:, 14:16], LAM[:, 5:6], None, ALU.mult)
                if h >= 1:
                    dve.wait_ge(diff_turned, h)
                for t in range(TB):
                    at = slice(t * P, (1 + 2 * t) * P)
                    ins = v.tensor_scalar(SCo[:, h % 2, 0, at], SCo[:, h % 2, 0, at], st[:, 12 + t:13 + t], None, ALU.mult)
                link(ins)
                for t in range(TB):
                    at = slice(t * P, (1 + 2 * t) * P)
                    v.scalar_tensor_tensor(out=PRo[:, at], in0=SCo[:, h % 2, 1, at], scalar=st[:, 16 + t:17 + t],
                                           in1=SCo[:, h % 2, 0, at], op0=ALU.mult, op1=ALU.add).then_inc(diff_ready, 1)
                if h + 2 < NH:
                    biased(h + 2)
                if h in fills1:
                    take_modulation(fills1[h])
                if h:
                    head_out(h - 1)
            head_out(NH - 1)
            add_mixed(1)
            moe(1)

        @block.tensor
        def _(pe):
            def mm(out_, lhsT, rhs, first, last, **kw):
                return pe.matmul(out_, lhsT, rhs, start=first, stop=last, **kw)

            def slab_ready(n):
                pe.wait_ge(slab_in[n % RING], landed(n))

            def modulation(n):
                s = slab_index("ada", n)
                slab_ready(s)
                if n in (0, 6):
                    pe.wait_ge(cond_in_place, 1 + n // 6)
                if n == 0:
                    pass
                else:
                    pe.wait_ge(ada_copied, n)
                    pe.wait_ge(ada_ready, n)
                if n == 2:
                    pe.wait_ge(cols_ready, 2)
                w = wide(s)
                for h in range(2):
                    for k in range(KD):
                        g = k % 4
                        ins = mm(PS[32 * g:32 * g + 32, 4 + h, :], (CREP if n < 6 else CREP1)[:, k, :], w[:, k, h * HALF:(h + 1) * HALF],
                                 k < 4, k >= 4, skip_group_check=True)
                ins.then_inc(ada_summed, 1)
                pe.wait_ge(ada_copied, n + 1)
                if n % 3 == 2:
                    mm(PS[:, 6, :], SEL[:, :], PART[:, 0:HALF], True, True)
                    mm(PS[:, 4, :], SEL[:, :], PART[:, HALF:D], True, True).then_inc(ada_joined, 1)
                else:
                    cols = PART[:, :].rearrange("p (q k) -> p k q", k=KD)
                    for k in range(KD):
                        ins = mm(PS[:, 6, k:k + 1], cols[:, k, :], SEL[:, 0:1], True, True)
                    ins.then_inc(ada_joined, 1)

            def small_columns():
                pe.wait_ge(rows_in, 16 * N_ROWS)
                pe.transpose(PS[:, 6, 0:TAPS * CB], CROW[0:TAPS * CB, 0, :], IDENT[0:TAPS * CB, 0:TAPS * CB]).then_inc(rows_turned, 1)
                pe.transpose(PS[:, 6, P:P + 23], CROW[0:23, 1, :], IDENT[0:23, 0:23]).then_inc(rows_turned, 1)

            def turn_xn(stage):
                pe.wait_ge(xn_ready, 2 * (stage + 1))
                for b in range(4):
                    for k in (2 * b, 2 * b + 1):
                        for t in range(TB):
                            ins = pe.transpose(PS[:, b, (k % 2) * S + t * P:(k % 2) * S + (t + 1) * P],
                                               XN[:, t, k, :], IDENT[:, :])
                    ins.then_inc(xn_turned, 1)

            def h_in_place(stage):
                pe.wait_ge(h_dve, 4 * (stage + 1))
                pe.wait_ge(h_act, 4 * (stage + 1))

            def project_T(bank, w, cols):
                for k in range(KD):
                    ins = mm(PS[:, bank, 0:S], w[:, k, cols:cols + P], HT[:, k, :], k == 0, k == KD - 1)
                return ins

            def project(bank, w, cols, t):
                for k in range(KD):
                    ins = mm(PS[:, bank, :], HT[:, k, t * P:(t + 1) * P], w[:, k, cols:cols + HALF], k == 0, k == KD - 1)
                return ins

            def mix_out(L, slab):
                slab_ready(slab)
                w = wide(slab)
                for u in range(4):
                    t, h = divmod(u, 2)
                    project(u, w, h * HALF, t).then_inc(wout_done, 1)

            pe.wait_ge(consts_ready, 1)
            modulation(0)
            turn_xn(0)
            modulation(1)

            h_in_place(0)
            for u in range(18):
                s = slab_index("even_in", 1 if u < 6 else 2 if u < 10 else 0)
                if u in (0, 6, 10):
                    slab_ready(s)
                if u == 0:
                    small_columns()
                if u >= 4:
                    w = u - 4
                    if w < 2 or w >= 10:
                        pe.wait_ge(qkv_out, w + 1 if w < 2 else w - 7)
                    else:
                        pe.wait_ge(glu_out, w - 1)
                if u < 2:
                    ins = project(u % 4, wide(s), 0, u)
                elif u < 6:
                    ins = project_T(u % 4, wide(s), HALF + (u - 2) * P)
                elif u < 10:
                    ins = project_T(u % 4, wide(s, HALF), (u - 6) * P)
                else:
                    ins = project_T(u % 4, wide(s), (u - 10) * P)
                ins.then_inc(proj_done, 1)

            def logits(i):
                if i == 0:
                    pe.wait_ge(qkv_out, 10)
                if i >= 2:
                    pe.wait_ge(logs_min, i - 1)
                for h in range(2):
                    r = slice(h * HD, (h + 1) * HD)
                    b = 2 * (i % 2) + h
                    mm(PS[:, b, 0:S], KTe[r, i, 0:P], QTe[r, i, :], True, True)
                    ins = mm(PS[:, b, S:S + P], KTe[r, i, P:S], QTe[r, i, P:S], False, True, skip_group_check=True)
                ins.then_inc(z_ready, 1)

            def tails(i):
                pe.wait_ge(fails_masked, 4 * (i + 1))
                for h in range(2):
                    b = 2 * (i % 2) + h
                    s = SPe[:, i % 2, h, :]
                    mm(PS[:, b, 0:3 * P], NEGTRI[:, :], s, False, True, skip_group_check=True)
                    ins = mm(PS[:, b, P:S], NEGONE[:, :], s[:, S:S + P], False, True, skip_group_check=True)
                ins.then_inc(logs_ready, 1)

            def values(i):
                pe.wait_ge(probs_masked, 4 * (i + 1))
                if i:
                    pe.wait_ge(heads_out, i)
                for h in range(2):
                    cols = slice(i * P + h * HD, i * P + (h + 1) * HD)
                    pr = PRe[:, i % 2, h, :]
                    o = PS[h * HD:(h + 1) * HD, 7, :]
                    mm(o[:, 0:S], Ve[:, 0, cols], pr[:, 0:S], True, True, skip_group_check=True)
                    ins = mm(o[:, P:S], Ve[:, 1, cols], pr[:, S:S + P], False, True, skip_group_check=True)
                ins.then_inc(pv_done, 1)

            logits(0)
            logits(1)
            for i in range(NPAIR):
                tails(i)
                if i:
                    values(i - 1)
                modulation(fills[i])
                if i + 2 < NPAIR:
                    logits(i + 2)
            values(NPAIR - 1)
            pe.wait_ge(conv_done, TAPS * CB)
            pe.wait_ge(heads_out, NPAIR)
            for b in range(CB):
                ins = mm(PS[:, 7, S:2 * S], ONES[:, :], CACC[:, b, :], b == 0, b == CB - 1, skip_group_check=True)
            ins.then_inc(conv_mean, 1)
            pe.wait_ge(conv_squared, 1)
            for b in range(CB):
                ins = mm(PS[:, 7, S:2 * S], ONES[:, :], CSQ[:, b, :], b == 0, b == CB - 1, skip_group_check=True)
            ins.then_inc(conv_var, 1)
            pe.wait_ge(conv_out, 1)
            mix_out(0, slab_index("even_out", 0))

            def moe(L):
                stage = 2 * L + 1
                turn_xn(stage)
                h_in_place(stage)
                pe.wait_ge(vectors_in, 16 * N_VECTORS)
                for t in range(TB):
                    for k in range(KD):
                        for e in range(2):
                            at = t * P + e * SLOT
                            ins = mm(PS[e * SLOT:(e + 1) * SLOT, 7, t * NL:(t + 1) * NL], HT[:, k, at:at + SLOT],
                                     WR[:, L, k, :], k == 0, k == KD - 1, skip_group_check=True)
                ins.then_inc(logits_done, 1)
                pe.wait_ge(onehot_ready, L + 1)
                chosen = ONEHOT[:, 2, :, :]
                mm(PS[:, 7, P:P + NE], BEFORE[:, :], chosen[:, 0, :], True, True, skip_group_check=True)
                mm(PS[:, 7, P + NE:P + 2 * NE], BEFORE[:, :], chosen[:, 1, :], True, False, skip_group_check=True)
                mm(PS[:, 7, P + NE:P + 2 * NE], ONES[:, :], chosen[:, 0, :], False, True, skip_group_check=True)
                mm(PS[:, 7, 2 * P:2 * P + NE], ONES[:, :], chosen[:, 0, :], True, False, skip_group_check=True)
                mm(PS[:, 7, 2 * P:2 * P + NE], ONES[:, :], chosen[:, 1, :], False, True,
                   skip_group_check=True).then_inc(rank_done, 1)

                def gather(buf, done):
                    for k in range(KD):
                        for t in range(TB):
                            for s in range(3):
                                ins = mm(PS[:, 2 + k // 4, (k % 4) * P:(k % 4 + 1) * P], XN3[:, s, t, k, :], SG[:, buf, t, :],
                                         t == 0 and s == 0, t == TB - 1 and s == 2)
                    ins.then_inc(done, 1)

                def widen(bank, w, xt, done):
                    for k in range(KD):
                        for e in range(2):
                            ins = mm(PS[e * SLOT:(e + 1) * SLOT, bank, :], xt[:, k, e * SLOT:(e + 1) * SLOT],
                                     w[:, e, k * F:(k + 1) * F], k == 0, k == KD - 1, skip_group_check=True)
                    ins.then_inc(done, 1)

                def narrow(w, done):
                    for h in range(2):
                        for k in range(KF):
                            for e in range(2):
                                ins = mm(PS[e * SLOT:(e + 1) * SLOT, 6 + h, :], HIDT[:, k, e * SLOT:(e + 1) * SLOT],
                                         w[:, e, k * D + h * HALF:k * D + (h + 1) * HALF], k == 0, k == KF - 1,
                                         skip_group_check=True)
                    ins.then_inc(done, 1)

                def turn_weights():
                    for t in range(TB):
                        ins = pe.transpose(PS[:, 5, t * P:(t + 1) * P], SW[:, t, :], IDENT[:, :])
                    return ins

                def turn_hidden():
                    for k in range(KF):
                        ins = pe.transpose(PS[:, 4, k * P:(k + 1) * P], HID[:, k, :], IDENT[:, :])
                    return ins

                def combine(buf, done):
                    for u, bank in enumerate((0, 1, 5, 0)):
                        t, h = divmod(u, 2)
                        if u == 3:
                            pe.wait_ge(x_added, done + 1)
                        mm(PS[:, bank, :], SWT[:, buf, t, :], YS[:, h * HALF:(h + 1) * HALF], True, True).then_inc(combined, 1)

                pe.wait_ge(split_act, 3 * (L + 1))
                pe.wait_ge(slots_built, 2 * ((EP + 1) * L + 1))
                gather(0, gathered)
                with pe.Fori(0, EP // UNROLL) as i:
                    for j in range(UNROLL):
                        n = i * UNROLL + (EP * L + j)
                        adds = i * (4 * UNROLL) + (ADDS * L + 1 + 4 * j)
                        slabs = [MOE0[L] + 3 * j + w for w in range(3)]
                        land = [i * (16 * GROUP) + landed(s) for s in slabs]
                        pe.wait_ge(xt_dve, i * (4 * UNROLL) + 4 * ((EP + 1) * L + j + 1))
                        pe.wait_ge(xt_act, i * (4 * UNROLL) + 4 * ((EP + 1) * L + j + 1))
                        pe.wait_ge(x_added, adds)
                        pe.wait_ge(slab_in[slabs[0] % RING], land[0])
                        widen(0, pair_slab(slabs[0]), XT[:, j % 2], gate_done)
                        pe.wait_ge(slab_in[slabs[1] % RING], land[1])
                        widen(1, pair_slab(slabs[1]), XT[:, j % 2], up_done)
                        pe.wait_ge(slots_built, i * (2 * UNROLL) + 2 * ((EP + 1) * L + j + 2))
                        gather((j + 1) % 2, gathered)
                        pe.wait_ge(weights_built, n * 2 + 2)
                        turn_weights().then_inc(weights_turned, 1)
                        pe.wait_ge(hidden_ready, n + 1)
                        turn_hidden().then_inc(hidden_turned, 1)
                        pe.wait_ge(y_ready, i * (2 * UNROLL) + 2 * ((EP + 1) * L + j + 1))
                        pe.wait_ge(weightsT_ready, n + 1)
                        combine((j + 1) % 2, adds)
                        pe.wait_ge(hiddenT_ready, n + 1)
                        pe.wait_ge(slab_in[slabs[2] % RING], land[2])
                        narrow(pair_slab(slabs[2]), down_done)
                pe.wait_ge(y_ready, 2 * (EP + 1) * (L + 1))
                pe.wait_ge(x_added, ADDS * (L + 1) - 4)
                combine((UNROLL + 1) % 2, ADDS * (L + 1) - 4)

                m = more[L]
                pe.wait_ge(count_ready, L + 1)
                count = pe.value_load(CNTI[0:1, 0:1], min_val=0, max_val=S)
                with pe.If(count > SLOT):
                    pe.wait_ge(x_added, ADDS * (L + 1))
                    with pe.Fori(0, ROUNDS - 1) as r:
                        with pe.Fori(0, EP) as q:
                            step = r * EP + q
                            st = r * (8 + 12 * EP) + q * 12 + 9
                            pe.wait_ge(m["slots"], step * 4 + 4)
                            gather(0, m["gathered"])
                            pe.wait_ge(m["slabs"], step * 48 + 48)
                            pe.wait_ge(m["dve"], st + 8)
                            widen(0, pair_slab(0), XT[:, 0], m["gate"])
                            widen(1, pair_slab(1), XT[:, 0], m["up"])
                            turn_weights()
                            pe.wait_ge(m["dve"], st + 10)
                            turn_hidden().then_inc(m["turned"], 1)
                            pe.wait_ge(m["copied"], step * 2 + 2)
                            narrow(pair_slab(2), m["down"])
                            pe.wait_ge(m["dve"], st + 12)
                            for u in range(4):
                                t, h = divmod(u, 2)
                                mm(PS[:, u, :], SWT[:, 0, t, :], YS[:, h * HALF:(h + 1) * HALF],
                                   True, True).then_inc(m["combined"], 1)
                    pe.wait_ge(m["added"], 4 * EP * (ROUNDS - 1))

            moe(0)

            modulation(6)
            modulation(7)
            turn_xn(2)
            h_in_place(2)

            def head_sums(u):
                pe.wait_ge(qk_squared, u + 1)
                if u >= 2:
                    pe.wait_ge(qk_rstd, u - 1)
                mm(PS[:, 4 + u % 2, 0:S], HEADSUM[:, :], SQo[u % 2][:, :], True, True).then_inc(qk_mean, 1)

            for u in range(20):
                s = slab_index("odd_in", 0 if u < 8 else 1 if u < 16 else 2)
                if u in (0, 8, 16):
                    slab_ready(s)
                if u >= 4:
                    pe.wait_ge(qk_out, u - 3)
                if u < 16:
                    ins = project_T(u % 4, wide(s), (u % 8) * P)
                else:
                    ins = project(u % 4, wide(s), ((u - 16) % 2) * HALF, (u - 16) // 2)
                ins.then_inc(proj_done, 1)
                if 1 <= u <= 16:
                    head_sums(u - 1)

            def scores(h):
                if h == 0:
                    pe.wait_ge(qk_out, 16)
                    pe.wait_ge(v_out, 4)
                if h:
                    pe.wait_ge(scores_max, h)
                for t in range(TB):
                    for cc in range(2):
                        r = slice(cc * HD, (cc + 1) * HD)
                        ins = mm(PS[:, cc, t * P:(1 + 2 * t) * P], QTo[r, h, t * P:(t + 1) * P],
                                 KTo[r, h, 0:(t + 1) * P], True, True, skip_group_check=True)
                ins.then_inc(scores_done, 1)

            def head_mean(h):
                pe.wait_ge(o_squared, h + 1)
                mm(PS[:, 7, 0:S], ONES[:, :], SQo[0][:, :], True, True, skip_group_check=True).then_inc(o_mean, 1)

            scores(0)
            scores(1)
            for h in range(NH):
                pe.wait_ge(diff_ready, 2 * (h + 1))
                if h:
                    pe.wait_ge(diffT_ready, h)
                for n in range(3):
                    ins = pe.transpose(PS[:, 2, n * P:(n + 1) * P], PRo[:, n * P:(n + 1) * P], IDENT[:, :])
                ins.then_inc(diff_turned, 1)
                if h:
                    head_mean(h - 1)
                if h + 2 < NH:
                    scores(h + 2)
                if h in fills1:
                    modulation(fills1[h])
                pe.wait_ge(diffT_ready, h + 1)
                if h:
                    pe.wait_ge(o_out, h)
                mm(PS[:, 3, 0:S], Vo[:, 0, h * P:(h + 1) * P], PTo[:, 0:S], True, True, skip_group_check=True)
                mm(PS[:, 3, P:S], Vo[:, 1, h * P:(h + 1) * P], PTo[:, S:S + P], False, True,
                   skip_group_check=True).then_inc(o_done, 1)
            head_mean(NH - 1)
            pe.wait_ge(o_out, NH)
            mix_out(1, slab_index("odd_out", 0))
            moe(1)


N_ROWS = 6 + 4
N_VECTORS = 2 + 8 + 4


_INS = ["x", "c", "w_ada", "b_ada", "mix_norm_g", "ffn_norm_g", "even_w_in", "conv_b_glu", "conv_dw", "conv_dw_b",
        "conv_ln_g", "conv_ln_b", "even_w_out", "odd_w_in", "qk_norm_q", "qk_norm_k", "lambda_q1", "lambda_k1",
        "lambda_q2", "lambda_k2", "diff_sub_g", "odd_w_out", "moe_w_group", "moe_b_group", "moe_w_router",
        "moe_b_router", "moe_w_gate", "moe_w_up", "moe_w_down"]


def kernel(**inputs):
    import numpy as np
    import concourse.bacc as bacc
    from concourse.bass_utils import run_bass_kernel_spmd

    nc = bacc.Bacc("TRN2", target_bir_lowering=False, num_devices=1)
    arrays, args = {}, []
    for name in _INS:
        a = np.ascontiguousarray(inputs[name])
        arrays[f"in_{name}"] = a
        args.append(nc.dram_tensor(f"in_{name}", a.shape, mybir.dt.from_np(a.dtype), kind="ExternalInput").ap())
    result = nc.dram_tensor("out", inputs["x"].shape, F32, kind="ExternalOutput").ap()
    build_trunk(nc, *args, result)
    r = run_bass_kernel_spmd(nc, [arrays], core_ids=[0])
    return r.results[0]["out"]
```

```python
import math
from contextlib import ExitStack

import concourse.bass as bass
from concourse import mybir

P = 128
F32 = mybir.dt.float32
BF16 = mybir.dt.bfloat16
I32 = mybir.dt.int32
U32 = mybir.dt.uint32
ALU = mybir.AluOpType
ACT = mybir.ActivationFunctionType
AX = mybir.AxisListType

EPS = 1e-6
FAR = 1.0e6
NEG = -1.0e30
LOWEST = -3.0e38
SIGMOID_FLOOR = -43.0


def build_trunk(nc, x, c, w_ada, b_ada, mix_norm_g, ffn_norm_g, even_w_in, conv_b_glu, conv_dw, conv_dw_b,
                conv_ln_g, conv_ln_b, even_w_out, odd_w_in, qk_norm_q, qk_norm_k, lambda_q1, lambda_k1,
                lambda_q2, lambda_k2, diff_sub_g, odd_w_out, moe_w_group, moe_b_group, moe_w_router,
                moe_b_router, moe_w_gate, moe_w_up, moe_w_down, out):
    _, S, D = x.shape
    TB = S // P
    KD = D // P
    TAPS, CONV = conv_dw.shape[1:]
    CB = CONV // P
    PAD = TAPS - 1
    HD = 64
    NPAIR = (even_w_in.shape[2] - 2 * CONV) // 3 // P
    NH = D // P
    NG = moe_w_group.shape[2]
    NE, _, F = moe_w_gate.shape[1:]
    EPG = NE // NG
    KF = F // P
    SLOT = 64
    EP = NE // 2
    ROUNDS = S // SLOT
    LAM0 = 0.8 - 0.6 * math.exp(-0.3)
    QSCALE = HD ** -0.5
    NL = NG + NE
    HALF = 512
    RING = 4
    ADA_FIRST = 6
    UNROLL = 4

    ctx = ExitStack()
    with ctx:
        def sb(name, shape, dt=F32):
            return ctx.enter_context(nc.sbuf_tensor(name, shape, dt))

        def sem(name):
            return ctx.enter_context(nc.semaphore(name))

        RINGT = sb("weight_ring", [P, RING, 8 * 1024])
        X = sb("x_tokens", [P, TB, D])
        HT = sb("h_or_mix_T", [P, KD, S])
        GATE = sb("gate_rows", [P, 2, D])
        PART = sb("ada_partials", [P, 1024])
        SHIFT = sb("shift", [P, 4, KD])
        SCALE = sb("scale", [P, 4, KD])
        GAIN = sb("norm_gain", [P, 4, KD])
        BADA = sb("ada_bias", [P, 12, KD])
        CCOL = sb("cond_cols", [P, 3, KD])
        IDENT = sb("ident", [P, P])
        NEGS = sb("neg_tri_and_one", [P, 2, P])
        NEGTRI, NEGONE = NEGS[:, 0, :], NEGS[:, 1, :]
        ONES = sb("ones", [P, P])
        BEFORE = sb("before", [P, P])
        HEADSUM = sb("head_sum", [P, P])
        SEL = sb("select_partials", [P, P])
        SLOTNO = sb("slot_number", [P, P])
        EXPNO = sb("expert_number", [P, NE])
        GRPNO = sb("group_of_expert", [P, NE])
        NDIST = sb("neg_distance", [P, 3 * P])
        EPSC = sb("eps", [P, 1])
        CV1 = sb("conv_taps", [P, TAPS * CB])
        CV2 = sb("small_cols", [P, 32])
        WR = sb("router_w", [P, 2, KD, NL])
        RB = sb("router_b", [P, 2, NL])
        LAMV = sb("lambda_rows", [P, 4, HD])
        LAM = sb("lambda", [P, 8])
        STAT = sb("norm_stat", [P, 4])
        LG = sb("router_logits", [P, TB, NE])
        GL8 = sb("group_logits", [P, TB, 8])
        GM8 = sb("group_top", [P, TB, 8])
        GI8 = sb("group_index", [P, TB, 8], U32)
        EM = sb("expert_logits", [P, TB, NE])
        EM8 = sb("expert_top", [P, TB, 8])
        EI8 = sb("expert_index", [P, TB, 8], U32)
        RT = sb("route_scratch", [P, 12, TB])
        EXPSEL = sb("chosen_experts", [P, TB, 2])
        EXPW = sb("chosen_weights", [P, TB, 2])
        ONEHOT = sb("expert_onehot", [P, 3, TB, NE])
        RANK = sb("rank_in_expert", [P, TB, 2])
        POS = sb("slot_of_token", [P, TB, 2])
        POST = sb("slot_scratch", [P, 3, TB, 2])
        CNT = sb("largest_count", [P, 1])
        CNTI = sb("largest_count_int", [P, 1], I32)

        U = sb("phase_region", [P, 9984])

        def part_of(at, *shape, dt=F32):
            n = math.prod(shape)
            words = n if dt == F32 else n // 2
            v = U[:, at:at + words]
            if dt != F32:
                v = v.bitcast(dt)
            if len(shape) == 1:
                return v
            names = "abcd"[:len(shape)]
            return v.rearrange(f"p ({' '.join(names)}) -> p {' '.join(names)}", **dict(zip(names, shape)))

        XN = part_of(0, TB, KD, P)
        QTe = part_of(0, NPAIR, S)
        KTe = part_of(1024, NPAIR, S)
        Ve = part_of(2048, TB, NPAIR * P)
        CIN = part_of(3072, CB, S + PAD)
        CSQ = part_of(3072, CB, S)
        CACC = part_of(4288, CB, S)
        SPe = part_of(5312, 2, 2, 3 * P)
        PRe = part_of(6848, 2, 2, 3 * P)
        RSTD = part_of(8384, S)
        CROW = part_of(6848, 2, P)
        CREP = part_of(8640, KD, 32)
        CREP1 = NEGS[:, :, :].rearrange("p a (k n) -> p (a k) n", n=32)
        QTo = part_of(0, NH, S)
        KTo = part_of(2048, NH, S)
        Vo = part_of(4096, TB, D)
        SCo = part_of(6144, 2, 2, 3 * P)
        PRo = part_of(7680, 3 * P)
        PTo = part_of(8064, 3 * P)
        SQo = [part_of(8448, S), part_of(8960, S)]
        RSo = [part_of(8704, S), part_of(9216, S)]
        BIAS = part_of(9216, 2, 3 * P)
        STo = ONEHOT[:, 0, :, :]
        XT = part_of(0, 2, KD, P)
        XN3 = part_of(2048, 3, TB, KD, P, dt=BF16)
        TH = part_of(5120, F)
        T1 = part_of(5632, F)
        HID = part_of(6144, KF, P)
        HIDT = part_of(6656, KF, P)
        YS = part_of(7168, D)
        SG = part_of(8192, 2, TB, P, dt=BF16)
        SW = part_of(8448, TB, P)
        SWT = part_of(8704, 2, TB, P)
        TMPA = part_of(9216, TB, P)
        TMPB = part_of(9472, TB, P)
        TMPC = part_of(9728, TB, P)

        PS = ctx.enter_context(nc.psum_tensor("psum", [P, 8, 512], F32))

        slab_in = [sem(f"slab_in_{i}") for i in range(RING)]
        rest_in = [sem(f"rest_in_{i}") for i in range(RING)]
        cond_in = sem("cond_in")
        x_in = sem("x_in")
        norm_in = sem("norm_in")
        rows_in = sem("rows_in")
        vectors_in = sem("vectors_in")
        gate_bias_in = sem("gate_bias_in")
        pool_step = sem("pool_step")
        consts_ready = sem("consts_ready")
        dve_step = sem("dve_step")
        act_step = sem("act_step")
        cond_exp = sem("cond_exp")
        cond_in_place = sem("cond_in_place")
        cond_negated = sem("cond_negated")
        ada_summed = sem("ada_summed")
        ada_copied = sem("ada_copied")
        ada_joined = sem("ada_joined")
        ada_ready = sem("ada_ready")
        rows_turned = sem("rows_turned")
        cols_ready = sem("cols_ready")
        norm_stat = sem("norm_stat")
        xn_ready = sem("xn_ready")
        xn_turned = sem("xn_turned")
        h_dve = sem("h_dve")
        h_act = sem("h_act")
        proj_done = sem("proj_done")
        qkv_out = sem("qkv_out")
        glu_out = sem("glu_out")
        glu_exp = sem("glu_exp")
        z_ready = sem("z_ready")
        softlog = sem("softlog")
        fail_sum_in = sem("fail_sum_in")
        fails_masked = sem("fails_masked")
        logs_ready = sem("logs_ready")
        logs_min = sem("logs_min")
        probs_exp = sem("probs_exp")
        probs_masked = sem("probs_masked")
        pv_done = sem("pv_done")
        heads_out = sem("heads_out")
        conv_done = sem("conv_done")
        conv_mean = sem("conv_mean")
        conv_centred = sem("conv_centred")
        conv_squared = sem("conv_squared")
        conv_var = sem("conv_var")
        conv_rstd = sem("conv_rstd")
        conv_floor = sem("conv_floor")
        conv_exp = sem("conv_exp")
        conv_out = sem("conv_out")
        wout_done = sem("wout_done")
        x_mixed = sem("x_mixed")
        qk_squared = sem("qk_squared")
        qk_mean = sem("qk_mean")
        qk_rstd = sem("qk_rstd")
        qk_out = sem("qk_out")
        v_out = sem("v_out")
        lam_sum = sem("lam_sum")
        lam_exp = sem("lam_exp")
        head_bias = sem("head_bias")
        scores_done = sem("scores_done")
        scores_max = sem("scores_max")
        scores_exp = sem("scores_exp")
        diff_ready = sem("diff_ready")
        diff_turned = sem("diff_turned")
        diffT_ready = sem("diffT_ready")
        o_done = sem("o_done")
        o_squared = sem("o_squared")
        o_mean = sem("o_mean")
        o_rstd = sem("o_rstd")
        o_out = sem("o_out")
        logits_done = sem("logits_done")
        group_top = sem("group_top")
        group_exp = sem("group_exp")
        expert_top = sem("expert_top")
        expert_exp = sem("expert_exp")
        onehot_ready = sem("onehot_ready")
        rank_done = sem("rank_done")
        count_ready = sem("count_ready")
        split_act = sem("split_act")
        split_pool = sem("split_pool")
        slots_built = sem("slots_built")
        weights_built = sem("weights_built")
        gathered = sem("gathered")
        xt_dve = sem("xt_dve")
        xt_act = sem("xt_act")
        half_used = [sem(f"{w}_half_used") for w in ("gate", "up", "down")]
        gate_done = sem("gate_done")
        up_done = sem("up_done")
        tanh_done = sem("tanh_done")
        t1_done = sem("t1_done")
        hidden_ready = sem("hidden_ready")
        hidden_turned = sem("hidden_turned")
        hiddenT_ready = sem("hiddenT_ready")
        weights_turned = sem("weights_turned")
        weightsT_ready = sem("weightsT_ready")
        down_done = sem("down_done")
        y_ready = sem("y_ready")
        combined = sem("combined")
        x_added = sem("x_added")
        slot_step = sem("slot_step")
        more = [{n: sem(f"more{L}_{n}") for n in ("slabs", "slots", "dve", "gathered", "gate", "tanh", "up", "turned",
                                                   "copied", "down", "combined", "added")} for L in range(2)]
        out_stored = sem("out_stored")

        fills = {0: 3, 1: 4}
        fills1 = {0: 8, 1: 9, 2: 10}
        head_slabs = ([("ada", a, ada_summed, a + 1) for a in range(2)]
                      + [("even_in", 1, proj_done, 10), ("even_in", 2, proj_done, 8), ("even_in", 0, proj_done, 18)]
                      + [("ada", a, ada_summed, a + 1) for a in range(2, 5)]
                      + [("even_out", 0, wout_done, 4), ("ada", 5, ada_summed, 6)])
        mid_slabs = ([("ada", a, ada_summed, a + 1) for a in range(6, 8)]
                     + [("odd_in", 0, proj_done, 26), ("odd_in", 1, proj_done, 34), ("odd_in", 2, proj_done, 38)]
                     + [("ada", a, ada_summed, a + 1) for a in range(8, 11)]
                     + [("odd_out", 0, wout_done, 8), ("ada", 11, ada_summed, 12)])
        MOE0 = [len(head_slabs), len(head_slabs) + 3 * EP + len(mid_slabs)]
        MID0 = MOE0[0] + 3 * EP
        assert (3 * UNROLL) % RING == 0 and EP % UNROLL == 0 and UNROLL == RING
        GROUP = 3 * UNROLL // RING
        ADDS = 4 * (EP + 1) + 1

        def place(n):
            return RINGT[:, n % RING, :]

        def landed(n):
            return 16 * (n // RING + 1)

        split_order = [(0, 0), (0, 1), (1, 0), (0, 2), (1, 1), (1, 2)]

        def copies_before(L, t, part):
            return 6 * L + split_order.index((t, part))

        def slab_index(kind, arg):
            for n, s in enumerate(head_slabs):
                if s[:2] == (kind, arg):
                    return n
            for n, s in enumerate(mid_slabs):
                if s[:2] == (kind, arg):
                    return MID0 + n

        def turned_banks(stage, t):
            return (0, 1) if (t == 0) == (stage == 0) else (2, 3)

        mixed_banks = (4, 5, 0, 1)

        ada_src = w_ada.rearrange("l (p k) n -> l p k n", k=KD)
        even_in_src = even_w_in[0].rearrange("(p k) n -> p k n", k=KD)
        odd_in_src = odd_w_in[0].rearrange("(p k) n -> p k n", k=KD)
        out_srcs = {"even_out": even_w_out[0].rearrange("(k p) n -> p k n", p=P),
                    "odd_out": odd_w_out[0].rearrange("(k p) n -> p k n", p=P)}
        gate_src = moe_w_gate.rearrange("l e (p k) f -> l p e (k f)", k=KD)
        up_src = moe_w_up.rearrange("l e (p k) f -> l p e (k f)", k=KD)
        down_src = moe_w_down.rearrange("l e (p k) n -> l p e (k n)", k=KF)

        def wide(n, cols=1024):
            return place(n)[:, 0:KD * cols].rearrange("p (k n) -> p k n", k=KD)

        def pair_slab(n):
            return place(n).rearrange("p (e n) -> p e n", e=2)

        block = ctx.enter_context(nc.Block())

        def overflow_loads(sp, L):
            m = more[L]
            sp.wait_ge(count_ready, L + 1)
            count = sp.value_load(CNTI[0:1, 0:1], min_val=0, max_val=S)
            with sp.If(count > SLOT):
                with sp.Fori(0, ROUNDS - 1) as r:
                    with sp.Fori(0, EP) as q:
                        step = r * EP + q
                        sp.wait_ge(down_done, 2 * EP * (L + 1))
                        sp.wait_ge(m["slots"], step * 4 + 4)
                        for w, src in enumerate((gate_src, up_src, down_src)):
                            sp.dma_start(pair_slab(w), src[L, :, bass.ds(q * 2, 2), :]).then_inc(m["slabs"], 16)
                sp.wait_ge(m["added"], 4 * EP * (ROUNDS - 1))

        @block.sync
        def _(sp):
            def load_fixed(n, kind, arg):
                if kind == "ada":
                    src = ada_src[arg // 6, :, :, (arg % 6) * D:(arg % 6 + 1) * D]
                    dst = wide(n)
                elif kind in ("even_in", "odd_in"):
                    src = (even_in_src if kind == "even_in" else odd_in_src)
                    cols = min(1024, src.shape[2] - 1024 * arg)
                    src = src[:, :, 1024 * arg:1024 * arg + cols]
                    dst = wide(n, cols)
                else:
                    src, dst = out_srcs[kind], wide(n)
                first = ADA_FIRST if kind == "ada" else KD // 2
                sp.dma_start(dst[:, 0:first], src[:, 0:first]).then_inc(slab_in[n % RING], 16)
                sp.dma_start(dst[:, first:KD], src[:, first:KD]).then_inc(rest_in[n % RING], 16)

            def load_pair_half(L, k, half, pair):
                n = MOE0[L] + k
                src = (gate_src, up_src, down_src)[k % 3]
                words = slice(half * KD * F // 2, (half + 1) * KD * F // 2)
                sp.dma_start(pair_slab(n)[:, :, words], src[L, :, bass.ds(pair * 2, 2), words]).then_inc(
                    (slab_in, rest_in)[half][n % RING], 16)

            def load_experts(L):
                before = (head_slabs, mid_slabs)[L]
                for k in range(RING):
                    sp.wait_ge(*before[len(before) - RING + k][2:])
                    for half in range(2):
                        load_pair_half(L, k, half, k // 3)

                def follow(turn, k):
                    pairs = turn * UNROLL + (EP * L + k // 3 + 1)
                    sp.wait_ge(half_used[k % 3], pairs)
                    load_pair_half(L, k + RING, 0, turn * UNROLL + (k + RING) // 3)
                    if k % 3 < 2:
                        sp.wait_ge((gate_done, up_done)[k % 3], pairs)
                    else:
                        sp.wait_ge(down_done, pairs * 2)
                    load_pair_half(L, k + RING, 1, turn * UNROLL + (k + RING) // 3)

                with sp.Fori(0, EP // UNROLL - 1) as i:
                    for k in range(3 * UNROLL):
                        follow(i, k)
                for k in range(3 * UNROLL - RING):
                    follow(EP // UNROLL - 1, k)

            sp.dma_start(CCOL[:, 0, :], c.rearrange("o (p k) -> p (o k)", k=KD)).then_inc(cond_in, 16)
            sp.dma_start(X[:, :, :], x[0].rearrange("(t p) d -> p t d", p=P)).then_inc(x_in, 16)
            load_fixed(0, *head_slabs[0][:2])
            with nc.allow_non_contiguous_dma(reason="small vectors"):
                for L in range(2):
                    sp.dma_start(BADA[:, 6 * L:6 * L + 6, :], b_ada[L].rearrange("(j p k) -> p j k", p=P, k=KD)).then_inc(norm_in, 16)
                    sp.dma_start(GAIN[:, 2 * L, :], mix_norm_g[L].rearrange("(p k) -> p k", k=KD)).then_inc(norm_in, 16)
                    sp.dma_start(GAIN[:, 2 * L + 1, :], ffn_norm_g[L].rearrange("(p k) -> p k", k=KD)).then_inc(norm_in, 16)
            for n, (kind, arg, _, _) in enumerate(head_slabs):
                if n == 0:
                    continue
                if n >= RING:
                    sp.wait_ge(*head_slabs[n - RING][2:])
                load_fixed(n, kind, arg)
            load_experts(0)
            overflow_loads(sp, 0)
            for n, (kind, arg, _, _) in enumerate(mid_slabs):
                if n < RING:
                    q, w = divmod(3 * EP - RING + n, 3)
                    sp.wait_ge((gate_done, up_done, down_done)[w], 2 * (q + 1) if w == 2 else q + 1)
                else:
                    sp.wait_ge(*mid_slabs[n - RING][2:])
                load_fixed(MID0 + n, kind, arg)
            load_experts(1)
            overflow_loads(sp, 1)
            for u in range(4):
                h, t = divmod(u, 2)
                sp.wait_ge(x_added, 2 * ADDS - 4 + u + 1)
                sp.dma_start(out[0, t * P:(t + 1) * P, h * HALF:(h + 1) * HALF],
                             X[:, t, h * HALF:(h + 1) * HALF]).then_inc(out_stored, 16)
            sp.wait_ge(out_stored, 16 * 4)

        @block.gpsimd
        def _(pool):
            g = nc.gpsimd
            steps = [0]

            def link(ins):
                steps[0] += 1
                ins.then_inc(pool_step, 1)
                pool.wait_ge(pool_step, steps[0])

            for t, v in ((IDENT, 0.0), (NEGTRI, -1.0), (NEGONE, -1.0), (ONES, 1.0), (BEFORE, 1.0),
                         (HEADSUM, 0.0), (SEL, 0.0)):
                link(g.memset(t[:, :], v))
            link(g.memset(EPSC[:, :], EPS))
            link(g.affine_select(out=IDENT[:, :], in_=IDENT[:, :], compare_op=ALU.not_equal, fill=1.0, base=0,
                                 pattern=[[-1, P]], channel_multiplier=1))
            link(g.affine_select(out=NEGTRI[:, :], in_=NEGTRI[:, :], compare_op=ALU.is_ge, fill=0.0, base=0,
                                 pattern=[[-1, P]], channel_multiplier=1))
            link(g.affine_select(out=BEFORE[:, :], in_=BEFORE[:, :], compare_op=ALU.is_gt, fill=0.0, base=0,
                                 pattern=[[1, P]], channel_multiplier=-1))
            for h in range(2):
                link(g.memset(HEADSUM[h * HD:(h + 1) * HD, h * HD:(h + 1) * HD], 1.0))
            for r in range(4):
                link(g.memset(SEL[32 * r:32 * r + 1, :], 1.0))
            link(g.iota(SLOTNO[:, :], pattern=[[1, P]], base=0, channel_multiplier=0, allow_small_or_imprecise_dtypes=True))
            link(g.iota(EXPNO[:, :], pattern=[[1, NE]], base=0, channel_multiplier=0, allow_small_or_imprecise_dtypes=True))
            link(g.iota(GRPNO[:, :], pattern=[[1, NG], [0, EPG]], base=0, channel_multiplier=0,
                        allow_small_or_imprecise_dtypes=True))
            link(g.iota(NDIST[:, 0:P], pattern=[[-1, P]], base=0, channel_multiplier=1, allow_small_or_imprecise_dtypes=True))
            link(g.iota(NDIST[:, P:3 * P], pattern=[[-1, 2 * P]], base=P, channel_multiplier=1,
                        allow_small_or_imprecise_dtypes=True))
            g.memset(GL8[:, :, :], LOWEST).then_inc(consts_ready, 1)

            def keep_past(tile, i, ready, done):
                pool.wait_ge(ready, i + 1)
                for h in range(2):
                    for at in (0, 2 * P):
                        v = tile[:, i % 2, h, at:at + P]
                        g.affine_select(out=v, in_=v, compare_op=ALU.is_gt, fill=0.0, base=0,
                                        pattern=[[1, P]], channel_multiplier=-1).then_inc(done, 1)

            for i in range(2):
                keep_past(SPe, i, fail_sum_in, fails_masked)
            for i in range(NPAIR):
                if 1 <= i < NPAIR - 1:
                    keep_past(SPe, i + 1, fail_sum_in, fails_masked)
                keep_past(PRe, i, probs_exp, probs_masked)

            def split_tokens(L):
                for t in range(TB):
                    for part in range(2):
                        pool.wait_ge(split_act, copies_before(L, t, part) + 1)
                        if part == 0:
                            pool.wait_ge(xn_turned, 4 * (2 * L + 1) + 2 * (t + 1))
                        g.tensor_tensor(XN[:, t], XN[:, t], XN3[:, part, t], ALU.subtract).then_inc(split_pool, 1)

            split_tokens(0)

            for h in range(NH):
                if h == 0:
                    pool.wait_ge(qk_out, 16)
                    pool.wait_ge(cols_ready, 4)
                if h >= 2:
                    pool.wait_ge(scores_max, h - 1)
                g.tensor_scalar(BIAS[:, h % 2, :], NDIST[:, :], 2.0 ** (-8.0 * (h + 1) / NH), 0.0,
                                ALU.mult, ALU.add).then_inc(head_bias, 1)
            split_tokens(1)

        @block.scalar
        def _(act):
            a = nc.scalar
            steps = [0]

            def link(ins):
                steps[0] += 1
                ins.then_inc(act_step, 1)
                act.wait_ge(act_step, steps[0])

            def load_vectors(pairs, arrived):
                with nc.allow_non_contiguous_dma(reason="small vectors"):
                    for dst, src in pairs:
                        act.dma_start(dst, src).then_inc(arrived, 16)

            rows = [(CROW[0:TAPS * CB, 0, :], conv_dw[0].rearrange("t (b c) -> (t b) c", c=P)),
                    (CROW[0:8, 1, :], conv_b_glu[0].rearrange("(b c) -> b c", c=P)),
                    (CROW[8:12, 1, :], conv_dw_b[0].rearrange("(b c) -> b c", c=P)),
                    (CROW[12:16, 1, :], conv_ln_g[0].rearrange("(b c) -> b c", c=P)),
                    (CROW[16:20, 1, :], conv_ln_b[0].rearrange("(b c) -> b c", c=P)),
                    (CROW[20:21, 1, :], diff_sub_g)]
            rows += [(CROW[r:r + 1, 1, h * HD:(h + 1) * HD], v)
                     for r, v in ((21, qk_norm_q), (22, qk_norm_k)) for h in range(2)]
            assert len(rows) == N_ROWS
            load_vectors(rows, rows_in)
            a.preload_act_table_set("natural_log_exp_and_others")
            act.wait_ge(cond_negated, 1)
            a.activation(CCOL[:, 1, :], CCOL[:, 1, :], ACT.Exp, scale=-1.0).then_inc(cond_exp, 1)

            def norm_statistics(stage, t):
                if stage % 2:
                    act.wait_ge(x_mixed, 2 * stage - 2 + 2 * (t + 1))
                elif stage:
                    act.wait_ge(x_added, ADDS - 1 + t)
                link(a.activation(XN[:, t, :, :].rearrange("p k q -> p (k q)"), X[:, t, :], ACT.Square,
                                  accum_out=STAT[:, t:t + 1]))
                link(a.activation(STAT[:, 2 + t:3 + t], STAT[:, t:t + 1], ACT.Ln, scale=1.0 / D, bias=EPSC[:, 0:1]))
                a.activation(STAT[:, 2 + t:3 + t], STAT[:, 2 + t:3 + t], ACT.Exp, scale=-0.5).then_inc(norm_stat, 1)

            def modulate(stage, t):
                act.wait_ge(ada_ready, 3 * stage + 2)
                act.wait_ge(xn_turned, 4 * stage + 2 * t + 2)
                bank = turned_banks(stage, t)[1]
                for k in range(KD // 2, KD):
                    ins = a.activation(HT[:, k, t * P:(t + 1) * P], PS[:, bank, (k % 4) * P:(k % 4 + 1) * P], ACT.Identity,
                                       scale=SCALE[:, stage, k:k + 1], bias=SHIFT[:, stage, k:k + 1])
                ins.then_inc(h_act, 1)

            def copy_partials(n):
                act.wait_ge(ada_summed, n + 1)
                if n:
                    act.wait_ge(ada_joined, n)
                a.copy(PART[:, :].rearrange("p (b n) -> p b n", b=2), PS[:, 4:6, :]).then_inc(ada_copied, 1)

            act.wait_ge(x_in, 16)
            act.wait_ge(consts_ready, 1)
            for t in range(TB):
                norm_statistics(0, t)
            copy_partials(0)
            copy_partials(1)
            for t in range(TB):
                modulate(0, t)
            later = [(GATE[:, 0, :], b_ada[0, 2 * D:3 * D].partition_broadcast(P)),
                     (GATE[:, 1, :], b_ada[0, 5 * D:6 * D].partition_broadcast(P))]
            for L in range(2):
                later += [(WR[:, L, :, 0:NG], moe_w_group[L].rearrange("(p k) g -> p k g", k=KD)),
                          (WR[:, L, :, NG:NL], moe_w_router[L].rearrange("(p k) e -> p k e", k=KD)),
                          (RB[:, L, 0:NG], moe_b_group[L].partition_broadcast(P)),
                          (RB[:, L, NG:NL], moe_b_router[L].partition_broadcast(P))]
            later += [(LAMV[:, n, :], v[0].partition_broadcast(P))
                      for n, v in enumerate((lambda_q1, lambda_k1, lambda_q2, lambda_k2))]
            assert len(later) == N_VECTORS
            load_vectors(later, vectors_in)
            def take_projection(u):
                act.wait_ge(proj_done, u + 1)
                if u < 10:
                    ins = a.copy(Ve[:, u - 8, :], PS[:, u % 4, :])
                elif u < 14:
                    ins = a.mul(QTe[:, u - 10, :], PS[:, u % 4, 0:S], QSCALE)
                else:
                    ins = a.copy(KTe[:, u - 14, :], PS[:, u % 4, 0:S])
                ins.then_inc(qkv_out, 1)

            def sigmoid(t, done):
                link(a.activation(t, t, ACT.Exp, scale=-1.0))
                link(a.activation(t, t, ACT.Ln, bias=1.0))
                a.activation(t, t, ACT.Exp, scale=-1.0).then_inc(done, 1)

            act.wait_ge(glu_out, 8)
            sigmoid(CACC[:, :, :], glu_exp)
            for u in range(8, 18):
                take_projection(u)

            def soft_logs(i):
                act.wait_ge(z_ready, i + 1)
                if i >= 2:
                    act.wait_ge(logs_ready, i - 1)
                b = 2 * (i % 2)
                v = SPe[:, i % 2, :, :]
                link(a.activation(v, PS[:, b:b + 2, 0:3 * P], ACT.Abs))
                link(a.activation(v, v, ACT.Exp, scale=-1.0))
                a.activation(v, v, ACT.Ln, bias=1.0).then_inc(softlog, 1)

            def take_heads(i):
                act.wait_ge(pv_done, i + 1)
                a.copy(HT[:, i, :], PS[:, 7, 0:S]).then_inc(heads_out, 1)

            soft_logs(0)
            soft_logs(1)
            copy_partials(2)
            for i in range(NPAIR):
                act.wait_ge(logs_min, i + 1)
                v = PRe[:, i % 2, :, :]
                a.activation(v, v, ACT.Exp).then_inc(probs_exp, 1)
                if i:
                    take_heads(i - 1)
                if i == 1:
                    act.wait_ge(conv_centred, 1)
                    a.activation(CSQ[:, :, :], CACC[:, :, :], ACT.Square).then_inc(conv_squared, 1)
                if i in fills:
                    copy_partials(fills[i])
                if i == 1:
                    act.wait_ge(conv_var, 1)
                    link(a.activation(RSTD[:, :], PS[:, 6, S:2 * S], ACT.Ln, scale=1.0 / CONV, bias=EPSC[:, 0:1]))
                    a.activation(RSTD[:, :], RSTD[:, :], ACT.Exp, scale=-0.5).then_inc(conv_rstd, 1)
                if i + 2 < NPAIR:
                    soft_logs(i + 2)
                if i == 2:
                    act.wait_ge(conv_floor, 1)
                    sigmoid(CSQ[:, :, :], conv_exp)
            take_heads(NPAIR - 1)

            def moe(L):
                stage = 2 * L + 1

                def split(t, part):
                    if part:
                        act.wait_ge(split_pool, 4 * L + 2 * t + part)
                    else:
                        act.wait_ge(xn_ready, 2 * stage + t + 1)
                    a.copy(XN3[:, part, t], XN[:, t]).then_inc(split_act, 1)

                norm_statistics(stage, 0)
                split(0, 0)
                modulate(stage, 0)
                split(0, 1)
                norm_statistics(stage, 1)
                if L == 0:
                    act.dma_start(GATE[:, 0, :], b_ada[1, 2 * D:3 * D].partition_broadcast(P)).then_inc(gate_bias_in, 16)
                split(1, 0)
                modulate(stage, 1)
                split(0, 2)
                split(1, 1)
                act.wait_ge(group_top, L + 1)
                for t in range(TB):
                    a.activation(RT[:, 8 + 2 * t:10 + 2 * t, :].rearrange("p a b -> p (a b)")[:, 0:NG],
                                 GL8[:, t, 0:NG], ACT.Exp, bias=RT[:, 0, t:t + 1],
                                 accum_out=RT[:, 1, t:t + 1]).then_inc(group_exp, 1)
                split(1, 2)
                act.wait_ge(expert_top, L + 1)
                a.activation(RT[:, 5, :], RT[:, 4, :], ACT.Exp).then_inc(expert_exp, 1)
                copy_partials(6 * L + 5)

                def spread(count, buf):
                    act.wait_ge(gathered, count)
                    for k in range(KD // 2, KD):
                        a.activation(XT[:, buf, k, :], PS[:, 2 + k // 4, (k % 4) * P:(k % 4 + 1) * P], ACT.Identity,
                                     scale=SCALE[:, stage, k:k + 1], bias=SHIFT[:, stage, k:k + 1]).then_inc(xt_act, 1)

                spread((EP + 1) * L + 1, 0)
                a.preload_act_table_set("exp_and_others")
                with act.Fori(0, EP // UNROLL) as i:
                    for j in range(UNROLL):
                        n = i * UNROLL + (EP * L + j)
                        act.wait_ge(gate_done, n + 1)
                        a.activation(TH[:, :], PS[:, 0, :], ACT.Tanh, scale=0.5).then_inc(tanh_done, 1)
                        spread(n + (L + 2), (j + 1) % 2)
                        act.wait_ge(weights_turned, n + 1)
                        a.copy(SWT[:, j % 2, :, :].rearrange("p t s -> p (t s)"), PS[:, 5, 0:TB * P]).then_inc(weightsT_ready, 1)
                        act.wait_ge(hidden_turned, n + 1)
                        a.copy(HIDT[:, :, :].rearrange("p k s -> p (k s)"), PS[:, 4, :]).then_inc(hiddenT_ready, 1)

                m = more[L]
                act.wait_ge(count_ready, L + 1)
                count = act.value_load(CNTI[0:1, 0:1], min_val=0, max_val=S)
                with act.If(count > SLOT):
                    with act.Fori(0, EP * (ROUNDS - 1)) as step:
                        act.wait_ge(m["gate"], step + 1)
                        a.activation(TH[:, :], PS[:, 0, :], ACT.Tanh, scale=0.5).then_inc(m["tanh"], 1)
                        act.wait_ge(m["turned"], step + 1)
                        a.copy(SWT[:, 0, :, :].rearrange("p t s -> p (t s)"), PS[:, 5, 0:TB * P]).then_inc(m["copied"], 1)
                        a.copy(HIDT[:, :, :].rearrange("p k s -> p (k s)"), PS[:, 4, :]).then_inc(m["copied"], 1)
                    act.wait_ge(m["added"], 4 * EP * (ROUNDS - 1))

            moe(0)

            a.preload_act_table_set("natural_log_exp_and_others")
            for t in range(TB):
                norm_statistics(2, t)
            act.dma_start(GATE[:, 1, :], b_ada[1, 5 * D:6 * D].partition_broadcast(P)).then_inc(gate_bias_in, 16)
            copy_partials(6)
            copy_partials(7)
            for t in range(TB):
                modulate(2, t)
            def exps(h):
                act.wait_ge(scores_max, h + 1)
                for cc in range(2):
                    for t in range(TB):
                        v = SCo[:, h % 2, cc, t * P:(1 + 2 * t) * P]
                        k = 2 * cc + t
                        ins = a.activation(v, v, ACT.Exp, bias=STo[:, h % 2, 4 + k:5 + k], accum_out=STo[:, h % 2, 8 + k:9 + k])
                        ins.then_inc(scores_exp, 1)

            act.wait_ge(lam_sum, 1)
            a.activation(LAM[:, 2:4], LAM[:, 0:2], ACT.Exp).then_inc(lam_exp, 1)
            for u in range(20):
                if u < 18:
                    act.wait_ge(proj_done, 18 + u + 1)
                if u < 16:
                    if u >= 2:
                        act.wait_ge(qk_mean, u - 1)
                    a.activation(SQo[u % 2][:, :], PS[:, u % 4, 0:S], ACT.Square).then_inc(qk_squared, 1)
                if 1 <= u <= 16:
                    w = u - 1
                    act.wait_ge(qk_mean, w + 1)
                    if w >= 2:
                        act.wait_ge(qk_out, w - 1)
                    link(a.activation(RSo[w % 2][:, :], PS[:, 4 + w % 2, 0:S], ACT.Ln, scale=1.0 / HD, bias=EPSC[:, 0:1]))
                    a.activation(RSo[w % 2][:, :], RSo[w % 2][:, :], ACT.Exp, scale=-0.5).then_inc(qk_rstd, 1)
                if u >= 18:
                    exps(u - 18)
                    act.wait_ge(proj_done, 18 + u + 1)
                if u >= 16:
                    v = u - 16
                    a.copy(Vo[:, v // 2, (v % 2) * HALF:(v % 2 + 1) * HALF], PS[:, 6 + u % 2, :]).then_inc(v_out, 1)

            def out_rstd(h):
                act.wait_ge(o_mean, h + 1)
                if h:
                    act.wait_ge(o_out, h)
                link(a.activation(RSo[0][:, :], PS[:, 7, 0:S], ACT.Ln, scale=1.0 / P, bias=EPSC[:, 0:1]))
                a.activation(RSo[0][:, :], RSo[0][:, :], ACT.Exp, scale=-0.5).then_inc(o_rstd, 1)

            for h in range(NH):
                act.wait_ge(diff_turned, h + 1)
                a.copy(PTo[:, :], PS[:, 2, 0:3 * P]).then_inc(diffT_ready, 1)
                if h:
                    out_rstd(h - 1)
                if h + 2 < NH:
                    exps(h + 2)
                if h in fills1:
                    copy_partials(fills1[h])
                act.wait_ge(o_done, h + 1)
                a.activation(SQo[0][:, :], PS[:, 3, 0:S], ACT.Square).then_inc(o_squared, 1)
            out_rstd(NH - 1)

            moe(1)

        @block.vector
        def _(dve):
            v = nc.vector
            steps = [0]

            def link(ins):
                steps[0] += 1
                ins.then_inc(dve_step, 1)
                dve.wait_ge(dve_step, steps[0])

            dve.wait_ge(cond_in, 16)
            v.tensor_scalar(CCOL[:, 1, :], CCOL[:, 0, :], SIGMOID_FLOOR, None, ALU.max).then_inc(cond_negated, 1)
            dve.wait_ge(cond_exp, 1)
            link(v.tensor_scalar(CCOL[:, 1, :], CCOL[:, 1, :], 1.0, None, ALU.add))
            link(v.reciprocal(CCOL[:, 2, :], CCOL[:, 1, :]))
            link(v.tensor_tensor(CCOL[:, 1, :], CCOL[:, 0, :], CCOL[:, 2, :], ALU.mult))
            v.tensor_copy(CREP[:, :, :], CCOL[:, 1, :].unsqueeze(2).broadcast_to([P, KD, 32])).then_inc(cond_in_place, 1)

            def take_modulation(n):
                L, j = divmod(n, 6)
                dve.wait_ge(ada_joined, n + 1)
                if j in (0, 3):
                    v.tensor_tensor(SHIFT[:, 2 * L + j // 3, :], PS[:, 6, 0:KD], BADA[:, n, :], ALU.add).then_inc(ada_ready, 1)
                elif j in (1, 4):
                    st = 2 * L + j // 3
                    link(v.tensor_tensor(SCALE[:, st, :], PS[:, 6, 0:KD], BADA[:, n, :], ALU.add))
                    v.scalar_tensor_tensor(out=SCALE[:, st, :], in0=SCALE[:, st, :], scalar=1.0, in1=GAIN[:, st, :],
                                           op0=ALU.add, op1=ALU.mult).then_inc(ada_ready, 1)
                else:
                    row = GATE[:, j // 3, :]
                    if L == 0:
                        dve.wait_ge(vectors_in, 16 * N_VECTORS)
                    else:
                        dve.wait_ge(gate_bias_in, 32)
                    link(v.tensor_tensor(row[:, 0:HALF], PS[:, 6, :], row[:, 0:HALF], ALU.add))
                    v.tensor_tensor(row[:, HALF:D], PS[:, 4, :], row[:, HALF:D], ALU.add).then_inc(ada_ready, 1)

            def normalise(stage, t):
                dve.wait_ge(norm_stat, 2 * stage + t + 1)
                v.tensor_scalar(XN[:, t, :, :], X[:, t, :].rearrange("p (q k) -> p k q", k=KD),
                                STAT[:, 2 + t:3 + t], None, ALU.mult).then_inc(xn_ready, 1)

            def modulate(stage, t):
                dve.wait_ge(ada_ready, 3 * stage + 2)
                dve.wait_ge(xn_turned, 4 * stage + 2 * t + 1)
                bank = turned_banks(stage, t)[0]
                for k in range(KD // 2):
                    ins = v.tensor_scalar(HT[:, k, t * P:(t + 1) * P], PS[:, bank, k * P:(k + 1) * P], SCALE[:, stage, k:k + 1],
                                          SHIFT[:, stage, k:k + 1], ALU.mult, ALU.add)
                ins.then_inc(h_dve, 1)

            def add_mixed(L, t):
                dve.wait_ge(ada_ready, 9 if L else 3)
                for h in range(2):
                    u = 2 * t + h
                    dve.wait_ge(wout_done, 4 * L + u + 1)
                    y = PS[:, mixed_banks[u], :]
                    link(v.tensor_tensor(y, y, GATE[:, 0, h * HALF:(h + 1) * HALF], ALU.mult))
                    xs = X[:, t, h * HALF:(h + 1) * HALF]
                    v.tensor_tensor(xs, y, xs, ALU.add).then_inc(x_mixed, 1)

            for t in range(TB):
                normalise(0, t)
            dve.wait_ge(norm_in, 16 * 6)
            take_modulation(0)
            dve.wait_ge(rows_turned, 2)
            v.tensor_copy(CV1[:, :], PS[:, 6, 0:TAPS * CB]).then_inc(cols_ready, 1)
            v.tensor_copy(CV2[:, 0:23], PS[:, 6, P:P + 23]).then_inc(cols_ready, 1)
            take_modulation(1)
            for t in range(TB):
                modulate(0, t)
            dve.wait_ge(cols_ready, 2)
            v.tensor_scalar(CV2[:, 23:24], CV2[:, 20:21], 1.0 - LAM0, None, ALU.mult)
            v.tensor_scalar(CV2[:, 24:25], CV2[:, 21:22], QSCALE, None, ALU.mult).then_inc(cols_ready, 1)
            link(v.memset(CIN[:, :, 0:PAD], 0.0))
            for b in range(CB):
                dve.wait_ge(proj_done, b + 1)
                v.tensor_scalar(CIN[:, b, PAD:PAD + S], PS[:, b % 4, 0:S], CV2[:, b:b + 1], None,
                                ALU.add).then_inc(glu_out, 1)
            for b in range(CB):
                dve.wait_ge(proj_done, CB + b + 1)
                v.tensor_scalar(CACC[:, b, :], PS[:, (CB + b) % 4, 0:S], CV2[:, 4 + b:5 + b], SIGMOID_FLOOR,
                                ALU.add, ALU.max).then_inc(glu_out, 1)

            def glu():
                dve.wait_ge(glu_exp, 1)
                link(v.tensor_tensor(CIN[:, :, PAD:PAD + S], CIN[:, :, PAD:PAD + S], CACC[:, :, :], ALU.mult))

            def conv_taps(lo, hi):
                for j in range(lo, hi):
                    for b in range(CB):
                        src = CIN[:, b, j:j + S]
                        tap = CV1[:, j * CB + b:j * CB + b + 1]
                        if j == 0:
                            ins = v.tensor_scalar(CACC[:, b, :], src, tap, CV2[:, 8 + b:9 + b], ALU.mult, ALU.add)
                        else:
                            dve.wait_ge(conv_done, CB * (j - 1) + b + 1)
                            ins = v.scalar_tensor_tensor(out=CACC[:, b, :], in0=src, scalar=tap, in1=CACC[:, b, :],
                                                         op0=ALU.mult, op1=ALU.add)
                        ins.then_inc(conv_done, 1)

            def soft_plus(i):
                dve.wait_ge(softlog, i + 1)
                b = 2 * (i % 2)
                s = SPe[:, i % 2, :, :]
                v.scalar_tensor_tensor(out=s, in0=PS[:, b:b + 2, 0:3 * P], scalar=0.0, in1=s,
                                       op0=ALU.max, op1=ALU.add).then_inc(fail_sum_in, 1)

            glu()
            late_taps = TAPS - 6
            conv_taps(0, late_taps)
            soft_plus(0)
            soft_plus(1)
            for i in range(NPAIR):
                dve.wait_ge(logs_ready, i + 1)
                if i >= 2:
                    dve.wait_ge(pv_done, i - 1)
                b = 2 * (i % 2)
                v.tensor_scalar(PRe[:, i % 2, :, :], PS[:, b:b + 2, 0:3 * P], 0.0, None, ALU.min).then_inc(logs_min, 1)
                if i == 0:
                    take_modulation(2)
                    conv_taps(late_taps, TAPS)
                if i == 1:
                    dve.wait_ge(conv_mean, 1)
                    for b in range(CB):
                        ins = v.scalar_tensor_tensor(out=CACC[:, b, :], in0=PS[:, 6, 0:S], scalar=-1.0 / CONV,
                                                     in1=CACC[:, b, :], op0=ALU.mult, op1=ALU.add)
                    ins.then_inc(conv_centred, 1)
                if i == 2:
                    dve.wait_ge(conv_rstd, 1)
                    for b in range(CB):
                        ins = v.scalar_tensor_tensor(out=CACC[:, b, :], in0=CACC[:, b, :], scalar=CV2[:, 12 + b:13 + b],
                                                     in1=RSTD[:, :], op0=ALU.mult, op1=ALU.mult)
                    link(ins)
                    for b in range(CB):
                        ins = v.tensor_scalar(CSQ[:, b, :], CACC[:, b, :], CV2[:, 16 + b:17 + b], SIGMOID_FLOOR,
                                              ALU.add, ALU.max)
                    ins.then_inc(conv_floor, 1)
                    take_modulation(4)
                if i == 3:
                    dve.wait_ge(conv_exp, 1)
                    for b in range(CB):
                        ins = v.scalar_tensor_tensor(out=HT[:, NPAIR + b, :], in0=CACC[:, b, :],
                                                     scalar=CV2[:, 16 + b:17 + b], in1=CSQ[:, b, :],
                                                     op0=ALU.add, op1=ALU.mult)
                    ins.then_inc(conv_out, 1)
                if i + 2 < NPAIR:
                    soft_plus(i + 2)
                if i == 0:
                    take_modulation(3)
            dve.wait_ge(consts_ready, 1)
            link(v.scalar_tensor_tensor(out=NDIST[:, :], in0=NDIST[:, :], scalar=-1.0, in1=NDIST[:, :],
                                        op0=ALU.mult, op1=ALU.min))
            link(v.memset(NDIST[0:HD, HD:P], NEG))
            v.memset(NDIST[0:HD, P + 3 * HD:3 * P], NEG).then_inc(cols_ready, 1)
            dve.wait_ge(vectors_in, 16 * N_VECTORS)
            for n in range(2):
                link(v.tensor_tensor(LAMV[:, 2 * n, :], LAMV[:, 2 * n, :], LAMV[:, 2 * n + 1, :], ALU.mult))
                ins = v.tensor_reduce(LAM[:, n:n + 1], LAMV[:, 2 * n, :], AX.X, ALU.add)
                if n == 0:
                    link(ins)
                else:
                    ins.then_inc(lam_sum, 1)

            def slot_positions():
                e64, off, pos = POST[:, 0], POST[:, 1], POST[:, 2]
                return [lambda: v.tensor_scalar(off, RANK[:, :, :], 0.0, FAR, ALU.is_lt, ALU.mult),
                        lambda: v.tensor_scalar(pos, RANK[:, :, :], float(SLOT), FAR, ALU.is_ge, ALU.mult),
                        lambda: v.tensor_tensor(off, off, pos, ALU.add),
                        lambda: v.tensor_scalar(e64, EXPSEL[:, :, :], float(SLOT), None, ALU.mult),
                        lambda: v.tensor_tensor(pos, RANK[:, :, :], e64, ALU.add),
                        lambda: v.tensor_tensor(POS[:, :, :], pos, off, ALU.add)]

            def moe(L):
                stage = 2 * L + 1
                for t in range(TB):
                    add_mixed(L, t)
                    normalise(stage, t)
                    modulate(stage, t)
                    if t == 0:
                        v.memset(YS[:, :], 0.0).then_inc(y_ready, 2)
                dve.wait_ge(logits_done, L + 1)
                logits = PS[:, 7, 0:TB * NL].rearrange("p (t n) -> p t n", t=TB)
                v.tensor_tensor(GL8[:, :, 0:NG], logits[:, :, 0:NG],
                                RB[:, L, 0:NG].unsqueeze(1).broadcast_to([P, TB, NG]), ALU.add)
                link(v.tensor_tensor(LG[:, :, :], logits[:, :, NG:NL],
                                     RB[:, L, NG:NL].unsqueeze(1).broadcast_to([P, TB, NE]), ALU.add))
                for t in range(TB):
                    ins = v.max(GM8[:, t, :], GL8[:, t, :])
                link(ins)
                v.tensor_scalar(RT[:, 0, :], GM8[:, :, 0], -1.0, None, ALU.mult).then_inc(group_top, 1)
                for t in range(TB):
                    ins = v.max_index(GI8[:, t, :], GM8[:, t, :], GL8[:, t, :])
                link(ins)
                link(v.tensor_copy(RT[:, 2, :], GI8[:, :, 0]))
                for t in range(TB):
                    ins = v.tensor_scalar(EM[:, t, :], GRPNO[:, :], RT[:, 2, t:t + 1], NEG, ALU.not_equal, ALU.mult)
                link(ins)
                link(v.tensor_tensor(EM[:, :, :], EM[:, :, :], LG[:, :, :], ALU.add))
                for t in range(TB):
                    ins = v.max(EM8[:, t, :], EM[:, t, :])
                link(ins)
                v.tensor_tensor(RT[:, 4, :], EM8[:, :, 1], EM8[:, :, 0], ALU.subtract).then_inc(expert_top, 1)
                for t in range(TB):
                    ins = v.max_index(EI8[:, t, :], EM8[:, t, :], EM[:, t, :])
                link(ins)
                link(v.tensor_copy(EXPSEL[:, :, :], EI8[:, :, 0:2]))
                for s in range(2):
                    for t in range(TB):
                        ins = v.tensor_scalar(ONEHOT[:, s, t, :], EXPNO[:, :], EXPSEL[:, t, s:s + 1], None, ALU.is_equal)
                link(ins)
                v.tensor_tensor(ONEHOT[:, 2, :, :], ONEHOT[:, 0, :, :], ONEHOT[:, 1, :, :], ALU.add).then_inc(onehot_ready, 1)
                first, far, pos = POST[:, 0], POST[:, 1], POST[:, 2]
                v.tensor_scalar(first, EXPSEL[:, :, :], float(SLOT), None, ALU.mult)
                dve.wait_ge(rank_done, L + 1)
                for s in range(2):
                    ins = v.tensor_tensor(ONEHOT[:, s, :, :], ONEHOT[:, s, :, :],
                                          PS[:, 7, P:P + TB * NE].rearrange("p (t n) -> p t n", t=TB), ALU.mult)
                link(ins)
                link(v.tensor_reduce(RANK.rearrange("p t s -> p s t"), ONEHOT[:, 0:2, :, :], AX.X, ALU.add))
                v.tensor_scalar(far, RANK[:, :, :], float(SLOT), FAR, ALU.is_ge, ALU.mult)
                link(v.tensor_tensor(pos, RANK[:, :, :], first, ALU.add))
                link(v.tensor_tensor(POS[:, :, :], pos, far, ALU.add))

                def build_slots(buf, done):
                    for t in range(TB):
                        v.tensor_scalar(TMPA[:, t, :], SLOTNO[:, :], POS[:, t, 0:1], None, ALU.is_equal).then_inc(done[0], 1)
                    for t in range(TB):
                        dve.wait_ge(done[0], done[1] + t + 1)
                        v.scalar_tensor_tensor(out=SG[:, buf, t, :], in0=SLOTNO[:, :], scalar=POS[:, t, 1:2], in1=TMPA[:, t, :],
                                               op0=ALU.is_equal, op1=ALU.add).then_inc(slots_built, 1)

                def spread(count, buf):
                    dve.wait_ge(gathered, count)
                    for k in range(KD // 2):
                        v.tensor_scalar(XT[:, buf, k, :], PS[:, 2 + k // 4, (k % 4) * P:(k % 4 + 1) * P],
                                        SCALE[:, stage, k:k + 1], SHIFT[:, stage, k:k + 1],
                                        ALU.mult, ALU.add).then_inc(xt_dve, 1)

                def add_combined(done):
                    for u in range(4):
                        h, t = divmod(u, 2)
                        dve.wait_ge(combined, done + u + 1)
                        xs = X[:, t, h * HALF:(h + 1) * HALF]
                        v.tensor_tensor(xs, PS[:, 4 + t, :], xs, ALU.add).then_inc(x_added, 1)

                per = 7
                base = (per * EP + 2) * L
                build_slots(0, (slot_step, base))
                dve.wait_ge(ada_summed, 6 * (L + 1))
                v.memset(SWT[:, :, :, :], 0.0).then_inc(x_added, 1)
                link(v.tensor_reduce(CNT[:, :], PS[:, 7, 2 * P:2 * P + NE], AX.X, ALU.max))
                v.tensor_copy(CNTI[:, :], CNT[:, :]).then_inc(count_ready, 1)
                dve.wait_ge(group_exp, 2 * (L + 1))
                dve.wait_ge(expert_exp, L + 1)
                link(v.tensor_scalar(RT[:, 6, :], RT[:, 5, :], 1.0, None, ALU.add))
                link(v.tensor_tensor(RT[:, 6, :], RT[:, 6, :], RT[:, 1, :], ALU.mult))
                link(v.reciprocal(EXPW[:, :, 0], RT[:, 6, :]))
                link(v.tensor_tensor(EXPW[:, :, 1], EXPW[:, :, 0], RT[:, 5, :], ALU.mult))
                spread((EP + 1) * L + 1, 0)
                take_modulation(6 * L + 5)
                dve.wait_ge(ada_ready, 6 * (L + 1))
                with dve.Fori(0, EP // UNROLL) as i:
                    for j in range(UNROLL):
                        n = i * UNROLL + (EP * L + j)
                        st = i * (UNROLL * per) + (base + 2 + per * j)
                        for t in range(TB):
                            v.tensor_scalar(TMPB[:, t, :], SLOTNO[:, :], POS[:, t, 0:1], EXPW[:, t, 0:1],
                                            ALU.is_equal, ALU.mult).then_inc(slot_step, 1)
                            v.tensor_scalar(TMPC[:, t, :], SLOTNO[:, :], POS[:, t, 1:2], EXPW[:, t, 1:2],
                                            ALU.is_equal, ALU.mult).then_inc(slot_step, 1)
                        for t in range(TB):
                            dve.wait_ge(slot_step, st + 2 * t + 2)
                            v.tensor_tensor(SW[:, t, :], TMPB[:, t, :], TMPC[:, t, :], ALU.add).then_inc(weights_built, 1)
                        dve.wait_ge(slot_step, st + 4)
                        v.tensor_scalar(POS[:, :, :], POS[:, :, :], -float(P), None, ALU.add).then_inc(slot_step, 1)
                        dve.wait_ge(slot_step, st + 5)
                        build_slots((j + 1) % 2, (slot_step, st + 5))
                        dve.wait_ge(tanh_done, n + 1)
                        v.scalar_tensor_tensor(out=T1[:, :], in0=TH[:, :], scalar=1.0, in1=PS[:, 0, :],
                                               op0=ALU.add, op1=ALU.mult).then_inc(t1_done, 1)
                        add_combined(i * (4 * UNROLL) + (4 * (EP + 1) * L + 4 * j))
                        dve.wait_ge(t1_done, n + 1)
                        dve.wait_ge(up_done, n + 1)
                        v.scalar_tensor_tensor(out=HID[:, :, :].rearrange("p k q -> p q k"),
                                               in0=T1[:, :].rearrange("p (q k) -> p q k", k=KF), scalar=0.5,
                                               in1=PS[:, 1, :].rearrange("p (q k) -> p q k", k=KF),
                                               op0=ALU.mult, op1=ALU.mult).then_inc(hidden_ready, 1)
                        spread(n + (L + 2), (j + 1) % 2)
                        for h in range(2):
                            dve.wait_ge(down_done, n * 2 + (h + 1))
                            v.tensor_tensor(YS[:, h * HALF:(h + 1) * HALF], PS[:, 6 + h, :],
                                            GATE[:, 1, h * HALF:(h + 1) * HALF], ALU.mult).then_inc(y_ready, 1)
                add_combined(4 * (EP + 1) * L + 4 * EP)

                m = more[L]
                count = dve.value_load(CNTI[0:1, 0:1], min_val=0, max_val=S)
                per_round, per_pair = 8, 12
                with dve.If(count > SLOT):
                    v.tensor_copy(CNT[:, :], CNT[:, :]).then_inc(m["dve"], 1)
                    with dve.Fori(0, ROUNDS - 1) as r:
                        at = r * (per_round + per_pair * EP) + 1
                        dve.wait_ge(m["dve"], at)
                        v.tensor_scalar(RANK[:, :, :], RANK[:, :, :], -float(SLOT), None, ALU.add).then_inc(m["dve"], 1)
                        for n, f in enumerate(slot_positions()):
                            dve.wait_ge(m["dve"], at + n + 1)
                            f().then_inc(m["dve"], 1)
                        dve.wait_ge(m["dve"], at + 7)
                        v.tensor_copy(CNT[:, :], CNT[:, :]).then_inc(m["dve"], 1)
                        with dve.Fori(0, EP) as q:
                            step = r * EP + q
                            st = r * (per_round + per_pair * EP) + q * per_pair + (per_round + 1)
                            dve.wait_ge(m["dve"], st)
                            for t in range(TB):
                                v.tensor_scalar(TMPA[:, t, :], SLOTNO[:, :], POS[:, t, 0:1], None,
                                                ALU.is_equal).then_inc(m["dve"], 1)
                                v.tensor_scalar(TMPB[:, t, :], SLOTNO[:, :], POS[:, t, 0:1], EXPW[:, t, 0:1],
                                                ALU.is_equal, ALU.mult).then_inc(m["dve"], 1)
                                v.tensor_scalar(TMPC[:, t, :], SLOTNO[:, :], POS[:, t, 1:2], EXPW[:, t, 1:2],
                                                ALU.is_equal, ALU.mult).then_inc(m["dve"], 1)
                            dve.wait_ge(m["dve"], st + 6)
                            for t in range(TB):
                                v.tensor_tensor(SW[:, t, :], TMPB[:, t, :], TMPC[:, t, :], ALU.add).then_inc(m["slots"], 1)
                                v.scalar_tensor_tensor(out=SG[:, 0, t, :], in0=SLOTNO[:, :], scalar=POS[:, t, 1:2],
                                                       in1=TMPA[:, t, :], op0=ALU.is_equal, op1=ALU.add).then_inc(m["slots"], 1)
                            dve.wait_ge(m["slots"], step * 4 + 4)
                            v.tensor_scalar(POS[:, :, :], POS[:, :, :], -float(P), None, ALU.add).then_inc(m["dve"], 1)
                            dve.wait_ge(m["gathered"], step + 1)
                            for k in range(KD):
                                ins = v.tensor_scalar(XT[:, 0, k, :], PS[:, 2 + k // 4, (k % 4) * P:(k % 4 + 1) * P],
                                                      SCALE[:, stage, k:k + 1], SHIFT[:, stage, k:k + 1], ALU.mult, ALU.add)
                            ins.then_inc(m["dve"], 1)
                            dve.wait_ge(m["tanh"], step + 1)
                            v.scalar_tensor_tensor(out=T1[:, :], in0=TH[:, :], scalar=1.0, in1=PS[:, 0, :],
                                                   op0=ALU.add, op1=ALU.mult).then_inc(m["dve"], 1)
                            dve.wait_ge(m["dve"], st + 9)
                            dve.wait_ge(m["up"], step + 1)
                            v.scalar_tensor_tensor(out=HID[:, :, :].rearrange("p k q -> p q k"),
                                                   in0=T1[:, :].rearrange("p (q k) -> p q k", k=KF), scalar=0.5,
                                                   in1=PS[:, 1, :].rearrange("p (q k) -> p q k", k=KF),
                                                   op0=ALU.mult, op1=ALU.mult).then_inc(m["dve"], 1)
                            dve.wait_ge(m["down"], step * 2 + 2)
                            for h in range(2):
                                v.tensor_tensor(YS[:, h * HALF:(h + 1) * HALF], PS[:, 6 + h, :],
                                                GATE[:, 1, h * HALF:(h + 1) * HALF], ALU.mult).then_inc(m["dve"], 1)
                            for u in range(4):
                                t, h = divmod(u, 2)
                                dve.wait_ge(m["combined"], step * 4 + (u + 1))
                                xs = X[:, t, h * HALF:(h + 1) * HALF]
                                v.tensor_tensor(xs, PS[:, u, :], xs, ALU.add).then_inc(m["added"], 1)
                    dve.wait_ge(m["added"], 4 * EP * (ROUNDS - 1))

            moe(0)

            v.tensor_copy(CREP1[:, :, :], CCOL[:, 1, :].unsqueeze(2).broadcast_to([P, KD, 32])).then_inc(cond_in_place, 1)
            for t in range(TB):
                normalise(2, t)
            take_modulation(6)
            take_modulation(7)
            for t in range(TB):
                modulate(2, t)
            dve.wait_ge(lam_exp, 1)
            link(v.tensor_tensor(LAM[:, 4:5], LAM[:, 3:4], LAM[:, 2:3], ALU.subtract))
            link(v.tensor_scalar(LAM[:, 5:6], LAM[:, 4:5], -LAM0, None, ALU.add))
            for u in range(16):
                dve.wait_ge(qk_rstd, u + 1)
                dst, gain = (QTo, CV2[:, 24:25]) if u < 8 else (KTo, CV2[:, 22:23])
                v.scalar_tensor_tensor(out=dst[:, u % 8, :], in0=PS[:, u % 4, 0:S], scalar=gain, in1=RSo[u % 2][:, :],
                                       op0=ALU.mult, op1=ALU.mult).then_inc(qk_out, 1)

            def biased(h):
                dve.wait_ge(scores_done, h + 1)
                dve.wait_ge(head_bias, h + 1)
                if h >= 2:
                    dve.wait_ge(diff_ready, 2 * (h - 1))
                for cc in range(2):
                    for t in range(TB):
                        at = slice(t * P, (1 + 2 * t) * P)
                        k = 2 * cc + t
                        ins = v.tensor_tensor_reduce(SCo[:, h % 2, cc, at], PS[:, cc, at], BIAS[:, h % 2, at],
                                                     1.0, LOWEST, ALU.add, ALU.max, STo[:, h % 2, k:k + 1])
                link(ins)
                v.tensor_scalar(STo[:, h % 2, 4:8], STo[:, h % 2, 0:4], -1.0, None, ALU.mult).then_inc(scores_max, 1)

            def head_out(h):
                dve.wait_ge(o_rstd, h + 1)
                v.scalar_tensor_tensor(out=HT[:, h, :], in0=PS[:, 3, 0:S], scalar=CV2[:, 23:24], in1=RSo[0][:, :],
                                       op0=ALU.mult, op1=ALU.mult).then_inc(o_out, 1)

            biased(0)
            biased(1)
            for h in range(NH):
                dve.wait_ge(scores_exp, 4 * (h + 1))
                st = STo[:, h % 2, :]
                link(v.reciprocal(st[:, 12:16], st[:, 8:12]))
                v.tensor_scalar(st[:, 16:18], st[:, 14:16], LAM[:, 5:6], None, ALU.mult)
                if h >= 1:
                    dve.wait_ge(diff_turned, h)
                for t in range(TB):
                    at = slice(t * P, (1 + 2 * t) * P)
                    ins = v.tensor_scalar(SCo[:, h % 2, 0, at], SCo[:, h % 2, 0, at], st[:, 12 + t:13 + t], None, ALU.mult)
                link(ins)
                for t in range(TB):
                    at = slice(t * P, (1 + 2 * t) * P)
                    v.scalar_tensor_tensor(out=PRo[:, at], in0=SCo[:, h % 2, 1, at], scalar=st[:, 16 + t:17 + t],
                                           in1=SCo[:, h % 2, 0, at], op0=ALU.mult, op1=ALU.add).then_inc(diff_ready, 1)
                if h - 1 in fills1:
                    take_modulation(fills1[h - 1])
                if h + 2 < NH:
                    biased(h + 2)
                if h:
                    head_out(h - 1)
            head_out(NH - 1)
            moe(1)

        @block.tensor
        def _(pe):
            def mm(out_, lhsT, rhs, first, last, **kw):
                return pe.matmul(out_, lhsT, rhs, start=first, stop=last, **kw)

            def slab_ready(n):
                pe.wait_ge(slab_in[n % RING], landed(n))

            def rest_ready(n):
                pe.wait_ge(rest_in[n % RING], landed(n))

            def modulation_sums(n, lo=0, hi=KD):
                s = slab_index("ada", n)
                if lo == 0:
                    slab_ready(s)
                    if n in (0, 6):
                        pe.wait_ge(cond_in_place, 1 + n // 6)
                    if n:
                        pe.wait_ge(ada_copied, n)
                    if n and n % 3 == 0:
                        pe.wait_ge(ada_ready, n)
                cond = CREP if n < 6 else CREP1
                for part in (range(lo, min(hi, ADA_FIRST)), range(max(lo, ADA_FIRST), hi)):
                    if ADA_FIRST in part:
                        rest_ready(s)
                    for h in range(2):
                        for k in part:
                            g = k % 4
                            ins = mm(PS[32 * g:32 * g + 32, 4 + h, :], cond[:, k, :], wide(s)[:, k, h * HALF:(h + 1) * HALF],
                                     k < 4, k >= 4, skip_group_check=True)
                if hi == KD:
                    ins.then_inc(ada_summed, 1)

            def modulation_join(n):
                pe.wait_ge(ada_copied, n + 1)
                if n:
                    pe.wait_ge(ada_ready, n)
                if n == 1:
                    pe.wait_ge(cols_ready, 2)
                if n % 3 == 2:
                    mm(PS[:, 6, :], SEL[:, :], PART[:, 0:HALF], True, True)
                    mm(PS[:, 4, :], SEL[:, :], PART[:, HALF:D], True, True).then_inc(ada_joined, 1)
                else:
                    cols = PART[:, :].rearrange("p (q k) -> p k q", k=KD)
                    for k in range(KD):
                        ins = mm(PS[:, 6, k:k + 1], cols[:, k, :], SEL[:, 0:1], True, True)
                    ins.then_inc(ada_joined, 1)

            def small_columns():
                pe.wait_ge(rows_in, 16 * N_ROWS)
                pe.wait_ge(ada_ready, 1)
                pe.transpose(PS[:, 6, 0:TAPS * CB], CROW[0:TAPS * CB, 0, :], IDENT[0:TAPS * CB, 0:TAPS * CB]).then_inc(rows_turned, 1)
                pe.transpose(PS[:, 6, P:P + 23], CROW[0:23, 1, :], IDENT[0:23, 0:23]).then_inc(rows_turned, 1)

            def turn_xn(stage, t):
                pe.wait_ge(xn_ready, 2 * stage + t + 1)
                for b, bank in enumerate(turned_banks(stage, t)):
                    for k in range(4):
                        ins = pe.transpose(PS[:, bank, k * P:(k + 1) * P], XN[:, t, 4 * b + k, :], IDENT[:, :])
                    ins.then_inc(xn_turned, 1)

            def h_in_place(stage, blocks):
                pe.wait_ge(h_dve, 2 * stage + blocks)
                pe.wait_ge(h_act, 2 * stage + blocks)

            def project_T(bank, w, cols, first_of=None, tiles=range(KD)):
                for k in tiles:
                    if first_of is not None and k == KD // 2:
                        rest_ready(first_of)
                    ins = mm(PS[:, bank, 0:S], w[:, k, cols:cols + P], HT[:, k, :], k == 0, k == KD - 1,
                             skip_group_check=True)
                return ins

            def project(bank, w, cols, t, first_of=None):
                for k in range(KD):
                    if first_of is not None and k == KD // 2:
                        rest_ready(first_of)
                    ins = mm(PS[:, bank, :], HT[:, k, t * P:(t + 1) * P], w[:, k, cols:cols + HALF], k == 0, k == KD - 1)
                return ins

            mixed = {}

            def mix_out(L, u, blocks):
                t, h = divmod(u, 2)
                slab = slab_index(("even_out", "odd_out")[L], 0)
                if (L, 0) not in mixed:
                    slab_ready(slab)
                    rest_ready(slab)
                    pe.wait_ge(ada_copied, 6 * L + 5)
                done = mixed.setdefault((L, u), set())
                for k in blocks:
                    ins = mm(PS[:, mixed_banks[u], :], HT[:, k, t * P:(t + 1) * P], wide(slab)[:, k, h * HALF:(h + 1) * HALF],
                             not done, len(done) == KD - 1, skip_group_check=True)
                    done.add(k)
                if len(done) == KD:
                    ins.then_inc(wout_done, 1)

            pe.wait_ge(consts_ready, 1)
            for t in range(TB):
                turn_xn(0, t)
            modulation_sums(0)
            modulation_join(0)
            small_columns()
            modulation_sums(1)
            modulation_join(1)

            s = slab_index("even_in", 1)
            slab_ready(s)
            for half in range(2):
                if half == 1:
                    rest_ready(s)
                for u in range(CB):
                    for tokens in (slice(0, P), slice(P, S)) if u == 0 and half == 0 else (slice(0, S),):
                        if half == 0:
                            h_in_place(0, tokens.stop // P)
                        for k in range(half * KD // 2, (half + 1) * KD // 2):
                            ins = mm(PS[:, u, tokens], wide(s)[:, k, HALF + u * P:HALF + (u + 1) * P], HT[:, k, tokens],
                                     k == 0 and tokens.start == 0, k == KD - 1, skip_group_check=True)
                    if half == 1:
                        ins.then_inc(proj_done, 1)
            for u in range(CB, 18):
                s = slab_index("even_in", 1 if u in (8, 9) else 2 if u < 8 else 0)
                if u in (4, 10):
                    slab_ready(s)
                w = u - 4
                if w < 8:
                    pe.wait_ge(glu_out, w + 1)
                else:
                    pe.wait_ge(qkv_out, w - 7)
                first_of = s if u in (4, 10) else None
                if u < 8:
                    ins = project_T(u % 4, wide(s, CONV), (u - 4) * P, first_of)
                elif u < 10:
                    ins = project(u % 4, wide(s), 0, u - 8)
                else:
                    ins = project_T(u % 4, wide(s), (u - 10) * P, first_of)
                ins.then_inc(proj_done, 1)

            def logits(i):
                if i == 0:
                    pe.wait_ge(qkv_out, 10)
                if i >= 2:
                    pe.wait_ge(logs_min, i - 1)
                for h in range(2):
                    r = slice(h * HD, (h + 1) * HD)
                    b = 2 * (i % 2) + h
                    mm(PS[:, b, 0:S], KTe[r, i, 0:P], QTe[r, i, :], True, True)
                    ins = mm(PS[:, b, S:S + P], KTe[r, i, P:S], QTe[r, i, P:S], False, True, skip_group_check=True)
                ins.then_inc(z_ready, 1)

            def tails(i):
                pe.wait_ge(fails_masked, 4 * (i + 1))
                for h in range(2):
                    b = 2 * (i % 2) + h
                    s = SPe[:, i % 2, h, :]
                    mm(PS[:, b, 0:3 * P], NEGTRI[:, :], s, False, True, skip_group_check=True)
                    ins = mm(PS[:, b, P:S], NEGONE[:, :], s[:, S:S + P], False, True, skip_group_check=True)
                ins.then_inc(logs_ready, 1)

            def values(i):
                pe.wait_ge(probs_masked, 4 * (i + 1))
                if i:
                    pe.wait_ge(heads_out, i)
                for h in range(2):
                    cols = slice(i * P + h * HD, i * P + (h + 1) * HD)
                    pr = PRe[:, i % 2, h, :]
                    o = PS[h * HD:(h + 1) * HD, 7, :]
                    mm(o[:, 0:S], Ve[:, 0, cols], pr[:, 0:S], True, True, skip_group_check=True)
                    ins = mm(o[:, P:S], Ve[:, 1, cols], pr[:, S:S + P], False, True, skip_group_check=True)
                ins.then_inc(pv_done, 1)

            logits(0)
            logits(1)
            modulation_sums(2)

            def channel_sum(tile, at):
                for b in range(CB):
                    ins = mm(PS[:, 6, at:at + S], ONES[:, :], tile[:, b, :], b == 0, b == CB - 1, skip_group_check=True)
                return ins

            for i in range(NPAIR):
                tails(i)
                if i == 0:
                    modulation_join(2)
                    modulation_sums(3)
                    logits(2)
                    modulation_join(3)
                if i == 1:
                    pe.wait_ge(conv_done, TAPS * CB)
                    pe.wait_ge(ada_ready, 4)
                    channel_sum(CACC, 0).then_inc(conv_mean, 1)
                    values(0)
                    modulation_sums(4)
                    pe.wait_ge(conv_squared, 1)
                    channel_sum(CSQ, S).then_inc(conv_var, 1)
                    logits(3)
                if i == 2:
                    values(1)
                    pe.wait_ge(conv_rstd, 1)
                    modulation_join(4)
                    pe.wait_ge(heads_out, 1)
                    for u in range(2):
                        mix_out(0, u, (0,))
                if i == 3:
                    values(2)
                    pe.wait_ge(heads_out, 2)
                    for u in range(2):
                        mix_out(0, u, (1,))
            values(NPAIR - 1)
            pe.wait_ge(heads_out, NPAIR - 1)
            for u in range(2):
                mix_out(0, u, (2,))
            mix_out(0, 2, (0, 1, 2))
            pe.wait_ge(conv_out, 1)
            mix_out(0, 2, (4, 5, 6, 7))
            pe.wait_ge(heads_out, NPAIR)
            for u in range(2):
                mix_out(0, u, (4, 5, 6, 7, 3))

            def moe(L):
                stage = 2 * L + 1
                mix_out(L, 2, [k for k in range(KD) if k not in mixed[L, 2]])
                before = (4, 1)[L]
                mix_out(L, 3, range(before))
                turn_xn(stage, 0)
                mix_out(L, 3, range(before, KD))
                pe.wait_ge(vectors_in, 16 * N_VECTORS)
                for t in range(TB):
                    if t:
                        modulation_sums(6 * L + 5, 0, KD // 2)
                        turn_xn(stage, t)
                    h_in_place(stage, t + 1)
                    for k in range(KD):
                        for e in range(2):
                            at = t * P + e * SLOT
                            ins = mm(PS[e * SLOT:(e + 1) * SLOT, 7, t * NL:(t + 1) * NL], HT[:, k, at:at + SLOT],
                                     WR[:, L, k, :], k == 0, k == KD - 1, skip_group_check=True)
                ins.then_inc(logits_done, 1)
                modulation_sums(6 * L + 5, KD // 2, KD)
                pe.wait_ge(onehot_ready, L + 1)
                chosen = ONEHOT[:, 2, :, :]
                mm(PS[:, 7, P:P + NE], BEFORE[:, :], chosen[:, 0, :], True, True, skip_group_check=True)
                mm(PS[:, 7, P + NE:P + 2 * NE], BEFORE[:, :], chosen[:, 1, :], True, False, skip_group_check=True)
                mm(PS[:, 7, P + NE:P + 2 * NE], ONES[:, :], chosen[:, 0, :], False, True, skip_group_check=True)
                mm(PS[:, 7, 2 * P:2 * P + NE], ONES[:, :], chosen[:, 0, :], True, False, skip_group_check=True)
                mm(PS[:, 7, 2 * P:2 * P + NE], ONES[:, :], chosen[:, 1, :], False, True,
                   skip_group_check=True).then_inc(rank_done, 1)

                def gather(buf, done):
                    for k in range(KD):
                        for t in range(TB):
                            for s in range(3):
                                ins = mm(PS[:, 2 + k // 4, (k % 4) * P:(k % 4 + 1) * P], XN3[:, s, t, k, :], SG[:, buf, t, :],
                                         t == 0 and s == 0, t == TB - 1 and s == 2)
                    ins.then_inc(done, 1)

                def widen(bank, w, xt, done, half=None, second=None):
                    for k in range(KD):
                        if second is not None and k == KD // 2:
                            pe.wait_ge(*second)
                        for e in range(2):
                            ins = mm(PS[e * SLOT:(e + 1) * SLOT, bank, :], xt[:, k, e * SLOT:(e + 1) * SLOT],
                                     w[:, e, k * F:(k + 1) * F], k == 0, k == KD - 1, skip_group_check=True)
                        if half is not None and k == KD // 2 - 1:
                            ins.then_inc(half, 1)
                    ins.then_inc(done, 1)

                def narrow(w, k_range, h, done):
                    for k in k_range:
                        for e in range(2):
                            ins = mm(PS[e * SLOT:(e + 1) * SLOT, 6 + h, :], HIDT[:, k, e * SLOT:(e + 1) * SLOT],
                                     w[:, e, k * D + h * HALF:k * D + (h + 1) * HALF], k == 0, k == KF - 1,
                                     skip_group_check=True)
                    if KF - 1 in k_range:
                        ins.then_inc(done, 1)
                    return ins

                def turn_weights():
                    for t in range(TB):
                        ins = pe.transpose(PS[:, 5, t * P:(t + 1) * P], SW[:, t, :], IDENT[:, :])
                    return ins

                def turn_hidden():
                    for k in range(KF):
                        ins = pe.transpose(PS[:, 4, k * P:(k + 1) * P], HID[:, k, :], IDENT[:, :])
                    return ins

                def combine(buf, done, y):
                    for u in range(4):
                        h, t = divmod(u, 2)
                        if u == 2:
                            pe.wait_ge(y_ready, y)
                        if u >= 2:
                            pe.wait_ge(x_added, done + u - 1)
                        mm(PS[:, 4 + t, :], SWT[:, buf, t, :], YS[:, h * HALF:(h + 1) * HALF], True, True).then_inc(combined, 1)

                modulation_join(6 * L + 5)
                pe.wait_ge(split_act, 6 * (L + 1))
                pe.wait_ge(slots_built, 2 * ((EP + 1) * L + 1))
                gather(0, gathered)
                with pe.Fori(0, EP // UNROLL) as i:
                    for j in range(UNROLL):
                        n = i * UNROLL + (EP * L + j)
                        adds = i * (4 * UNROLL) + (ADDS * L + 1 + 4 * j)
                        slabs = [MOE0[L] + 3 * j + w for w in range(3)]
                        land = [i * (16 * GROUP) + landed(s) for s in slabs]
                        pe.wait_ge(xt_dve, i * (4 * UNROLL) + 4 * ((EP + 1) * L + j + 1))
                        pe.wait_ge(xt_act, i * (4 * UNROLL) + 4 * ((EP + 1) * L + j + 1))
                        pe.wait_ge(slab_in[slabs[0] % RING], land[0])
                        widen(0, pair_slab(slabs[0]), XT[:, j % 2], gate_done, half_used[0],
                              (rest_in[slabs[0] % RING], land[0]))
                        y = i * (2 * UNROLL) + 2 * ((EP + 1) * L + j + 1)
                        pe.wait_ge(y_ready, y - 1)
                        pe.wait_ge(x_added, adds)
                        pe.wait_ge(ada_ready, 6 * (L + 1))
                        combine((j + 1) % 2, adds, y)
                        pe.wait_ge(slab_in[slabs[1] % RING], land[1])
                        widen(1, pair_slab(slabs[1]), XT[:, j % 2], up_done, half_used[1],
                              (rest_in[slabs[1] % RING], land[1]))
                        pe.wait_ge(slots_built, i * (2 * UNROLL) + 2 * ((EP + 1) * L + j + 2))
                        gather((j + 1) % 2, gathered)
                        pe.wait_ge(weights_built, n * 2 + 2)
                        pe.wait_ge(x_added, adds + 4)
                        turn_weights().then_inc(weights_turned, 1)
                        pe.wait_ge(hidden_ready, n + 1)
                        turn_hidden().then_inc(hidden_turned, 1)
                        pe.wait_ge(weightsT_ready, n + 1)
                        pe.wait_ge(hiddenT_ready, n + 1)
                        pe.wait_ge(slab_in[slabs[2] % RING], land[2])
                        for h in range(2):
                            ins = narrow(pair_slab(slabs[2]), range(KF // 2), h, None)
                        ins.then_inc(half_used[2], 1)
                        pe.wait_ge(rest_in[slabs[2] % RING], land[2])
                        for h in range(2):
                            narrow(pair_slab(slabs[2]), range(KF // 2, KF), h, down_done)
                y = 2 * (EP + 1) * (L + 1)
                pe.wait_ge(y_ready, y - 1)
                pe.wait_ge(x_added, ADDS * (L + 1) - 4)
                combine((UNROLL + 1) % 2, ADDS * (L + 1) - 4, y)

                m = more[L]
                pe.wait_ge(count_ready, L + 1)
                count = pe.value_load(CNTI[0:1, 0:1], min_val=0, max_val=S)
                with pe.If(count > SLOT):
                    pe.wait_ge(x_added, ADDS * (L + 1))
                    with pe.Fori(0, ROUNDS - 1) as r:
                        with pe.Fori(0, EP) as q:
                            step = r * EP + q
                            st = r * (8 + 12 * EP) + q * 12 + 9
                            pe.wait_ge(m["slots"], step * 4 + 4)
                            gather(0, m["gathered"])
                            pe.wait_ge(m["slabs"], step * 48 + 48)
                            pe.wait_ge(m["dve"], st + 8)
                            widen(0, pair_slab(0), XT[:, 0], m["gate"])
                            widen(1, pair_slab(1), XT[:, 0], m["up"])
                            turn_weights()
                            pe.wait_ge(m["dve"], st + 10)
                            turn_hidden().then_inc(m["turned"], 1)
                            pe.wait_ge(m["copied"], step * 2 + 2)
                            for h in range(2):
                                narrow(pair_slab(2), range(KF), h, m["down"])
                            pe.wait_ge(m["dve"], st + 12)
                            for u in range(4):
                                t, h = divmod(u, 2)
                                mm(PS[:, u, :], SWT[:, 0, t, :], YS[:, h * HALF:(h + 1) * HALF],
                                   True, True).then_inc(m["combined"], 1)
                    pe.wait_ge(m["added"], 4 * EP * (ROUNDS - 1))

            moe(0)

            modulation_sums(6)
            for t in range(TB):
                turn_xn(2, t)
            modulation_join(6)
            modulation_sums(7)
            modulation_join(7)
            h_in_place(2, TB)

            def head_sums(u):
                pe.wait_ge(qk_squared, u + 1)
                if u >= 2:
                    pe.wait_ge(qk_rstd, u - 1)
                mm(PS[:, 4 + u % 2, 0:S], HEADSUM[:, :], SQo[u % 2][:, :], True, True).then_inc(qk_mean, 1)

            def scores(h):
                if h == 0:
                    pe.wait_ge(qk_out, 16)
                if h:
                    pe.wait_ge(scores_max, h)
                for t in range(TB):
                    for cc in range(2):
                        r = slice(cc * HD, (cc + 1) * HD)
                        ins = mm(PS[:, cc, t * P:(1 + 2 * t) * P], QTo[r, h, t * P:(t + 1) * P],
                                 KTo[r, h, 0:(t + 1) * P], True, True, skip_group_check=True)
                ins.then_inc(scores_done, 1)

            for u in range(20):
                s = slab_index("odd_in", 0 if u < 8 else 1 if u < 16 else 2)
                if u in (0, 8, 16):
                    slab_ready(s)
                if 4 <= u < 16:
                    pe.wait_ge(qk_out, u - 3)
                if u >= 18:
                    pe.wait_ge(v_out, u - 17)
                first_of = s if u in (8, 16) else None
                if u == 0:
                    for w in range(4):
                        project_T(w, wide(s), w * P, None, range(KD // 2))
                    rest_ready(s)
                if u < 4:
                    ins = project_T(u, wide(s), u * P, None, range(KD // 2, KD))
                elif u < 16:
                    ins = project_T(u % 4, wide(s), (u % 8) * P, first_of)
                else:
                    ins = project(6 + u % 2, wide(s), ((u - 16) % 2) * HALF, (u - 16) // 2, first_of)
                ins.then_inc(proj_done, 1)
                if 1 <= u <= 16:
                    head_sums(u - 1)
                if u in (17, 18):
                    scores(u - 17)

            def head_mean(h):
                pe.wait_ge(o_squared, h + 1)
                mm(PS[:, 7, 0:S], ONES[:, :], SQo[0][:, :], True, True, skip_group_check=True).then_inc(o_mean, 1)

            early = {3: range(0, 1), 4: range(1, 3), 5: range(3, 4), 6: range(4, 5), 7: range(5, 6)}
            for h in range(NH):
                pe.wait_ge(diff_ready, 2 * (h + 1))
                if h:
                    pe.wait_ge(diffT_ready, h)
                for n in range(3):
                    ins = pe.transpose(PS[:, 2, n * P:(n + 1) * P], PRo[:, n * P:(n + 1) * P], IDENT[:, :])
                ins.then_inc(diff_turned, 1)
                if h:
                    head_mean(h - 1)
                if h + 2 < NH:
                    scores(h + 2)
                if h in fills1:
                    modulation_sums(fills1[h])
                if h in early:
                    pe.wait_ge(o_out, early[h].stop)
                    for u in range(2):
                        mix_out(1, u, early[h])
                pe.wait_ge(diffT_ready, h + 1)
                if h:
                    pe.wait_ge(o_out, h)
                else:
                    pe.wait_ge(v_out, 4)
                mm(PS[:, 3, 0:S], Vo[:, 0, h * P:(h + 1) * P], PTo[:, 0:S], True, True, skip_group_check=True)
                mm(PS[:, 3, P:S], Vo[:, 1, h * P:(h + 1) * P], PTo[:, S:S + P], False, True,
                   skip_group_check=True).then_inc(o_done, 1)
                if h in fills1:
                    modulation_join(fills1[h])
            pe.wait_ge(o_out, NH - 1)
            for u in range(2):
                mix_out(1, u, (NH - 2,))
            head_mean(NH - 1)
            mix_out(1, 2, range(4))
            pe.wait_ge(o_out, NH)
            for u in range(2):
                mix_out(1, u, (NH - 1,))
            moe(1)


N_ROWS = 6 + 4
N_VECTORS = 2 + 8 + 4


_INS = ["x", "c", "w_ada", "b_ada", "mix_norm_g", "ffn_norm_g", "even_w_in", "conv_b_glu", "conv_dw", "conv_dw_b",
        "conv_ln_g", "conv_ln_b", "even_w_out", "odd_w_in", "qk_norm_q", "qk_norm_k", "lambda_q1", "lambda_k1",
        "lambda_q2", "lambda_k2", "diff_sub_g", "odd_w_out", "moe_w_group", "moe_b_group", "moe_w_router",
        "moe_b_router", "moe_w_gate", "moe_w_up", "moe_w_down"]


def kernel(**inputs):
    import numpy as np
    import concourse.bacc as bacc
    from concourse.bass_utils import run_bass_kernel_spmd

    nc = bacc.Bacc("TRN2", target_bir_lowering=False, num_devices=1)
    arrays, args = {}, []
    for name in _INS:
        a = np.ascontiguousarray(inputs[name])
        arrays[f"in_{name}"] = a
        args.append(nc.dram_tensor(f"in_{name}", a.shape, mybir.dt.from_np(a.dtype), kind="ExternalInput").ap())
    result = nc.dram_tensor("out", inputs["x"].shape, F32, kind="ExternalOutput").ap()
    build_trunk(nc, *args, result)
    r = run_bass_kernel_spmd(nc, [arrays], core_ids=[0])
    return r.results[0]["out"]
```
